# Optimizing a Trainium2 kernel written in Bass

```python
import jax
import jax.numpy as jnp
from jax import lax
import numpy as np

D_MODEL = 1024
BATCH = 1
SEQ = 256
DEPTH = 1
DEC_BATCH = 8
DEC_SEQ = 4
PAST_LEN = 1024
PAGE_SIZE = 128

M_HEADS = 4
M_DH = D_MODEL // 8
M_WIDTH = M_HEADS * M_DH
M_CHUNK = 64
A_HEADS = 8
A_KV = 2
A_HPG = A_HEADS // A_KV
A_DH = 64
A_WIDTH = A_HEADS * A_DH
CMP_STRIDE = 16
CMP_LEN = 2 * CMP_STRIDE
SEL_LEN = 64
N_SEL = 16
WINDOW = 512
Q_BLOCK = 128
SEL_Q_BLOCK = 64
ROPE_THETA = 500000.0
ROT_DIM = A_DH // 4
ATT_SCALE = A_DH ** -0.5
N_EXPERTS = 32
TOP_K = 4
D_EXPERT = D_MODEL
SWIGLU_LIMIT = 7.0
SWIGLU_ALPHA = 1.702
MOE_BLOCK = 128
EPS = 1e-6
IN_SIZES = (M_WIDTH, M_WIDTH, M_WIDTH, M_WIDTH, M_HEADS, M_HEADS, A_WIDTH, 6 * A_KV * A_DH, 3 * A_HEADS, D_MODEL, D_MODEL)
N_IN = 4 * M_WIDTH + 2 * M_HEADS + A_WIDTH + 6 * A_KV * A_DH + 3 * A_HEADS + 2 * D_MODEL
F_GATE_OFF = 4 * M_WIDTH + M_HEADS

kernel_name = 'hybrid_mlstm_nsa_moe_adaln_step'

def _rmsnorm(x, g):
    xf = x.astype(jnp.float32)
    y = xf * lax.rsqrt(jnp.mean(xf * xf, axis=-1, keepdims=True) + EPS)
    return (y * g.astype(jnp.float32)).astype(x.dtype)

def _partial_rope(x, pos):
    half = ROT_DIM // 2
    inv = ROPE_THETA ** (-jnp.arange(half, dtype=jnp.float32) * (2.0 / ROT_DIM))
    ang = pos.astype(jnp.float32)[:, None] * inv[None, :]
    cos = jnp.cos(ang)[None, :, None, :]
    sin = jnp.sin(ang)[None, :, None, :]
    xf = x.astype(jnp.float32)
    x1, x2 = xf[..., :half], xf[..., half:ROT_DIM]
    out = jnp.concatenate([x1 * cos - x2 * sin, x1 * sin + x2 * cos, xf[..., ROT_DIM:]], axis=-1)
    return out.astype(x.dtype)

def _masked_softmax(s, mask):
    s = jnp.where(mask, s, -jnp.inf)
    m = jnp.max(s, axis=-1, keepdims=True)
    m = jnp.where(jnp.isfinite(m), m, 0.0)
    e = jnp.exp(s - m)
    d = jnp.sum(e, axis=-1, keepdims=True)
    return e / jnp.where(d > 0, d, 1.0)

def _adaln(c, w, b):
    mod = jax.nn.silu(c) @ w + b
    return jnp.split(mod[:, None, :], 6, axis=-1)

def _mixer_inputs(h, pos, p):
    B, T, _ = h.shape
    z = h @ p['w_in'] + p['b_in']
    parts = []
    off = 0
    for size in IN_SIZES:
        parts.append(z[..., off:off + size])
        off += size
    mq, mk, mv, mo, mi, mf, aq, akv, ag, ga, gb = parts
    to_heads = lambda a: jnp.moveaxis(a.reshape(B, T, M_HEADS, M_DH), 2, 1)
    mq, mk, mv = to_heads(mq), to_heads(mk) * (M_DH ** -0.5), to_heads(mv)
    mi, mf = jnp.moveaxis(mi, 2, 1), jnp.moveaxis(mf, 2, 1)
    q = _rmsnorm(aq.reshape(B, T, A_HEADS, A_DH), p['q_norm_g'])
    q_rope = _partial_rope(q, pos)
    kv = akv.reshape(B, T, 6, A_KV, A_DH)
    k_sel = _partial_rope(_rmsnorm(kv[:, :, 2], p['k_norm_g'][1]), pos)
    k_win = _partial_rope(_rmsnorm(kv[:, :, 4], p['k_norm_g'][2]), pos)
    rows = jnp.stack([kv[:, :, 0], kv[:, :, 1], k_sel, kv[:, :, 3]], axis=2)
    win_rows = jnp.stack([k_win, kv[:, :, 5]], axis=2)
    br_gates = jax.nn.sigmoid(ag.reshape(B, T, A_HEADS, 3))
    return (mq, mk, mv, mi, mf, mo), (q, q_rope, rows, win_rows, br_gates), (ga, gb)

def _mlstm_chunkwise(q, k, v, i_pre, f_pre, C0, n0, m0, chunk):
    B, H, T, Dh = q.shape
    nc = T // chunk
    f32 = jnp.float32

    def chunks(a):
        return jnp.moveaxis(a.astype(f32).reshape(B, H, nc, chunk, *a.shape[3:]), 2, 0)

    causal = jnp.tril(jnp.ones((chunk, chunk), bool))

    def step(carry, inp):
        C, n, m = carry
        q_, k_, v_, i_, lf_ = inp
        b = jnp.cumsum(lf_, axis=-1)
        dmat = jnp.where(causal, b[..., :, None] - b[..., None, :] + i_[..., None, :], -jnp.inf)
        inter = b + m[..., None]
        m_row = jnp.maximum(jnp.max(dmat, axis=-1), inter)
        w = jnp.exp(dmat - m_row[..., None])
        w_inter = jnp.exp(inter - m_row)
        s = jnp.einsum('bhtd,bhsd->bhts', q_, k_) * w
        num = jnp.einsum('bhts,bhsd->bhtd', s, v_) + w_inter[..., None] * jnp.einsum('bhvk,bhtk->bhtv', C, q_)
        den = jnp.sum(s, axis=-1) + w_inter * jnp.einsum('bhk,bhtk->bht', n, q_)
        h = num / jnp.maximum(jnp.abs(den), jnp.exp(-m_row))[..., None]
        bL = b[..., -1]
        dec = bL[..., None] - b + i_
        m_new = jnp.maximum(bL + m, jnp.max(dec, axis=-1))
        ws = jnp.exp(dec - m_new[..., None])
        wc = jnp.exp(bL + m - m_new)
        C_new = wc[..., None, None] * C + jnp.einsum('bhs,bhsv,bhsk->bhvk', ws, v_, k_)
        n_new = wc[..., None] * n + jnp.einsum('bhs,bhsk->bhk', ws, k_)
        return (C_new, n_new, m_new), h

    xs = (chunks(q), chunks(k), chunks(v), chunks(i_pre), chunks(jax.nn.log_sigmoid(f_pre.astype(f32))))
    (C, n, m), h = lax.scan(step, (C0.astype(f32), n0.astype(f32), m0.astype(f32)), xs)
    h = jnp.moveaxis(h, 0, 2).reshape(B, H, T, Dh)
    return h, (C.astype(C0.dtype), n.astype(n0.dtype), m.astype(m0.dtype))

def _compress(k_rows, pe, w):
    B, Tk, G, Dh = k_rows.shape
    seg = k_rows.reshape(B, Tk // CMP_STRIDE, CMP_STRIDE, G, Dh)
    blocks = jnp.concatenate([seg[:, :-1], seg[:, 1:]], axis=2)
    return jnp.einsum('bnlgd,lde->bnge', blocks + pe[None, None, :, None, :], w)

def _cmp_attention(q, kc, vc, q_pos):
    B, Tq = q.shape[:2]
    nc = kc.shape[1]
    qg = q.reshape(B, Tq, A_KV, A_HPG, A_DH)
    s = jnp.einsum('btghd,bngd->btghn', qg, kc).astype(jnp.float32) * ATT_SCALE
    end = jnp.arange(nc) * CMP_STRIDE + (CMP_LEN - 1)
    mask = end[None, :] <= q_pos[:, None]
    p = _masked_softmax(s, mask[None, :, None, None, :])
    o = jnp.einsum('btghn,bngd->btghd', p, vc.astype(jnp.float32))
    return o.reshape(B, Tq, A_HEADS, A_DH), p

def _select_blocks(p_cmp, q_pos, nsb):
    B, Tq = p_cmp.shape[:2]
    per = SEL_LEN // CMP_STRIDE
    imp = jnp.sum(p_cmp, axis=3)
    nc = imp.shape[-1]
    imp = jnp.pad(imp, ((0, 0), (0, 0), (0, 0), (0, nsb * per - nc)))
    imp = jnp.sum(imp.reshape(B, Tq, A_KV, nsb, per), axis=-1)
    cur = q_pos // SEL_LEN
    past = jnp.arange(nsb)[None, :] < cur[:, None]
    imp = jnp.where(past[None, :, None, :], imp, -1.0)
    top_v, top_i = lax.top_k(imp, min(N_SEL - 1, nsb))
    cur_b = jnp.broadcast_to(cur[None, :, None, None], (B, Tq, A_KV, 1)).astype(top_i.dtype)
    idx = jnp.concatenate([cur_b, top_i], axis=-1)
    valid = jnp.concatenate([jnp.ones((B, Tq, A_KV, 1), bool), top_v >= 0.0], axis=-1)
    return idx, valid

def _sel_attention(qg, k_blk, v_blk, idx, valid, q_pos):
    B, Tq = qg.shape[:2]
    ns = idx.shape[-1]
    bi = jnp.arange(B)[:, None, None, None]
    gi = jnp.arange(A_KV)[None, None, :, None]
    kg = k_blk[bi, gi, idx]
    vg = v_blk[bi, gi, idx]
    s = jnp.einsum('btghd,btgnjd->btghnj', qg, kg).astype(jnp.float32) * ATT_SCALE
    kpos = idx[..., None] * SEL_LEN + jnp.arange(SEL_LEN)
    mask = valid[..., None] & (kpos <= q_pos[None, :, None, None, None])
    p = _masked_softmax(s.reshape(B, Tq, A_KV, A_HPG, ns * SEL_LEN), mask.reshape(B, Tq, A_KV, 1, ns * SEL_LEN))
    o = jnp.einsum('btghm,btgmd->btghd', p, vg.reshape(B, Tq, A_KV, ns * SEL_LEN, A_DH).astype(jnp.float32))
    return o.reshape(B, Tq, A_HEADS, A_DH)

def _window_prompt(q, win_rows):
    B, T = q.shape[:2]
    nq = T // Q_BLOCK
    span = WINDOW + Q_BLOCK
    kv = jnp.pad(win_rows, ((0, 0), (WINDOW, 0), (0, 0), (0, 0), (0, 0)))
    kidx = jnp.arange(nq)[:, None] * Q_BLOCK + jnp.arange(span)[None, :]
    kvb = kv[:, kidx]
    qb = q.reshape(B, nq, Q_BLOCK, A_KV, A_HPG, A_DH)
    s = jnp.einsum('bcqghd,bckgd->bcghqk', qb, kvb[:, :, :, 0]).astype(jnp.float32) * ATT_SCALE
    qpos = jnp.arange(nq)[:, None] * Q_BLOCK + jnp.arange(Q_BLOCK)[None, :]
    kpos = kidx - WINDOW
    diff = qpos[:, :, None] - kpos[:, None, :]
    mask = (diff >= 0) & (diff < WINDOW) & (kpos[:, None, :] >= 0)
    p = _masked_softmax(s, mask[None, :, None, None])
    o = jnp.einsum('bcghqk,bckgd->bcqghd', p, kvb[:, :, :, 1].astype(jnp.float32))
    return o.reshape(B, T, A_HEADS, A_DH)

def _window_sample(q, win_all, q_pos, k_pos):
    B, Tq = q.shape[:2]
    qg = q.reshape(B, Tq, A_KV, A_HPG, A_DH)
    s = jnp.einsum('btghd,bkgd->btghk', qg, win_all[:, :, 0]).astype(jnp.float32) * ATT_SCALE
    diff = q_pos[:, None] - k_pos[None, :]
    mask = (diff >= 0) & (diff < WINDOW)
    p = _masked_softmax(s, mask[None, :, None, None, :])
    o = jnp.einsum('btghk,bkgd->btghd', p, win_all[:, :, 1].astype(jnp.float32))
    return o.reshape(B, Tq, A_HEADS, A_DH)

def _nsa(q, q_rope, br_gates, rows, q_pos, o_win, p):
    B, Tq = q.shape[:2]
    Tk = rows.shape[1]
    kc = _rmsnorm(_compress(rows[:, :, 0], p['cmp_pe_k'], p['cmp_w_k']), p['k_norm_g'][0])
    vc = _compress(rows[:, :, 1], p['cmp_pe_v'], p['cmp_w_v'])
    o_cmp, p_cmp = _cmp_attention(q, kc, vc, q_pos)
    nsb = Tk // SEL_LEN
    idx, valid = _select_blocks(p_cmp, q_pos, nsb)
    k_blk = jnp.moveaxis(rows[:, :, 2].reshape(B, nsb, SEL_LEN, A_KV, A_DH), 3, 1)
    v_blk = jnp.moveaxis(rows[:, :, 3].reshape(B, nsb, SEL_LEN, A_KV, A_DH), 3, 1)
    qg = q_rope.reshape(B, Tq, A_KV, A_HPG, A_DH)
    blk = SEL_Q_BLOCK if Tq % SEL_Q_BLOCK == 0 else Tq
    nq = Tq // blk
    if nq == 1:
        o_sel = _sel_attention(qg, k_blk, v_blk, idx, valid, q_pos)
    else:
        split = lambda a: jnp.moveaxis(a.reshape(a.shape[0], nq, blk, *a.shape[2:]), 1, 0)
        o_sel = lax.map(lambda a: _sel_attention(a[0], k_blk, v_blk, a[1], a[2], a[3]),
                        (split(qg), split(idx), split(valid), q_pos.reshape(nq, blk)))
        o_sel = jnp.moveaxis(o_sel, 0, 1).reshape(B, Tq, A_HEADS, A_DH)
    g = br_gates.astype(jnp.float32)
    return g[..., 0:1] * o_cmp + g[..., 1:2] * o_sel + g[..., 2:3] * o_win

def _mixer_out(h_m, mo, o_nsa, ga, gb, p):
    B, T = mo.shape[:2]
    hm = jnp.moveaxis(h_m, 1, 2).reshape(B, T, M_WIDTH).astype(mo.dtype)
    ym = (jax.nn.sigmoid(mo) * hm) @ p['w_up_m']
    ya = o_nsa.reshape(B, T, A_WIDTH).astype(mo.dtype) @ p['w_up_a']
    return (jax.nn.sigmoid(ga) * ym + jax.nn.sigmoid(gb) * ya) @ p['w_out']

def _expert(xb, e, w_gu, b_gu, w_dn, b_dn):
    gu = xb @ w_gu[e] + b_gu[e]
    g = jnp.minimum(gu[..., :D_EXPERT], SWIGLU_LIMIT)
    u = jnp.clip(gu[..., D_EXPERT:], -SWIGLU_LIMIT, SWIGLU_LIMIT)
    act = g * jax.nn.sigmoid(SWIGLU_ALPHA * g) * (u + 1.0)
    return act @ w_dn[e] + b_dn[e]

def _moe(x, p):
    M, D = x.shape
    logits = (x @ p['w_router'] + p['b_router']).astype(jnp.float32)
    top_v, top_e = lax.top_k(logits, TOP_K)
    gate = jax.nn.softmax(top_v, axis=-1)
    MK = M * TOP_K
    flat_e = top_e.reshape(MK)
    order = jnp.argsort(flat_e)
    sorted_e = flat_e[order]
    counts = jnp.bincount(flat_e, length=N_EXPERTS)
    padded = (counts + MOE_BLOCK - 1) // MOE_BLOCK * MOE_BLOCK
    pad_end = jnp.cumsum(padded)
    pad_start = pad_end - padded
    start = jnp.cumsum(counts) - counts
    dest = pad_start[sorted_e] + jnp.arange(MK) - start[sorted_e]
    n_blocks = (MK + N_EXPERTS * (MOE_BLOCK - 1) + MOE_BLOCK - 1) // MOE_BLOCK
    src_tok = jnp.full((n_blocks * MOE_BLOCK,), M, jnp.int32).at[dest].set((order // TOP_K).astype(jnp.int32))
    block_e = jnp.minimum(jnp.searchsorted(pad_end, jnp.arange(n_blocks) * MOE_BLOCK, side='right'), N_EXPERTS - 1)
    xp = jnp.concatenate([x, jnp.zeros((1, D), x.dtype)], axis=0)
    xb = xp[src_tok].reshape(n_blocks, MOE_BLOCK, D)
    yb = lax.map(lambda a: _expert(a[0], a[1], p['w_gu'], p['b_gu'], p['w_dn'], p['b_dn']), (xb, block_e))
    y_sorted = yb.reshape(-1, D)[dest]
    y_slots = jnp.zeros((MK, D), yb.dtype).at[order].set(y_sorted)
    return jnp.einsum('mkd,mk->md', y_slots.reshape(M, TOP_K, D), gate.astype(y_slots.dtype))

def _ffn(x, sh, sc, p):
    B, T, D = x.shape
    h = _rmsnorm(x, p['g_ffn']) * (1.0 + sc) + sh
    return _moe(h.reshape(B * T, D), p).reshape(B, T, D)

def _prompt_layer(x, c, p):
    B, T, _ = x.shape
    sh1, sc1, gt1, sh2, sc2, gt2 = _adaln(c, p['w_ada'], p['b_ada'])
    h = _rmsnorm(x, p['g_mix']) * (1.0 + sc1) + sh1
    pos = jnp.arange(T, dtype=jnp.int32)
    (mq, mk, mv, mi, mf, mo), (q, q_rope, rows, win_rows, br_gates), (ga, gb) = _mixer_inputs(h, pos, p)
    C0 = jnp.zeros((B, M_HEADS, M_DH, M_DH), x.dtype)
    n0 = jnp.zeros((B, M_HEADS, M_DH), x.dtype)
    m0 = jnp.zeros((B, M_HEADS), x.dtype)
    h_m, (C, n, m) = _mlstm_chunkwise(mq, mk, mv, mi, mf, C0, n0, m0, min(M_CHUNK, T))
    o_win = _window_prompt(q_rope, win_rows)
    o_nsa = _nsa(q, q_rope, br_gates, rows, pos, o_win, p)
    x = x + gt1 * _mixer_out(h_m, mo, o_nsa, ga, gb, p)
    x = x + gt2 * _ffn(x, sh2, sc2, p)
    win_state = win_rows[:, T - min(WINDOW, T):]
    return x, rows, win_state, C, n, m

def _sample_layer(x, c, cache_kv, page_table, win_buf, C0, n0, m0, p):
    B, T, _ = x.shape
    sh1, sc1, gt1, sh2, sc2, gt2 = _adaln(c, p['w_ada'], p['b_ada'])
    h = _rmsnorm(x, p['g_mix']) * (1.0 + sc1) + sh1
    pos = PAST_LEN + jnp.arange(T, dtype=jnp.int32)
    (mq, mk, mv, mi, mf, mo), (q, q_rope, rows, win_rows, br_gates), (ga, gb) = _mixer_inputs(h, pos, p)
    h_m, (C, n, m) = _mlstm_chunkwise(mq, mk, mv, mi, mf, C0, n0, m0, T)
    n_pages = page_table.shape[1]
    past = cache_kv[page_table].reshape(B, n_pages * PAGE_SIZE, 4, A_KV, A_DH)
    pad = (-T) % SEL_LEN
    all_rows = jnp.concatenate([past, rows.astype(past.dtype), jnp.zeros((B, pad, 4, A_KV, A_DH), past.dtype)], axis=1)
    win_all = jnp.concatenate([win_buf, win_rows.astype(win_buf.dtype)], axis=1)
    wb = win_buf.shape[1]
    k_pos = PAST_LEN - wb + jnp.arange(wb + T, dtype=jnp.int32)
    o_win = _window_sample(q_rope, win_all, pos, k_pos)
    o_nsa = _nsa(q, q_rope, br_gates, all_rows, pos, o_win, p)
    x = x + gt1 * _mixer_out(h_m, mo, o_nsa, ga, gb, p)
    x = x + gt2 * _ffn(x, sh2, sc2, p)
    return x, rows, win_all[:, T:], C, n, m

def setup_inputs(seed: int = 0) -> dict:
    key = jax.random.key(seed)
    ks = jax.random.split(key, 32)
    f32 = jnp.float32
    nrm = lambda k, shape, scale: jax.random.normal(k, shape, f32) * scale
    n_pages = PAST_LEN // PAGE_SIZE
    n_used = DEC_BATCH * n_pages
    n_phys = n_used + n_used // 4
    win_buf = min(WINDOW, PAST_LEN)
    page_table = jax.random.permutation(ks[0], n_phys)[:n_used].reshape(DEC_BATCH, n_pages).astype(jnp.int32)
    b_in = nrm(ks[14], (DEPTH, N_IN), 0.02)
    b_in = b_in.at[:, F_GATE_OFF:F_GATE_OFF + M_HEADS].add(3.0)
    return {
        'x_prompt': nrm(ks[1], (BATCH, SEQ, D_MODEL), 1.0),
        'x_sample': nrm(ks[2], (DEC_BATCH, DEC_SEQ, D_MODEL), 1.0),
        'cache_nsa_kv': nrm(ks[3], (DEPTH, n_phys, PAGE_SIZE, 4, A_KV, A_DH), 1.0),
        'state_win_kv': nrm(ks[4], (DEPTH, DEC_BATCH, win_buf, 2, A_KV, A_DH), 1.0),
        'state_mlstm_C': nrm(ks[5], (DEPTH, DEC_BATCH, M_HEADS, M_DH, M_DH), 0.1),
        'state_mlstm_n': nrm(ks[6], (DEPTH, DEC_BATCH, M_HEADS, M_DH), 0.5),
        'state_mlstm_m': nrm(ks[7], (DEPTH, DEC_BATCH, M_HEADS), 0.5),
        'page_table': page_table,
        'c_prompt': nrm(ks[8], (BATCH, D_MODEL), 1.0),
        'c_sample': nrm(ks[9], (DEC_BATCH, D_MODEL), 1.0),
        'w_ada': nrm(ks[10], (DEPTH, D_MODEL, 6 * D_MODEL), 0.5 * D_MODEL ** -0.5),
        'b_ada': nrm(ks[11], (DEPTH, 6 * D_MODEL), 0.02),
        'g_mix': 1.0 + nrm(ks[12], (DEPTH, D_MODEL), 0.02),
        'g_ffn': 1.0 + nrm(ks[13], (DEPTH, D_MODEL), 0.02),
        'w_in': nrm(ks[15], (DEPTH, D_MODEL, N_IN), D_MODEL ** -0.5),
        'b_in': b_in,
        'q_norm_g': 1.0 + nrm(ks[16], (DEPTH, A_DH), 0.02),
        'k_norm_g': 1.0 + nrm(ks[17], (DEPTH, 3, A_DH), 0.02),
        'cmp_pe_k': nrm(ks[18], (DEPTH, CMP_LEN, A_DH), 0.02),
        'cmp_pe_v': nrm(ks[19], (DEPTH, CMP_LEN, A_DH), 0.02),
        'cmp_w_k': nrm(ks[20], (DEPTH, CMP_LEN, A_DH, A_DH), (CMP_LEN * A_DH) ** -0.5),
        'cmp_w_v': nrm(ks[21], (DEPTH, CMP_LEN, A_DH, A_DH), (CMP_LEN * A_DH) ** -0.5),
        'w_up_m': nrm(ks[22], (DEPTH, M_WIDTH, D_MODEL), M_WIDTH ** -0.5),
        'w_up_a': nrm(ks[23], (DEPTH, A_WIDTH, D_MODEL), A_WIDTH ** -0.5),
        'w_out': nrm(ks[24], (DEPTH, D_MODEL, D_MODEL), D_MODEL ** -0.5),
        'w_router': nrm(ks[25], (DEPTH, D_MODEL, N_EXPERTS), D_MODEL ** -0.5),
        'b_router': nrm(ks[26], (DEPTH, N_EXPERTS), 0.01),
        'w_gu': nrm(ks[27], (DEPTH, N_EXPERTS, D_MODEL, 2 * D_EXPERT), D_MODEL ** -0.5),
        'b_gu': nrm(ks[28], (DEPTH, N_EXPERTS, 2 * D_EXPERT), 0.01),
        'w_dn': nrm(ks[29], (DEPTH, N_EXPERTS, D_EXPERT, D_MODEL), D_EXPERT ** -0.5),
        'b_dn': nrm(ks[30], (DEPTH, N_EXPERTS, D_MODEL), 0.01),
    }

def reference(x_prompt, x_sample, cache_nsa_kv, state_win_kv, state_mlstm_C, state_mlstm_n, state_mlstm_m,
              page_table, c_prompt, c_sample, w_ada, b_ada, g_mix, g_ffn, w_in, b_in, q_norm_g, k_norm_g,
              cmp_pe_k, cmp_pe_v, cmp_w_k, cmp_w_v, w_up_m, w_up_a, w_out, w_router, b_router,
              w_gu, b_gu, w_dn, b_dn):
    y_p, y_s = x_prompt, x_sample
    kv_p, kv_s, win_p, win_s = [], [], [], []
    Cp, np_, mp, Cs, ns, ms = [], [], [], [], [], []
    for l in range(DEPTH):
        p = dict(w_ada=w_ada[l], b_ada=b_ada[l], g_mix=g_mix[l], g_ffn=g_ffn[l], w_in=w_in[l], b_in=b_in[l],
                 q_norm_g=q_norm_g[l], k_norm_g=k_norm_g[l], cmp_pe_k=cmp_pe_k[l], cmp_pe_v=cmp_pe_v[l],
                 cmp_w_k=cmp_w_k[l], cmp_w_v=cmp_w_v[l], w_up_m=w_up_m[l], w_up_a=w_up_a[l], w_out=w_out[l],
                 w_router=w_router[l], b_router=b_router[l], w_gu=w_gu[l], b_gu=b_gu[l], w_dn=w_dn[l], b_dn=b_dn[l])
        y_p, r_p, w_p, C_p, n_p, m_p = _prompt_layer(y_p, c_prompt, p)
        y_s, r_s, w_s, C_s, n_s, m_s = _sample_layer(y_s, c_sample, cache_nsa_kv[l], page_table, state_win_kv[l],
                                                     state_mlstm_C[l], state_mlstm_n[l], state_mlstm_m[l], p)
        kv_p.append(r_p); kv_s.append(r_s); win_p.append(w_p); win_s.append(w_s)
        Cp.append(C_p); np_.append(n_p); mp.append(m_p); Cs.append(C_s); ns.append(n_s); ms.append(m_s)
    kv_prompt, kv_sample = jnp.stack(kv_p), jnp.stack(kv_s)
    win_prompt, win_sample = jnp.stack(win_p), jnp.stack(win_s)
    C_prompt, n_prompt, m_prompt = jnp.stack(Cp), jnp.stack(np_), jnp.stack(mp)
    C_sample, n_sample, m_sample = jnp.stack(Cs), jnp.stack(ns), jnp.stack(ms)
    return (y_p, y_s, kv_prompt, kv_sample, win_prompt, win_sample,
            C_prompt, n_prompt, m_prompt, C_sample, n_sample, m_sample)


_drawn_inputs = setup_inputs


def setup_inputs(seed=0):
    import zlib

    import numpy as np

    out = dict(_drawn_inputs(seed))
    spreads = {}
    factors = {'cache_nsa_kv': 2.696,
     'g_ffn': 2.854,
     'q_norm_g': 8.0,
     'k_norm_g': 4.544,
     'cmp_pe_k': 8.0,
     'cmp_pe_v': 8.0,
     'b_router': 4.118,
     'b_gu': 8.0,
     'b_dn': 45.727}
    for name, (base, spread) in spreads.items():
        noise = np.random.default_rng([zlib.crc32(name.encode()), seed]).standard_normal(out[name].shape)
        drawn = base * np.exp(spread * noise) if base else spread * noise
        out[name] = jnp.asarray(drawn.astype(out[name].dtype))
    for name, factor in factors.items():
        out[name] = (out[name] * factor).astype(out[name].dtype)
    return out
```

```python
import numpy as np
import concourse.bass as bass
from concourse import mybir
from contextlib import ExitStack

F32 = mybir.dt.float32
BF16 = mybir.dt.bfloat16
I32 = mybir.dt.int32
U32 = mybir.dt.uint32
ALU = mybir.AluOpType
ACT = mybir.ActivationFunctionType
AX = mybir.AxisListType

P = 128
D = 1024
SEQ = 256
DB, DT = 8, 4
NTOK = SEQ + DB * DT
TILES = [(0, 128), (128, 128), (256, 32)]
PAST = 1024
PAGE = 128
NPAGE = PAST // PAGE
MH, MD = 4, 128
AH, KV, HPG, DH = 8, 2, 4, 64
SEG = 16
NC_P = SEQ // SEG - 1
NC_S = PAST // SEG - 1
WIN = 512
NEXP, TOPK = 32, 4
CAP = 64
OVER = (NTOK * TOPK + NEXP * (CAP - 1)) // CAP - NEXP
NBLK = NEXP + OVER
NIN = 5408
SCALE = DH ** -0.5
EPS = 1e-6
STAGES = 9
NEG = -1e30

ZV, ZI, ZF, ZQ, ZKV, ZG, ZN = 0, 512, 516, 520, 1032, 1800, 1824
ROW_CHUNKS = [(1024, 512, 0), (2048, 512, 512), (2560, 512, 1024), (3072, 288, 1536)]
COL_CHUNKS = [0, 512, 1536, 3360, 3872, 4384, 4896]
STAGE1 = [("ada", 4), ("row", 0), ("ada", 5), ("ada", 6), ("row", 1), ("ada", 7), ("row", 2), ("ada", 8),
          ("row", 3), ("ada", 9), ("col", 0), ("ada", 10), ("col", 1), ("ada", 11)]
WORDS = 4096
NW = 3


def constants():
    t = {}
    i = np.arange(P)
    t["ident"] = np.eye(P)
    t["zeros"] = np.zeros((P, P))
    t["causal"] = np.where(i[None, :] <= i[:, None], 0.0, NEG)
    t["causal_t"] = np.where(i[:, None] <= i[None, :], 0.0, NEG)
    t["zeros_t"] = np.zeros((P, P))
    sel = np.zeros((P, NTOK))
    sel[0, :SEQ] = 1
    for b in range(DB):
        sel[1 + b, SEQ + b * DT:SEQ + (b + 1) * DT] = 1
    t["sel"] = sel
    pos = np.concatenate([np.arange(SEQ), PAST + np.tile(np.arange(DT), DB)]).astype(np.float32)
    inv = (np.float32(500000.0) ** (-np.arange(8, dtype=np.float32) * np.float32(2.0 / 16))).astype(np.float32)
    ang = np.zeros((3 * P, 8), np.float32)
    ang[:NTOK] = pos[:, None] * inv[None, :]
    t["cos"] = np.cos(ang.astype(np.float64)).reshape(3, P, 8).transpose(1, 0, 2).reshape(P, 24)
    t["sin"] = np.sin(ang.astype(np.float64)).reshape(3, P, 8).transpose(1, 0, 2).reshape(P, 24)
    oh = np.zeros((P, MH * P))
    for h in range(MH):
        oh[h, h * P:(h + 1) * P] = 1
    t["head_row"] = oh
    r = np.arange(DB * DT)
    same = (r[:, None] // DT == r[None, :] // DT) & (r[:, None] <= r[None, :])
    m = np.full((P, DB * DT), NEG)
    m[:DB * DT] = np.where(same, 0.0, NEG)
    t["sample_t"] = m
    m = np.zeros((P, DB))
    m[r, r // DT] = 1
    t["batch_of"] = m
    t["ones"] = np.ones((P, P))
    n = np.arange(NC_P)
    q = np.arange(SEQ)
    m = np.where(n[None, :] * SEG + 2 * SEG - 1 <= q[:, None], 0.0, NEG)
    t["cmp_mask"] = m.reshape(2, P, NC_P).transpose(1, 0, 2).reshape(P, 2 * NC_P)
    t["cmp_valid"] = (q >= 2 * SEG - 1).astype(float).reshape(2, P).T
    combo, j, tt = i // 32, (i % 32) // DT, i % DT
    used = i % 32 < HPG * DT
    g = (combo[:, None] == combo[None, :]) & (tt[:, None] == tt[None, :]) & used[:, None] & used[None, :]
    t["head_sum"] = g.astype(float)
    m = np.full((P, 4, DB * DT), 0.0)
    for rnd in range(4):
        b = 2 * rnd + combo // 2
        ok = (r[None, :] // DT == b[:, None]) & (r[None, :] % DT <= tt[:, None])
        m[:, rnd] = np.where(ok, 0.0, NEG)
    t["new_mask"] = m.reshape(P, -1)
    key = np.arange(WIN)
    t["win_mask"] = np.where(key[None, :] > tt[:, None], 0.0, NEG)
    t["blk1"] = np.tile(np.arange(1, 17), (P, 1))
    blk = (i[:, None] // DH == i[None, :] // DH) / DH
    t["half_mean"] = blk
    t["pair_in_page"] = (i % 64)[:, None]
    t["first_page"] = (i < 64)[:, None].astype(float)
    t["second_page"] = (i >= 64)[:, None].astype(float)
    t["before"] = (i[:, None] < i[None, :]).astype(float)
    t["expert"] = np.tile(np.arange(NEXP), (P, 1))
    t["token"] = np.stack([i, i + 128, i + 256], 1)
    t["expert_mod"] = (i % NEXP)[:, None]
    t["over_id"] = np.tile(np.arange(OVER), (P, 1))
    m = np.zeros((P, NEXP))
    m[np.arange(96), np.arange(96) % NEXP] = 1
    t["expert_row"] = m
    t["one"] = np.ones((P, 1))
    t["eps"] = np.full((P, 1), EPS)
    cols, at = {}, 0
    for k, v in t.items():
        cols[k] = (at, at + v.shape[1])
        at += v.shape[1]
    return np.concatenate(list(t.values()), 1).astype(np.float32), cols



class Steps:

    def __init__(self, eng, own, sem):
        self.eng, self.own, self.sem, self.count = eng, own, sem, {}

    def __call__(self, ins, name=None):
        name = name or self.own
        self.count[name] = self.count.get(name, 0) + 1
        ins.then_inc(self.sem(name), 1)
        self.eng.wait_ge(self.sem(name), self.count[name])


def program(nc, a, outs, stages=9):
    _, CC = constants()
    ncols = max(e for _, e in CC.values())
    (y_prompt, y_sample, kv_prompt, kv_sample, win_prompt, win_sample,
     C_prompt, n_prompt, m_prompt, C_sample, n_sample, m_sample) = outs
    ctx = ExitStack()
    with ctx:
        def sb(name, shape, dt=F32):
            return ctx.enter_context(nc.sbuf_tensor(name, shape, dt))

        names = {}

        def sem(name):
            if name not in names:
                names[name] = ctx.enter_context(nc.semaphore(name))
            return names[name]

        mod_dram = nc.dram_tensor("mod_rows", [9, 6 * D], F32).ap()
        h2_dram = nc.dram_tensor("h2_rows", [NTOK, D], F32).ap()
        y_dram = nc.dram_tensor("expert_rows", [NBLK * CAP, D], F32).ap()
        slot_dram = nc.dram_tensor("slot_token", [(NBLK + 1) * CAP, 1], F32).ap()
        gate_dram = nc.dram_tensor("branch_gates", [DB * DT, AH * 3], F32).ap()

        C = sb("const_tables", [P, ncols])
        x = sb("x_rows", [P, 3, D])
        ARENA = 47300
        arena = sb("arena", [P, ARENA])

        def K(name, rows=P, lo=0, hi=None):
            b, e = CC[name]
            return C[0:rows, b + lo:(b + hi if hi is not None else e)]

        at = [NW * WORDS]

        def take(*shape, dt=F32):
            n = int(np.prod(shape))
            words = n if dt != BF16 else (n + 1) // 2
            words += words % 2
            assert at[0] + words <= ARENA, (at[0] + words, ARENA)
            v = arena[:, at[0]:at[0] + words]
            at[0] += words
            if dt != F32:
                v = v.bitcast(dt)
            v = v[:, 0:n]
            if len(shape) == 2:
                v = v.rearrange("p (a b) -> p a b", a=shape[0])
            if len(shape) == 3:
                v = v.rearrange("p (a b c) -> p a b c", a=shape[0], b=shape[1])
            return v

        slots = [arena[:, n * WORDS:(n + 1) * WORDS] for n in range(NW)]
        zr = take(3, ZN)
        hT = take(8, NTOK)
        qT = take(HPG, NTOK)
        qrT = take(HPG, NTOK)
        kselT = take(NTOK)
        kwinT = take(NTOK)
        oT = take(4, NTOK)
        hmT = take(MH, NTOK)
        w2 = take(2, 8, 128)
        colT = take(62)
        pebc = take(2)
        BASE = at[0]
        mq = take(8, NTOK)
        AFTER_MQ = at[0]

        bank_v = [ctx.enter_context(nc.psum_tensor(f"bank_v{n}", [P, 512], F32)) for n in range(4)]
        bank_s = [ctx.enter_context(nc.psum_tensor(f"bank_s{n}", [P, 512], F32)) for n in range(4)]
        tags = {"v": [], "s": [], "v_taken": [], "s_taken": []}
        cur = {}

        def fill(pe, ring, tag):
            n = len(tags[ring])
            tags[ring].append(tag)
            if n >= 4:
                pe.wait_ge(sem(f"{ring}_drained"), n - 3)
            return (bank_v if ring == "v" else bank_s)[n % 4]

        def filled(ring, ins):
            ins.then_inc(sem(f"{ring}_filled"), 1)

        def drain(eng, ring, tag):
            n = len(tags[ring + "_taken"])
            assert tags[ring][n] == tag, (tags[ring][n], tag)
            tags[ring + "_taken"].append(tag)
            eng.wait_ge(sem(f"{ring}_filled"), n + 1)
            return (bank_v if ring == "v" else bank_s)[n % 4]

        def after(eng, ring, tag):
            n = len(tags[ring]) - 1 - tags[ring][::-1].index(tag)
            eng.wait_ge(sem(f"{ring}_drained"), n + 1)

        barriers = {}

        def barrier(eng, who):
            n = barriers[who] = barriers.get(who, 0) + 1
            eng.drain().then_inc(sem("stage_left"), 1)
            eng.wait_ge(sem("stage_left"), 5 * n)

        def vec(ap_):
            return ap_.rearrange("(a n) -> a n", a=1)

        A = a
        w_in, b_in = A["w_in"][0], A["b_in"][0]
        kt_ = lambda w: w.rearrange("(t p) n -> p t n", p=P)
        chunks = []
        def chunk_of(tag):
            kind, n = tag
            if kind == "ada":
                return kt_(A["w_ada"][0][:, n * 512:(n + 1) * 512])
            c, w = (ROW_CHUNKS[n][0], ROW_CHUNKS[n][1]) if kind == "row" else (COL_CHUNKS[n], 512)
            return kt_(w_in[:, c:c + w])

        for tag in [("ada", n) for n in range(4)] + STAGE1 + [("col", n) for n in range(2, len(COL_CHUNKS))]:
            chunks.append((tag, chunk_of(tag)))
        chunks.append((("up_m", 0), kt_(A["w_up_m"][0])))
        chunks.append((("up_a", 0), kt_(A["w_up_a"][0])))
        for n in range(2):
            chunks.append((("out", n), kt_(A["w_out"][0][:, n * 512:(n + 1) * 512])))
        NCHUNK = len(chunks)
        chunk_at = {c[0]: n for n, c in enumerate(chunks)}

        def weights(pe, tag):
            n = chunk_at[tag]
            pe.wait_ge(sem(f"weights_{n % NW}"), 16 * (n // NW + 1))
            src = chunks[n][1]
            t, w = src.shape[1], src.shape[2]
            return slots[n % NW][:, 0:t * w].rearrange("p (t n) -> p t n", t=t)

        at[0] = BASE + 2304
        csil = take(8, 9)
        crow = take(D)
        ctmp = take(D)
        gmix = take(D)
        gffn = take(D)
        mod = take(6 * D)
        hrow = take(2, D)
        rowbias = take(ZN)
        ssum = take(3)
        rstd = take(3)
        rows61 = take(P)
        sqs = take(D)
        at[0] = AFTER_MQ
        gi, gf, gb, ga_, gM, gnd, gml = (take(NTOK) for _ in range(7))
        gtmp = take(NTOK)
        gws, gwi = take(32), take(32)
        m0T = take(8)
        gwc = take(8)
        aT = take(3, 4)
        ndT = take(3, 4)
        wsT, wiT, wcT = take(4), take(4), take(4)
        wcb = take(32)
        n0r, n0T = take(P), take(32)
        nqT = take(4)
        DTt = take(2, 416)
        WT = take(2, 416)
        STt = take(2, 416)
        krow = take(2, 384)
        C0h = take(2, 1024)
        CTh = take(2, 1024)
        vw = take(2, 256)
        wsb = take(2, 8)
        vwb = take(2, 1024)
        numI = take(2, 32)
        hrw = take(2, 384)
        den = take(2, 4)
        Cn = take(2, 1024)
        Cpr = take(2, P)
        npr = take(MH, P)
        nsr = take(MH, P)
        n0s = take(MH, P)
        mfin = take(16)
        at[0] = BASE
        sq = take(512)
        qg = take(64)
        kg = take(3, 64)
        rs8 = take(8)
        qn = take(2, 512)
        qr = take(2, 512)
        rt = take(4, 64)
        pair = take(1024)
        cTp = take(4, P)
        y2c = take(2, 128)
        kcT = take(P)
        vcT = take(P)
        tmpT = take(P)
        vcr = take(2, P)
        gt24 = take(3, 24)
        sc_c = take(2, 128)
        ptc = take(8, P)
        ob = take(2, 512)
        stat = take(4, 16)
        Su = take(2, 512)
        Pu = take(2, 512)
        PTu = take(2, 512)
        moT = take(MH, NTOK)
        assert at[0] <= 42000
        at[0] = ARENA - 16 * NTOK
        gT = take(16, NTOK)
        at[0] = ARENA - 16 * NTOK - 400
        grd = take(4, 3)
        idx_f = take(64)
        idx_t = take(64)
        idx_u = take(32, dt=U32)
        pgi = take(64, dt=I32)
        pgf = take(64)
        assert at[0] <= ARENA - 16 * NTOK
        at[0] = 0
        pt_even = take(8, 1024)
        at[0] = hT.offset
        wn_even = take(2, 4, 256)
        at[0] = zr.offset
        wn_odd = take(2, 4, 256)
        Ss = take(1056)
        Sw = take(544)
        assert at[0] <= zr.offset + 2 * ZN
        at[0] = BASE
        pts, wns = (pt_even, take(8, 1024)), (wn_even, wn_odd)
        cT = take(2, 1024)
        ksT = take(2, 1024)
        kwT = cT[:, 0, :].rearrange("p (b n) -> p b n", b=2)
        Sc = take(64)
        PTs = take(9, P)
        PTw = cT[:, 1, 0:640].rearrange("p (t n) -> p t n", t=5)
        PTc = take(P)
        kc2 = take(2, 64)
        vc2 = take(2, 64)
        t2 = take(P)
        y22 = take(P)
        vcr2 = take(2, P)
        pnrm = take(64)
        imp = take(64)
        imb = take(4, 16)
        st4 = take(16)
        qTr = take(2, 32)
        qrTr = take(2, 32)
        orow = take(64)
        assert at[0] <= ARENA - 16 * NTOK - 400, at[0]

        def ze(i, n, c, w):
            return zr[0:n, i, c:c + w]

        def kvrows(i, n, kind, g=None):
            c = ZKV + kind * 128
            return ze(i, n, c, 128) if g is None else ze(i, n, c + g * DH, DH)

        ident = K("ident")
        UNITS = [(br, i, g, jp) for br in range(2) for i in range(2) for g in range(2) for jp in range(2)]
        chunk_last = {}

        GATE_GROUPS = [(c, m) for c in range(2, len(COL_CHUNKS)) for m in range(4)]

        def quarters(w):
            return [(c0, min(P, w - c0)) for c0 in range(0, w, P)]

        def cols_of(lo, n):
            return b_in[lo:lo + n * P].rearrange("(a p) -> a p", p=P)

        def bc(v, n):
            return v.partition_broadcast(n)

        first = [(C[:, :], A["tables"]),
                 (crow[0:1, :], A["c_prompt"]), (crow[1:9, :], A["c_sample"])]
        small = [(rows61[0:8, :], cols_of(0, 8)), (rows61[8:12, :], cols_of(1536, 4)),
                 (rows61[12:28, :], cols_of(3360, 16)),
                 (rows61[28:29, 0:64], A["k_norm_g"][0][0:1]), (rows61[28:29, 64:128], A["k_norm_g"][0][0:1]),
                 (rows61[29:45, :], A["cmp_pe_k"][0].rearrange("(a r) d -> a (r d)", r=2)),
                 (rows61[45:61, :], A["cmp_pe_v"][0].rearrange("(a r) d -> a (r d)", r=2)),
                 (gmix[0:9, :], bc(A["g_mix"][0], 9)), (gffn[0:9, :], bc(A["g_ffn"][0], 9)),
                 (mod[0:9, :], bc(A["b_ada"][0], 9)),
                 (rowbias[:, 0:512], bc(b_in[1024:1536], P)), (rowbias[:, 512:ZN], bc(b_in[2048:3360], P)),
                 (x[:, 0, :], A["x_prompt"][0][0:128]), (x[:, 1, :], A["x_prompt"][0][128:256]),
                 (x[0:32, 2, :], A["x_sample"].rearrange("b t d -> (b t) d"))]
        for kind, name in enumerate(("cmp_w_k", "cmp_w_v")):
            src = A[name][0].rearrange("(h u r) d e -> r h d u e", h=2, r=2)
            for par in range(2):
                for half in range(2):
                    small.append((w2[par * DH:(par + 1) * DH, kind, :, half * DH:(half + 1) * DH], src[par, half]))
        L1_FIRST, L1_SMALL = len(first), len(small)


        def view_at(v_, *shape):
            o = v_.offset
            n = int(np.prod(shape))
            w_ = arena[:, o:o + n]
            return w_.rearrange("p (a b) -> p a b", a=shape[0]) if len(shape) == 2 else w_

        brow = view_at(zr, 3 * D)
        bmid = view_at(zr, 2, 3 * D)[:, 1]
        merged = view_at(qT, 8, NTOK)
        at[0] = BASE
        squares = take(D)
        modl = take(3, D)
        h2 = take(2, D)
        h2T = take(8, NTOK)
        assert at[0] <= 38400
        at[0] = 38400
        wr = take(8, NEXP)
        brt = take(NEXP)
        ss2 = take(3)
        L = take(3, NEXP)
        m8 = take(3, 8)
        i8 = take(3, 8, dt=U32)
        i8f = take(3, 8)
        pick = take(4, 3 * NEXP)
        picked = take(3, NEXP)
        pos = take(3, NEXP)
        cnt = take(NEXP)
        ov = take(NEXP)
        ove = take(NEXP)
        ovs = take(NEXP)
        base_ = take(NEXP)
        tmp32 = take(OVER * NEXP)
        tmp32b = take(OVER * NEXP)
        destf = take(3, 4)
        zslot = take(P)
        slotr = take(P)
        assert at[0] <= 41000, at[0]
        at[0] = 41000
        bias3 = take(3 * D, dt=BF16)
        gt2 = take(D)
        gate4 = take(3, 4)
        dest = take(12, dt=U32)
        slotu = take(NBLK + 1, dt=U32)
        over_e = take(OVER, dt=I32)
        over_n = take(2, dt=I32)
        ohx = take(NBLK + 1)
        bfi = take(OVER)
        NE = 6
        eslots = [arena[:, n * WORDS:(n + 1) * WORDS] for n in range(NE)]
        at[0] = NE * WORDS
        xg = take(D)
        xT = take(8, CAP)
        gbuf = take(2, 512)
        sgb = take(2, 512)
        ub = take(2, 512)
        actT = take(2, 4 * CAP)
        yb = take(512)
        idx_cur = take(2, dt=U32)
        bsel_gu = take(CAP, dt=BF16)
        bsel_dn = take(CAP, dt=BF16)
        assert at[0] <= 38400
        at[0] = 0
        yk = take(12, D)
        fin = take(3, D)
        ROUNDS_OVER = -(-NTOK // CAP) - 1

        def ebank(k):
            return (bank_v + bank_s)[k]

        block = ctx.enter_context(nc.Block())

        def pe_late(pe, mm, tr, col_chunk, used):
            for name, src, need in (("up_m", hmT, "gated"), ("up_a", oT, None)):
                if need:
                    pe.wait_ge(sem(need), 1)
                w = weights(pe, (name, 0))
                for m in range(8):
                    b = fill(pe, "v", (name, m))
                    for t in range(4):
                        last = mm(b[:, 0:NTOK], w[:, t, m * P:(m + 1) * P], src[:, t, :], t == 0, t == 3)
                    filled("v", last)
                used((name, 0), "v")
            pe.wait_ge(sem("mod_reloaded"), 16 * 3)

            def spread(i, n, row, tag):
                o = TILES[i][0]
                b = fill(pe, "v", tag)
                filled("v", mm(b[0:n, :], K("sel", 9, o, o + n), row, True, True))

            pe.wait_ge(sem("merged_ready"), 8)
            for half in range(2):
                w = weights(pe, ("out", half))
                hs = slice(half * 512, half * 512 + 512)
                for i, (o, n) in enumerate(TILES):
                    b = fill(pe, "v", ("mix", half, i))
                    for t in range(8):
                        if i < 2:
                            last = mm(b[0:n, :], merged[:, t, o:o + n], w[:, t, :], t == 0, t == 7)
                        else:
                            for j in range(4):
                                last = mm(b[32 * j:32 * j + n, 0:P], merged[:, t, o:o + n], w[:, t, j * P:(j + 1) * P], t == 0, t == 7)
                    filled("v", last)
                    spread(i, n, modl[0:9, 0, hs], ("gate1", half, i))
                used(("out", half), "v")
            for i, (o, n) in enumerate(TILES):
                for half in range(2):
                    hs = slice(half * 512, half * 512 + 512)
                    spread(i, n, modl[0:9, 2, hs], ("scale2", i, half))
                    spread(i, n, modl[0:9, 1, hs], ("shift2", i, half))
                for half in range(2):
                    pe.wait_ge(sem("h2_rows"), 2 * i + half + 1)
                    b = fill(pe, "s", ("h2T", i, half))
                    for j in range(4):
                        last = tr(b[:, j * n:(j + 1) * n], h2[0:n, i % 2, (4 * half + j) * P:(4 * half + j + 1) * P])
                    filled("s", last)
            pe.wait_ge(sem("router_loaded"), 32)
            after(pe, "s", ("h2T", 2, 1))
            for i, (o, n) in enumerate(TILES):
                b = fill(pe, "v", ("router", i))
                for t in range(8):
                    last = mm(b[0:n, 0:NEXP], h2T[:, t, o:o + n], wr[:, t, :], t == 0, t == 7)
                filled("v", last)
            pe.wait_ge(sem("picked_ready"), 3)
            for i, (o, n) in enumerate(TILES):
                b = fill(pe, "v", ("place", i))
                for j in range(i + 1):
                    nj = TILES[j][1]
                    lhs = K("before", nj, 0, n) if j == i else K("ones", nj, 0, n)
                    last = mm(b[0:n, 0:NEXP], lhs, picked[0:nj, j, :], j == 0, j == i)
                filled("v", last)
            b = fill(pe, "v", "count")
            for i, (o, n) in enumerate(TILES):
                last = mm(b[:, 0:NEXP], K("ones", n), picked[0:n, i, :], i == 0, i == 2)
            filled("v", last)
            pe.wait_ge(sem("slots_loaded"), 16)
            b = fill(pe, "v", "slots")
            filled("v", tr(b[0:CAP, 0:NBLK + 1], slotr[0:NBLK + 1, 0:CAP]))
            barrier(pe, "pe")
            W = eslots

            def beside(bank, half):
                return ebank(bank)[half * CAP:(half + 1) * CAP, :]

            def turn(bank, rows, c0):
                for j in range(4):
                    last = tr(ebank(bank)[:, j * CAP:(j + 1) * CAP], rows[:, c0 + j * P:c0 + (j + 1) * P])
                return last

            def pe_block(e):
                pe.wait_ge(sem("rows_turned"), 2 * e + 2)
                pe.wait_ge(sem("gu_bias_ready"), e + 1)
                for c in range(2):
                    pe.wait_ge(sem(f"expert_weights_{2 * c}"), 16 * e + 16)
                    pe.wait_ge(sem(f"expert_weights_{2 * c + 1}"), 16 * e + 16)
                    pe.wait_ge(sem("gu_drained"), 2 * e + c + 1)
                    for q in range(2):
                        b0 = q * D + c * 512
                        mm(beside(c, q), bsel_gu[0:96, :], bias3[0:96, b0:b0 + 512], True, False)
                    for t in range(8):
                        for q in range(2):
                            w = W[2 * c + q].rearrange("p (t n) -> p t n", t=8)
                            last = mm(beside(c, q), xT[:, t, :], w[:, t, :], False, t == 7)
                    last.then_inc(sem("gu_filled"), 1)
                for c in range(2):
                    pe.wait_ge(sem("act_ready"), 2 * e + c + 1)
                    if c == 1:
                        pe.wait_ge(sem("rows_turned"), 2 * e + 3)
                    pe.sem_inc(sem("act_seen"), 1)
                    turn(6 + c, ub[0:CAP, c, :], 0).then_inc(sem("act_turning"), 1)
                    if c == 0:
                        pe.wait_ge(sem("act_turned"), 2 * e + 2)
                        pe.wait_ge(sem("rows_gathered"), 16 * e + 32)
                        pe.sem_inc(sem("rows_seen"), 1)
                        turn(7, xg[0:CAP, :], 0).then_inc(sem("rows_turning"), 1)
                        pe.wait_ge(sem("act_turned"), 2 * e + 3)
                        pe.sem_inc(sem("rows_seen"), 1)
                        turn(6, xg[0:CAP, :], 512).then_inc(sem("rows_turning"), 1)
                        pe.wait_ge(sem("y_drained"), e + 1)
                        pe.wait_ge(sem("dn_bias_ready"), e + 1)
                        for half in range(2):
                            b0 = 2 * D + half * 512
                            mm(beside(4, half), bsel_dn[0:96, :], bias3[0:96, b0:b0 + 512], True, False)
                    pe.wait_ge(sem("act_turned"), 2 * e + 3 + c)
                    pe.wait_ge(sem(f"expert_weights_{4 + c}"), 16 * e + 16)
                    w = W[4 + c].rearrange("p (t n) -> p t n", t=4)
                    for t in range(4):
                        for half in range(2):
                            last = mm(beside(4, half), actT[:, c, t * CAP:(t + 1) * CAP], w[:, t, half * 512:half * 512 + 512],
                                      False, c == 1 and t == 3)
                    last.then_inc(sem("dn_filled"), 1)

            pe.wait_ge(sem("rows_gathered"), 16)
            turn(7, xg[0:CAP, :], 0).then_inc(sem("rows_turning"), 1)
            turn(6, xg[0:CAP, :], 512).then_inc(sem("rows_turning"), 1)
            blocks(pe, pe_block)
            barrier(pe, "pe")
            pe.wait_ge(sem("gate2_loaded"), 16)
            for i, (o, n) in enumerate(TILES):
                for half in range(2):
                    spread(i, n, gt2[0:9, half * 512:half * 512 + 512], ("gate2", i, half))
            barrier(pe, "pe")

        def rounds(front, scored, selected):
            front(0)
            for r in range(4):
                scored(r)
                if r < 3:
                    front(r + 1)
                selected(r)

        def blocks(eng, body, further=None):
            with eng.Fori(0, NEXP) as e:
                body(e)
            n = eng.value_load(over_n[0:1, 0:1], min_val=0, max_val=OVER)
            with eng.If(n > 0):
                with eng.Fori(NEXP, NEXP + n) as e:
                    (further or body)(e)

        def ve_late(ve, v, got, copy, tt, ts, stt, red, recip):
            VD, add, mul, sub, mx, mn = "v_drained", ALU.add, ALU.mult, ALU.subtract, ALU.max, ALU.min
            for m in range(8):
                b = got(("up_m", m))
                if m == 0:
                    ve.wait_ge(sem("merge_gates"), 4)
                tt(merged[:, m, :], b[:, 0:NTOK], gT[:, m, :], mul, VD)
            for m in range(8):
                b = got(("up_a", m))
                tt(gT[:, 8 + m, :], b[:, 0:NTOK], gT[:, 8 + m, :], mul, VD)
                tt(merged[:, m, :], merged[:, m, :], gT[:, 8 + m, :], add, "merged_ready")
            ve.wait_ge(sem("mod_reloaded"), 16 * 3)
            for half in range(2):
                hs = slice(half * 512, half * 512 + 512)
                for i, (o, n) in enumerate(TILES):
                    b = got(("mix", half, i))
                    t_ = h2[0:n, 0, 0:512]
                    if i < 2:
                        copy(t_, b[0:n, :], VD)
                    else:
                        for j in range(4):
                            copy(h2[0:n, 0, j * P:(j + 1) * P], b[32 * j:32 * j + n, 0:P], VD if j == 3 else None)
                    b = got(("gate1", half, i))
                    tt(t_, t_, b[0:n, :], mul, VD)
                    tt(x[0:n, i, hs], x[0:n, i, hs], t_, add, "x_mixed")
            for i, (o, n) in enumerate(TILES):
                ve.wait_ge(sem("rms"), 4 + i)
                recip(ss2[0:n, i:i + 1], ss2[0:n, i:i + 1])
                if i == 2:
                    after(ve, "s", ("h2T", 0, 1))
                    ve.wait_ge(sem("h2_stored_0"), 16)
                for half in range(2):
                    hs = slice(half * 512, (half + 1) * 512)
                    b = got(("scale2", i, half))
                    stt(h2[0:n, i % 2, hs], x[0:n, i, hs], ss2[0:n, i:i + 1], b[0:n, :], mul, mul, VD)
                    b = got(("shift2", i, half))
                    tt(h2[0:n, i % 2, hs], h2[0:n, i % 2, hs], b[0:n, :], add, VD)
                    v(ve.nop(), "h2_rows")
            ve.wait_ge(sem("bias_loaded"), 32)
            bm = bmid.bitcast(BF16)[0:32, 0:3 * D]
            br_ = brow[0:32, :]
            copy(bias3[0:32, :], br_)
            tt(br_, br_, bias3[0:32, :], sub)
            copy(bm, br_)
            copy(bias3[32:64, :], br_)
            tt(br_, br_, bm, sub)
            copy(bias3[64:96, :], br_)
            v(ve.memset(zslot[:, :], 0.0), "zero_slots")
            for i, (o, n) in enumerate(TILES):
                b = got(("router", i))
                l_ = L[0:n, i, :]
                tt(l_, b[0:n, 0:NEXP], brt[0:n, :], add, VD)
                v(ve.max(m8[0:n, i, :], l_))
                v(ve.max_index(i8[0:n, i, :], m8[0:n, i, :], l_))
                copy(i8f[0:n, i, :], i8[0:n, i, :])
                for k in range(TOPK):
                    pk = pick[0:n, k, i * NEXP:(i + 1) * NEXP]
                    ts(pk, K("expert", n), i8f[0:n, i, k:k + 1], ALU.is_equal)
                    if k == 1:
                        tt(picked[0:n, i, :], pick[0:n, 0, i * NEXP:(i + 1) * NEXP], pk, add)
                    if k > 1:
                        tt(picked[0:n, i, :], picked[0:n, i, :], pk, add, "picked_ready" if k == 3 else None)
                ts(gate4[0:n, i, :], m8[0:n, i, 0:4], m8[0:n, i, 0:1], sub, name="gate_shifted")
            for i, (o, n) in enumerate(TILES):
                b = got(("place", i))
                copy(pos[0:n, i, :], b[0:n, 0:NEXP], VD)
            b = got("count")
            copy(cnt, b[:, 0:NEXP], VD)
            ts(ov, cnt, float(CAP), ALU.is_gt)
            for j in range(2, ROUNDS_OVER + 1):
                ts(ovs, cnt, float(CAP * j), ALU.is_gt)
                tt(ov, ov, ovs, add)
            v(ve.memset(ovs, 0.0))
            v(ve.tensor_tensor_scan(ove, ov, ovs, 0.0, add, add))
            tt(ovs, ove, ov, sub)
            ts(base_, ovs, float(NEXP - 1), add)
            tt(base_, base_, K("expert"), sub)
            for i, (o, n) in enumerate(TILES):
                p_ = pos[0:n, i, :]
                t_ = tmp32[0:n, 0:NEXP]
                ts(t_, p_, float(CAP), ALU.is_ge)
                tt(t_, t_, base_[0:n, :], mul)
                tt(t_, t_, K("expert", n), add)
                stt(p_, t_, float(CAP), p_, mul, add)
                for k in range(TOPK):
                    tt(t_, pick[0:n, k, i * NEXP:(i + 1) * NEXP], p_, mul)
                    red(destf[0:n, i, k:k + 1], t_, add)
                copy(dest[0:n, 4 * i:4 * i + 4], destf[0:n, i, :])
            v(ve.nop(), "dest_ready")
            o3 = lambda t_: t_.rearrange("p (b e) -> p b e", b=OVER)
            full = [P, OVER, NEXP]
            ids = K("over_id").unsqueeze(2).to_broadcast(full)
            tt(o3(tmp32), ovs.unsqueeze(1).to_broadcast(full), ids, ALU.is_le)
            tt(o3(tmp32b), ove.unsqueeze(1).to_broadcast(full), ids, ALU.is_gt)
            tt(o3(tmp32), o3(tmp32), o3(tmp32b), mul)
            tt(o3(tmp32), o3(tmp32), K("expert").unsqueeze(1).to_broadcast(full), mul)
            red(bfi, o3(tmp32), add)
            copy(over_e, bfi)
            copy(over_n[:, 0:1], ove[:, NEXP - 1:NEXP])
            v(ve.memset(ohx, 0.0))
            copy(ohx[0:96, 0:NEXP], K("expert_row", 96))
            ts(ohx[0:96, NEXP:NBLK], bfi[0:96, :], K("expert_mod", 96), ALU.is_equal)
            for i, (o, n) in enumerate(TILES):
                ve.wait_ge(sem("gate_exp"), i + 1)
                red(ss2[0:n, i:i + 1], gate4[0:n, i, :], add)
                recip(ss2[0:n, i:i + 1], ss2[0:n, i:i + 1])
                ts(gate4[0:n, i, :], gate4[0:n, i, :], ss2[0:n, i:i + 1], mul)
            b = got("slots")
            copy(slotu[0:CAP, :], b[0:CAP, 0:NBLK + 1], VD)
            v(ve.nop(), "slots_ready")
            for _ in range(2):
                ve.nop().then_inc(sem("gu_drained"), 1)
            barrier(ve, "ve")
            n_own = [0]

            def select(dst, e):
                return ve.tensor_scalar(dst[0:96, :], ohx[0:96, bass.ds(e, 1)].to_broadcast([96, CAP]), 1.0, None, mul)

            v(select(bsel_gu, 0), "gu_bias_ready")
            v(select(bsel_dn, 0), "dn_bias_ready")

            def ve_block(e):
                for c in range(2):
                    g_, u_, s_ = gbuf[0:CAP, c, :], ub[0:CAP, c, :], sgb[0:CAP, c, :]
                    ve.wait_ge(sem("gu_filled"), 2 * e + c + 1)
                    ve.tensor_scalar(g_, ebank(c)[0:CAP, :], 7.0, None, mn).then_inc(sem("g_ready"), 1)
                    ve.tensor_scalar(u_, ebank(c)[CAP:2 * CAP, :], 7.0, -7.0, mn, mx).then_inc(sem("gu_drained"), 1)
                    ve.wait_ge(sem("g_ready"), 2 * e + c + 1)
                    ve.wait_ge(sem("gu_drained"), 2 * e + c + 3)
                    ve.scalar_tensor_tensor(out=u_, in0=u_, scalar=1.0, in1=g_, op0=add, op1=mul).then_inc(sem("gu_product"), 1)
                    ve.wait_ge(sem("gu_product"), 2 * e + c + 1)
                    ve.wait_ge(sem("sigmoid_ready"), 2 * e + c + 1)
                    ve.tensor_tensor(u_, u_, s_, mul).then_inc(sem("act_ready"), 1)
                ve.wait_ge(sem("gu_filled"), 2 * e + 2)
                select(bsel_gu, e + 1).then_inc(sem("gu_bias_ready"), 1)
                ve.wait_ge(sem("dn_filled"), 2 * e + 1)
                select(bsel_dn, e + 1).then_inc(sem("dn_bias_ready"), 1)

            blocks(ve, ve_block)
            barrier(ve, "ve")
            for i, (o, n) in enumerate(TILES):
                for k in range(TOPK):
                    ve.wait_ge(sem(f"picked_rows_{i}"), 16 * 4)
                    if k == 0:
                        ts(fin[0:n, i, :], yk[0:n, 4 * i, :], gate4[0:n, i, 0:1], mul)
                    else:
                        stt(fin[0:n, i, :], yk[0:n, 4 * i + k, :], gate4[0:n, i, k:k + 1], fin[0:n, i, :], mul, add)
                for half in range(2):
                    hs = slice(half * 512, half * 512 + 512)
                    b = got(("gate2", i, half))
                    tt(fin[0:n, i, hs], fin[0:n, i, hs], b[0:n, :], mul, VD)
                tt(fin[0:n, i, :], fin[0:n, i, :], x[0:n, i, :], add, "y_rows")
            barrier(ve, "ve")

        def se_late(se, act, got):
            SD = "s_drained"
            se.wait_ge(sem("x_mixed"), 6)
            for i, (o, n) in enumerate(TILES):
                act(squares[0:n, :], x[0:n, i, :], ACT.Square, accum_out=ss2[0:n, i:i + 1])
                act(ss2[0:n, i:i + 1], ss2[0:n, i:i + 1], ACT.Sqrt, "rms", bias=K("eps", n), scale=1.0 / D)
            for i, (o, n) in enumerate(TILES):
                for half in range(2):
                    b = got(("h2T", i, half))
                    act(h2T[:, 4 * half:4 * half + 4, o:o + n], b[:, 0:4 * n].rearrange("p (j n) -> p j n", j=4), ACT.Copy, SD)
            for i, (o, n) in enumerate(TILES):
                se.wait_ge(sem("gate_shifted"), i + 1)
                act(gate4[0:n, i, :], gate4[0:n, i, :], ACT.Exp, "gate_exp")
            for _ in range(2):
                se.nop().then_inc(sem("act_turned"), 1)
            se.nop().then_inc(sem("y_drained"), 1)
            se.sem_inc(sem("y_stored"), 32)
            barrier(se, "se")
            for k, bank in ((0, 7), (1, 6)):
                se.wait_ge(sem("rows_turning"), k + 1)
                se.activation(xT[:, 4 * k:4 * k + 4, :], ebank(bank)[:, 0:4 * CAP].rearrange("p (j n) -> p j n", j=4), ACT.Copy).then_inc(sem("rows_turned"), 1)

            def se_block(e):
                for c in range(2):
                    se.wait_ge(sem("g_ready"), 2 * e + c + 1)
                    se.activation(sgb[0:CAP, c, :], gbuf[0:CAP, c, :], ACT.Sigmoid, scale=1.702).then_inc(sem("sigmoid_ready"), 1)

                def act_turn(c):
                    se.wait_ge(sem("act_turning"), 2 * e + c + 1)
                    se.activation(actT[:, c, :], ebank(6 + c)[:, 0:4 * CAP], ACT.Copy).then_inc(sem("act_turned"), 1)

                act_turn(0)
                for k, bank in ((0, 7), (1, 6)):
                    se.wait_ge(sem("rows_turning"), 2 * e + 3 + k)
                    se.activation(xT[:, 4 * k:4 * k + 4, :], ebank(bank)[:, 0:4 * CAP].rearrange("p (j n) -> p j n", j=4), ACT.Copy).then_inc(sem("rows_turned"), 1)
                act_turn(1)
                se.wait_ge(sem("dn_filled"), 2 * e + 2)
                se.wait_ge(sem("y_stored"), 32 * e + 32)
                se.activation(yb[:, :], ebank(4)[:, :], ACT.Copy).then_inc(sem("y_drained"), 1)
                se.wait_ge(sem("y_drained"), e + 2)
                for half in range(2):
                    dst = y_dram.rearrange("(b s) d -> b s d", s=CAP)[bass.ds(e, 1), :, half * 512:half * 512 + 512]
                    se.dma_start(dst.rearrange("o s d -> (o s) d"), yb[half * CAP:(half + 1) * CAP, :]).then_inc(sem("y_stored"), 16)

            def se_further(e):
                se_block(e)
                se.wait_ge(sem("y_stored"), 32 * e + 64)

            blocks(se, se_block, se_further)
            se.wait_ge(sem("y_stored"), 32 * NEXP + 32)
            barrier(se, "se")
            barrier(se, "se")

        def pool_late(pool, dma):
            for k, part in enumerate((2, 3, 4)):
                dma(modl[0:9, k, :], mod_dram[:, part * D:(part + 1) * D], "mod_reloaded")
            dma(wr, A["w_router"][0].rearrange("(t p) e -> p t e", p=P), "router_loaded")
            dma(brt, bc(A["b_router"][0], P), "router_loaded")
            pool.wait_ge(sem("merged_ready"), 8)
            dma(gt2[0:9, :], mod_dram[:, 5 * D:6 * D], "gate2_loaded")
            dma(brow[0:32, 0:2 * D], A["b_gu"][0], "bias_loaded")
            dma(brow[0:32, 2 * D:3 * D], A["b_dn"][0], "bias_loaded")
            for i, (o, n) in enumerate(TILES):
                pool.wait_ge(sem("h2_rows"), 2 * i + 2)
                dma(h2_dram[o:o + n, :], h2[0:n, i % 2, :], f"h2_stored_{i}")
            pool.wait_ge(sem("zero_slots"), 1)
            dma(slot_dram.rearrange("(b s) o -> b (s o)", s=CAP), zslot[0:NBLK + 1, 0:CAP], "slots_cleared")
            pool.wait_ge(sem("slots_cleared"), 16)
            pool.wait_ge(sem("dest_ready"), 1)
            for i, (o, n) in enumerate(TILES):
                for k in range(TOPK):
                    pool.indirect_dma_start(out=slot_dram, out_offset=bass.IndirectOffsetOnAxis(dest[0:n, 4 * i + k:4 * i + k + 1], 0),
                                            in_=K("token", n, i, i + 1), in_offset=None).then_inc(sem("slots_written"), 16)
            pool.wait_ge(sem("slots_written"), 16 * 12)
            dma(slotr[0:NBLK + 1, 0:CAP], slot_dram.rearrange("(b s) o -> b (s o)", s=CAP), "slots_loaded")
            pool.wait_ge(sem("slots_loaded"), 16)
            for i in range(3):
                pool.wait_ge(sem(f"h2_stored_{i}"), 16)
            barrier(pool, "pool")
            def gather(e):
                pool.tensor_copy(idx_cur[0:CAP, 0:1], slotu[0:CAP, bass.ds(e, 1)]).then_inc(sem("block_index"), 1)
                pool.wait_ge(sem("block_index"), e + 1)
                pool.sem_inc(sem("block_index_seen"), 1)
                pool.indirect_dma_start(out=xg[0:CAP, :], out_offset=None, in_=h2_dram,
                                        in_offset=bass.IndirectOffsetOnAxis(idx_cur[0:CAP, 0:1], 0)).then_inc(sem("rows_gathered"), 16)

            gather(0)

            def pool_block(e):
                pool.wait_ge(sem("rows_turning"), 2 * e + 2)
                gather(e + 1)

            blocks(pool, pool_block)
            barrier(pool, "pool")
            for i, (o, n) in enumerate(TILES):
                for k in range(TOPK):
                    pool.indirect_dma_start(out=yk[0:n, 4 * i + k, :], out_offset=None, in_=y_dram,
                                            in_offset=bass.IndirectOffsetOnAxis(dest[0:n, 4 * i + k:4 * i + k + 1], 0)).then_inc(sem(f"picked_rows_{i}"), 16)
            for i, (o, n) in enumerate(TILES):
                pool.wait_ge(sem("y_rows"), i + 1)
                out = y_prompt[0][o:o + n, :] if i < 2 else y_sample.rearrange("b t d -> (b t) d")
                dma(out, fin[0:n, i, :], "output_stored")
            pool.wait_ge(sem("output_stored"), 48)
            barrier(pool, "pool")

        def sp_late(sp):
            wg, wd = A["w_gu"][0], A["w_dn"][0]

            def load_chunk(k, e):
                if k < 4:
                    c0 = (k % 2) * D + (k // 2) * 512
                    src = wg[bass.ds(e, 1), :, c0:c0 + 512].rearrange("o (t p) n -> p (o t) n", p=P)
                    dst = eslots[k].rearrange("p (t n) -> p t n", t=8)
                else:
                    r0 = (k - 4) * 512
                    src = wd[bass.ds(e, 1), r0:r0 + 512, :].rearrange("o (t p) n -> p (o t) n", p=P)
                    dst = eslots[k].rearrange("p (t n) -> p t n", t=4)
                sp.dma_start(dst, src).then_inc(sem(f"expert_weights_{k}"), 16)

            sp.wait_ge(sem("further_cleared"), 16 * (D // P))
            for k in range(3):
                last_in_slot = max(n for n in range(NCHUNK) if n % NW == k)
                ring, m = chunk_last[chunks[last_in_slot][0]]
                sp.wait_ge(sem(f"{ring}_filled"), m)
                load_chunk(k, 0)
            barrier(sp, "sp")
            for k in range(3, 6):
                load_chunk(k, 0)

            def reload(e1, expert):
                for k in range(6):
                    if k < 4:
                        sp.wait_ge(sem("gu_filled"), 2 * e1 - 1 + k // 2)
                    else:
                        sp.wait_ge(sem("dn_filled"), 2 * e1 + (k - 5))
                    load_chunk(k, expert)

            with sp.Fori(1, NEXP) as e:
                reload(e, e)
            n = sp.value_load(over_n[0:1, 0:1], min_val=0, max_val=OVER)
            with sp.If(n > 0):
                with sp.Fori(0, n) as b:
                    expert = sp.value_load(over_e[0:1, bass.ds(b, 1)], min_val=0, max_val=NEXP - 1)
                    reload(NEXP + b, expert)
            barrier(sp, "sp")
            barrier(sp, "sp")

        @block.tensor
        def _(pe):
            def mm(out, l, r, first, last):
                return pe.matmul(out, l, r, start=first, stop=last)

            def tr(out, in_):
                n = in_.shape[0]
                return pe.transpose(out, in_, ident[0:n, 0:n])

            def used(tag, ring):
                chunk_last[tag] = (ring, len(tags[ring]))

            pe.wait_ge(sem("c_silu"), 1)
            pe.wait_ge(sem("first_loads"), 16 * L1_FIRST)
            b = fill(pe, "v", "cT")
            for t in range(8):
                last = tr(b[:, t * 9:t * 9 + 9], crow[0:9, t * P:(t + 1) * P])
            filled("v", last)
            b = fill(pe, "s", "cols")
            pe.wait_ge(sem("small_loads"), 16 * L1_SMALL)
            filled("s", tr(b[:, 0:61], rows61[0:61, :]))
            after(pe, "v", "cT")

            def ada_chunk(n):
                w = weights(pe, ("ada", n))
                b = fill(pe, "v", ("ada", n))
                for t in range(8):
                    for j in range(4):
                        last = mm(b[32 * j:32 * j + 9, 0:P], csil[:, t, :], w[:, t, j * P:(j + 1) * P], t == 0, t == 7)
                filled("v", last)
                used(("ada", n), "v")

            for n in range(4):
                ada_chunk(n)
            pe.wait_ge(sem("mod_ready"), 1)

            def spread(i, n, part, half, tag):
                o = TILES[i][0]
                b = fill(pe, "v", tag)
                filled("v", mm(b[0:n, :], K("sel", 9, o, o + n), mod[0:9, part * D + half * 512:part * D + half * 512 + 512], True, True))

            for i, (o, n) in enumerate(TILES):
                for half in range(2):
                    spread(i, n, 1, half, ("scale", i, half))
                    spread(i, n, 0, half, ("shift", i, half))
            for i, (o, n) in enumerate(TILES):
                for half in range(2):
                    pe.wait_ge(sem("h_rows"), 2 * i + half + 1)
                    b = fill(pe, "s", ("hT", i, half))
                    for j in range(4):
                        last = tr(b[:, j * n:(j + 1) * n], hrow[0:n, i % 2, (4 * half + j) * P:(4 * half + j + 1) * P])
                    filled("s", last)
            after(pe, "s", ("hT", 2, 1))

            def row_chunk(c):
                w_ = ROW_CHUNKS[c][1]
                w = weights(pe, ("row", c))
                for i, (o, n) in enumerate(TILES):
                    b = fill(pe, "v", ("row", c, i))
                    for t in range(8):
                        if i < 2:
                            last = mm(b[0:n, 0:w_], hT[:, t, o:o + n], w[:, t, :], t == 0, t == 7)
                        else:
                            for j, (c0, cw) in enumerate(quarters(w_)):
                                last = mm(b[32 * j:32 * j + n, 0:cw], hT[:, t, o:o + n], w[:, t, c0:c0 + cw], t == 0, t == 7)
                    filled("v", last)
                used(("row", c), "v")

            def col_group(c, m):
                if m == 0:
                    cur["col"] = weights(pe, ("col", c))
                b = fill(pe, "s", ("col", c, m))
                for t in range(8):
                    last = mm(b[:, 0:NTOK], cur["col"][:, t, m * P:(m + 1) * P], hT[:, t, :], t == 0, t == 7)
                filled("s", last)
                if m == 3:
                    used(("col", c), "s")

            def col_chunk(c):
                for m in range(4):
                    col_group(c, m)

            for kind, n in STAGE1:
                {"ada": ada_chunk, "row": row_chunk, "col": col_chunk}[kind](n)
            barrier(pe, "pe")
            if stages < 2:
                return
            for name, c in (("gi", ZI), ("gf", ZF)):
                b = fill(pe, "v", name)
                for i, (o, n) in enumerate(TILES):
                    last = tr(b[0:4, o:o + n], ze(i, n, c, 4))
                filled("v", last)
            pe.wait_ge(sem("state_small"), 16 * 3)
            b = fill(pe, "v", "n0T")
            filled("v", tr(b[:, 0:32], n0r[0:32, :]))
            pe.wait_ge(sem("gate_exps"), 4)
            pe.wait_ge(sem("gate_logs"), 1)
            b = fill(pe, "v", "gcols")
            for i, (o, n) in enumerate(TILES):
                tr(b[0:n, i * 4:i * 4 + 4], ga_[0:4, o:o + n])
                tr(b[0:n, 12 + i * 4:16 + i * 4], gnd[0:4, o:o + n])
            tr(b[0:32, 24:28], gws[0:4, :])
            tr(b[0:32, 28:32], gwi[0:4, :])
            filled("v", tr(b[0:8, 32:36], gwc[0:4, :]))
            b = fill(pe, "v", "wcb")
            for h in range(MH):
                last = mm(b[:, h * 8:h * 8 + 8], K("head_row", 4, h * P, (h + 1) * P), gwc[0:4, :], True, True)
            filled("v", last)
            for h in range(MH):
                q_, k_ = mq[:, h, :], mq[:, 4 + h, :]
                b = fill(pe, "v", ("krow", h))
                for i, (o, n) in enumerate(TILES):
                    last = tr(b[0:n, o:o + P], k_[:, o:o + n])
                filled("v", last)
                b = fill(pe, "v", ("M", h))
                filled("v", mm(b[:, 0:NTOK], K("head_row", 4, h * P, (h + 1) * P), gM[0:4, :], True, True))
                b = fill(pe, "v", ("S", h))
                mm(b[:, 0:256], k_[:, 0:128], q_[:, 0:256], True, True)
                mm(b[:, 256:384], k_[:, 128:256], q_[:, 128:256], True, True)
                filled("v", mm(b[0:32, 384:416], k_[:, 256:288], q_[:, 256:288], True, True))
                pe.wait_ge(sem(f"state_C_{h % 2}"), 16 * (h // 2 + 1))
                for half in range(2):
                    b = fill(pe, "s", ("CT", h, half))
                    for j in range(4):
                        bb = half * 4 + j
                        last = tr(b[:, j * P:(j + 1) * P], C0h[:, h % 2, bb * P:(bb + 1) * P])
                    filled("s", last)
                after(pe, "v", ("S", h))
                b = fill(pe, "v", ("num", h))
                S_ = STt[:, h % 2, :]
                one = K("one")
                v_ = [ze(i, n, ZV + h * MD, MD) for i, (o, n) in enumerate(TILES)]
                mm(b[:, 0:128], S_[:, 0:128], v_[0], True, True)
                mm(b[:, 128:129], S_[:, 0:128], one, True, True)
                mm(b[:, 129:257], S_[:, 128:256], v_[0], True, False)
                mm(b[:, 129:257], S_[:, 256:384], v_[1], False, True)
                mm(b[:, 257:258], S_[:, 128:256], one, True, False)
                mm(b[:, 257:258], S_[:, 256:384], one, False, True)
                mm(b[0:32, 258:386], S_[0:32, 384:416], v_[2], True, True)
                filled("v", mm(b[0:32, 386:387], S_[0:32, 384:416], one[0:32, :], True, True))
                after(pe, "s", ("CT", h, 1))
                b = fill(pe, "v", ("numI", h))
                for bb in range(DB):
                    mm(b[:, bb * 4:bb * 4 + 4], CTh[:, h % 2, bb * P:(bb + 1) * P], q_[:, 256 + 4 * bb:260 + 4 * bb], True, True)
                filled("v", mm(b[0:32, 64:72], q_[:, 256:288], n0T[:, h:32:4], True, True))
                pe.wait_ge(sem("inter_rows"), h + 1)
                b = fill(pe, "v", ("numIT", h))
                filled("v", tr(b[0:32, 0:128], numI[:, h % 2, :]))
                pe.wait_ge(sem("state_ops"), h + 1)
                kr = krow[:, h % 2, :]
                b = fill(pe, "v", ("Cp", h))
                mm(b[:, 0:128], vw[:, h % 2, 0:128], kr[:, 0:128], True, False)
                mm(b[:, 0:128], vw[:, h % 2, 128:256], kr[:, 128:256], False, True)
                mm(b[0:1, 128:256], WT[:, h % 2, 255:256], kr[:, 0:128], True, False)
                filled("v", mm(b[0:1, 128:256], WT[:, h % 2, 383:384], kr[:, 128:256], False, True))
                for half in range(2):
                    b = fill(pe, "v", ("Cs", h, half))
                    for j in range(4):
                        bb = half * 4 + j
                        last = mm(b[:, j * P:(j + 1) * P], vwb[0:32, h % 2, bb * P:(bb + 1) * P], kr[0:32, 256:384], True, True)
                    filled("v", last)
                b = fill(pe, "v", ("ns", h))
                filled("v", mm(b[0:8, 0:128], wsb[0:32, h % 2, :], kr[0:32, 256:384], True, True))
                pe.wait_ge(sem("head_rows"), h + 1)
                b = fill(pe, "s", ("hmT", h))
                for i, (o, n) in enumerate(TILES):
                    last = tr(b[:, o:o + n], hrw[0:n, h % 2, o:o + P])
                filled("s", last)
            barrier(pe, "pe")
            if stages < 3:
                return
            b = fill(pe, "v", "pe")
            for kind in range(2):
                for u in range(8):
                    c = 29 + kind * 16 + u
                    last = mm(b[:, kind * 2:kind * 2 + 2], w2[:, kind, u, :], colT[:, c:c + 9:8], u == 0, u == 7)
            filled("v", last)
            groups = iter(GATE_GROUPS)

            def gate_groups(count):
                for _ in range(count):
                    col_group(*next(groups))

            for i, (o, n) in enumerate(TILES):
                gate_groups(2)
                pe.wait_ge(sem("q_rows"), i + 1)
                for name, src in (("q", qn), ("qr", qr)):
                    b = fill(pe, "s", (name, i))
                    for j in range(4):
                        last = tr(b[:, j * n:(j + 1) * n], src[0:n, i % 2, j * P:(j + 1) * P])
                    filled("s", last)
                gate_groups(1)
                pe.wait_ge(sem("kv_rows"), i + 1)
                b = fill(pe, "s", ("k", i))
                tr(b[:, 0:n], kvrows(i, n, 2))
                filled("s", tr(b[:, n:2 * n], kvrows(i, n, 4)))
            b = fill(pe, "v", "pages")
            pe.wait_ge(sem("page_rows"), 1)
            filled("v", mm(b[:, 0:64], K("ones", 1), pgf[0:1, :], True, True))
            gate_groups(3)
            pe.wait_ge(sem("pair_rows"), 16)
            b = fill(pe, "s", "cTp")
            for kp in range(4):
                c = (kp % 2) * 512 + (kp // 2) * P
                last = tr(b[:, kp * P:(kp + 1) * P], pair[:, c:c + P])
            filled("s", last)
            gate_groups(1)
            after(pe, "s", "cTp")
            b = fill(pe, "v", "cmp_p")
            for kg_ in range(4):
                for u in range(8):
                    last = mm(b[:, kg_ * 16:kg_ * 16 + 16], w2[:, kg_ // 2, u, :], cTp[:, kg_, u:P:8], u == 0, u == 7)
            filled("v", last)
            gate_groups(1)
            pe.wait_ge(sem("kc_squared"), 1)
            b = fill(pe, "v", "kc_mean")
            filled("v", mm(b[:, 0:NC_P], K("half_mean"), tmpT[:, 0:NC_P], True, True))
            b = fill(pe, "v", "vc_rows")
            filled("v", tr(b[0:NC_P, 0:P], vcT[:, 0:NC_P]))
            gate_groups(1)
            pe.wait_ge(sem("kc_ready"), 1)
            for i in range(2):
                for g in range(2):
                    b = fill(pe, "v", ("cs", i, g))
                    gp = slice(g * DH, (g + 1) * DH)
                    for j in range(HPG):
                        last = mm(b[:, j * 16:j * 16 + NC_P], qT[gp, j, i * P:(i + 1) * P], kcT[gp, 0:NC_P], True, True)
                    filled("v", last)
            for i in range(2):
                gate_groups(1)
                pe.wait_ge(sem("cmp_probs"), i + 1)
                for half in range(2):
                    b = fill(pe, "s", ("pc", i, half))
                    for j in range(4):
                        h = half * 4 + j
                        last = tr(b[0:NC_P, j * P:(j + 1) * P], sc_c[:, i, h * 16:h * 16 + NC_P])
                    filled("s", last)
                after(pe, "s", ("pc", i, 1))
                b = fill(pe, "v", ("oc", i))
                for h in range(AH):
                    g = h // HPG
                    last = mm(b[:, h * DH:(h + 1) * DH], ptc[0:NC_P, h, :], vcr[0:NC_P, 0, g * DH:(g + 1) * DH], True, True)
                filled("v", last)

            def scores(u):
                br, i, g, jp = UNITS[u]
                keys = (kselT, kwinT)[br]
                nk = (i + 1) * P
                b = fill(pe, "v", ("sc", u))
                gp = slice(g * DH, (g + 1) * DH)
                for hh in range(2):
                    last = mm(b[:, hh * nk:(hh + 1) * nk], qrT[gp, 2 * jp + hh, i * P:(i + 1) * P], keys[gp, 0:nk], True, True)
                filled("v", last)

            gate_groups(3)
            assert next(groups, None) is None
            scores(0)
            for u, (br, i, g, jp) in enumerate(UNITS):
                if u + 1 < len(UNITS):
                    scores(u + 1)
                nt = i + 1
                pe.wait_ge(sem("probs"), 2 * (u + 1))
                b = fill(pe, "s", ("pt", u))
                for m in range(2 * nt):
                    last = tr(b[:, m * P:(m + 1) * P], Pu[:, u % 2, m * P:(m + 1) * P])
                filled("s", last)
                after(pe, "s", ("pt", u))
                b = fill(pe, "v", ("pv", u))
                for hh in range(2):
                    for t in range(nt):
                        m = hh * nt + t
                        last = mm(b[:, hh * DH:(hh + 1) * DH], PTu[:, u % 2, m * P:(m + 1) * P], kvrows(t, P, 3 + 2 * br, g), t == 0, t == nt - 1)
                filled("v", last)
            pe.wait_ge(sem("prompt_out"), 1)
            for i in range(2):
                b = fill(pe, "s", ("oT", i))
                for t in range(4):
                    last = tr(b[:, t * P:(t + 1) * P], ob[:, i, t * P:(t + 1) * P])
                filled("s", last)
            barrier(pe, "pe")
            if stages < 4:
                return
            def rows_of(r):
                return [pts[r % 2][:, m, :].rearrange("p (r c) -> p r c", r=2) for m in range(8)]

            def front(r):
                tv, wn = rows_of(r), wns[r % 2]
                pe.wait_ge(sem(f"cache_rows_{r % 2}"), 16 * 8 * (r // 2 + 1))
                for kind in range(2):
                    for m2 in range(4):
                        ring = "vs"[m2 % 2]
                        b = fill(pe, ring, ("cT", r, kind, m2))
                        for q in range(4):
                            m, par = 2 * m2 + q % 2, q // 2
                            last = tr(b[:, q * P:(q + 1) * P], tv[m][:, par, kind * P:(kind + 1) * P])
                        filled(ring, last)
                    after(pe, "v", ("cT", r, kind, 2))
                    after(pe, "s", ("cT", r, kind, 3))
                    b = fill(pe, "v", ("cmp_s", r, kind))
                    for g in range(2):
                        for u in range(8):
                            last = mm(b[:, g * P:(g + 1) * P], w2[:, kind, u, :], cT[:, g, u:1024:8], u == 0, u == 7)
                    filled("v", last)
                for q4 in range(4):
                    b = fill(pe, "s", ("ks", r, q4))
                    for q in range(4):
                        m, par = (4 * q4 + q) // 2, q % 2
                        last = tr(b[:, q * P:(q + 1) * P], tv[m][:, par, 2 * P:3 * P])
                    filled("s", last)
                pe.wait_ge(sem(f"win_rows_{r % 2}"), 32 * (r // 2 + 1))
                for q2 in range(2):
                    b = fill(pe, "s", ("kw", r, q2))
                    for q in range(4):
                        last = tr(b[:, q * P:(q + 1) * P], wn[:, q2, q, 0:P])
                    filled("s", last)
                pe.wait_ge(sem("kc_squared"), 2 + r)
                b = fill(pe, "v", ("kc_mean", r))
                filled("v", mm(b[:, 0:P], K("half_mean"), t2[:, :], True, True))
                b = fill(pe, "v", ("vc_rows", r))
                for b2 in range(2):
                    last = tr(b[0:NC_S, b2 * P:(b2 + 1) * P], vc2[:, b2, 0:NC_S])
                filled("v", last)

            def four(tag, width, lhs, rhs):
                b = fill(pe, "v", tag)
                for c in range(4):
                    b2, g = c // 2, c % 2
                    gp = slice(g * DH, (g + 1) * DH)
                    last = mm(b[32 * c:32 * c + 32, 0:width], lhs(gp, b2), rhs(gp, b2), True, True)
                filled("v", last)

            def scored(r):
                wn = wns[r % 2]
                pe.wait_ge(sem("kc_ready"), 2 + r)
                four(("sc_c", r), NC_S, lambda gp, b2: qTr[gp, b2, :], lambda gp, b2: kc2[gp, b2, 0:NC_S])
                after(pe, "s", ("ks", r, 3))
                for half in range(2):
                    four(("sc_s", r, half), 512, lambda gp, b2: qrTr[gp, b2, :],
                         lambda gp, b2: ksT[gp, b2, half * 512:(half + 1) * 512])
                four(("sc_n", r), 32, lambda gp, b2: qrTr[gp, b2, :], lambda gp, b2: kselT[gp, 256:288])
                after(pe, "s", ("kw", r, 1))
                four(("sc_w", r), 512, lambda gp, b2: qrTr[gp, b2, :], lambda gp, b2: kwT[gp, b2, :])
                four(("sc_v", r), 32, lambda gp, b2: qrTr[gp, b2, :], lambda gp, b2: kwinT[gp, 256:288])
                pe.wait_ge(sem("cmp_norm"), r + 1)
                b = fill(pe, "v", ("imp", r))
                filled("v", mm(b[:, 0:NC_S], K("head_sum"), pnrm[:, 0:NC_S], True, True))
                b = fill(pe, "s", ("PTc", r))
                filled("s", tr(b[0:NC_S, 0:P], pnrm[:, 0:NC_S]))
                after(pe, "s", ("PTc", r))
                b = fill(pe, "v", ("o_c", r))
                for c in range(4):
                    b2, g = c // 2, c % 2
                    last = mm(b[32 * c:32 * c + 32, 0:DH], PTc[0:NC_S, 32 * c:32 * c + 32], vcr2[0:NC_S, b2, g * DH:(g + 1) * DH], True, True)
                filled("v", last)
                pe.wait_ge(sem("win_probs"), r + 1)
                b = fill(pe, "s", ("PTw", r))
                for t in range(4):
                    last = tr(b[:, t * P:(t + 1) * P], Sw[:, t * P:(t + 1) * P])
                filled("s", last)
                b = fill(pe, "s", ("PTv", r))
                filled("s", tr(b[0:32, 0:P], Sw[:, 512:544]))
                after(pe, "s", ("PTv", r))
                b = fill(pe, "v", ("o_w", r))
                for c in range(4):
                    b2, g = c // 2, c % 2
                    o_ = b[32 * c:32 * c + 32, 0:DH]
                    for t in range(4):
                        mm(o_, PTw[:, t, 32 * c:32 * c + 32], wn[:, b2, t, P + g * DH:P + (g + 1) * DH], t == 0, False)
                    last = mm(o_, PTw[0:32, 4, 32 * c:32 * c + 32], kvrows(2, 32, 5, g), False, True)
                filled("v", last)

            def selected(r):
                tv = rows_of(r)
                pe.wait_ge(sem("sel_probs"), r + 1)
                for half in range(2):
                    b = fill(pe, "s", ("PTs", r, half))
                    for t in range(4):
                        last = tr(b[:, t * P:(t + 1) * P], Ss[:, (half * 4 + t) * P:(half * 4 + t + 1) * P])
                    filled("s", last)
                b = fill(pe, "s", ("PTn", r))
                filled("s", tr(b[0:32, 0:P], Ss[:, 1024:1056]))
                after(pe, "s", ("PTn", r))
                b = fill(pe, "v", ("o_s", r))
                for c in range(4):
                    b2, g = c // 2, c % 2
                    o_ = b[32 * c:32 * c + 32, 0:DH]
                    for t in range(8):
                        v_ = tv[4 * b2 + t // 2][:, t % 2, 3 * P + g * DH:3 * P + (g + 1) * DH]
                        mm(o_, PTs[:, t, 32 * c:32 * c + 32], v_, t == 0, False)
                    last = mm(o_, PTs[0:32, 8, 32 * c:32 * c + 32], kvrows(2, 32, 3, g), False, True)
                filled("v", last)
                pe.wait_ge(sem("round_out"), r + 1)
                b = fill(pe, "v", ("oTr", r))
                filled("v", tr(b[0:DH, 0:P], orow[:, :]))

            rounds(front, scored, selected)
            barrier(pe, "pe")
            if stages < 5:
                return
            pe_late(pe, mm, tr, col_chunk, used)


        def store_state(pool, dma, h):
            pool.wait_ge(sem("new_state"), h + 1)
            dma(C_prompt[0][0, h], Cpr[:, h % 2, :], f"state_stored_{h % 2}")
            dma(C_sample[0][:, h].rearrange("b v k -> v b k"), Cn[:, h % 2, :].rearrange("p (b k) -> p b k", b=DB), f"state_stored_{h % 2}")

        @block.vector
        def _(ve):
            v = Steps(ve, "vector_step", sem)

            def copy(out, in_, name=None):
                v(ve.tensor_copy(out, in_), name)

            def tt(out, p, q, op, name=None):
                v(ve.tensor_tensor(out, p, q, op), name)

            def ts(out, p, s1, op0, s2=None, op1=None, name=None):
                if op1 is None:
                    v(ve.tensor_scalar(out, p, s1, None, op0), name)
                else:
                    v(ve.tensor_scalar(out, p, s1, s2, op0, op1), name)

            def stt(out, p, s1, q, op0, op1, name=None):
                v(ve.scalar_tensor_tensor(out=out, in0=p, scalar=s1, in1=q, op0=op0, op1=op1), name)

            def red(out, p, op, name=None, negate=None):
                v(ve.tensor_reduce(out, p, AX.X, op, negate=negate), name)

            def recip(out, p, name=None):
                v(ve.reciprocal(out, p), name)

            def got(tag):
                return drain(ve, "v", tag)

            VD, add, mul, sub, mx, mn = "v_drained", ALU.add, ALU.mult, ALU.subtract, ALU.max, ALU.min

            ve.wait_ge(sem("first_loads"), 16 * L1_FIRST)
            ve.wait_ge(sem("c_sigmoid"), 1)
            tt(crow[0:9, :], crow[0:9, :], ctmp[0:9, :], mul, "c_silu")
            b = got("cT")
            copy(csil.rearrange("p a b -> p (a b)"), b[:, 0:72], VD)
            ve.wait_ge(sem("small_loads"), 16 * L1_SMALL)

            def ada_chunk(n):
                b = got(("ada", n))
                for j in range(4):
                    cs = slice(n * 512 + j * P, n * 512 + (j + 1) * P)
                    tt(mod[0:9, cs], b[32 * j:32 * j + 9, 0:P], mod[0:9, cs], add, VD if j == 3 else None)

            def row_chunk(c):
                _, w_, zc = ROW_CHUNKS[c]
                for i, (o, n) in enumerate(TILES):
                    b = got(("row", c, i))
                    if i < 2:
                        tt(zr[0:n, i, zc:zc + w_], b[0:n, 0:w_], rowbias[0:n, zc:zc + w_], add, VD)
                        continue
                    parts = quarters(w_)
                    for j, (c0, cw) in enumerate(parts):
                        tt(zr[0:n, i, zc + c0:zc + c0 + cw], b[32 * j:32 * j + n, 0:cw], rowbias[0:n, zc + c0:zc + c0 + cw], add,
                           VD if j == len(parts) - 1 else None)

            for n in range(4):
                ada_chunk(n)
            stt(mod[0:9, D:2 * D], mod[0:9, D:2 * D], 1.0, gmix[0:9, :], add, mul, "mod_ready")
            for i, (o, n) in enumerate(TILES):
                ve.wait_ge(sem("rms"), i + 1)
                recip(rstd[0:n, i:i + 1], ssum[0:n, i:i + 1])
                if i == 2:
                    after(ve, "s", ("hT", 0, 1))
                for half in range(2):
                    hs = slice(half * 512, (half + 1) * 512)
                    b = got(("scale", i, half))
                    stt(hrow[0:n, i % 2, hs], x[0:n, i, hs], rstd[0:n, i:i + 1], b[0:n, :], mul, mul, VD)
                    b = got(("shift", i, half))
                    tt(hrow[0:n, i % 2, hs], hrow[0:n, i % 2, hs], b[0:n, :], add, VD)
                    v(ve.nop(), "h_rows")
            for kind, n in STAGE1:
                if kind != "col":
                    {"ada": ada_chunk, "row": row_chunk}[kind](n)
            stt(mod[0:9, 4 * D:5 * D], mod[0:9, 4 * D:5 * D], 1.0, gffn[0:9, :], add, mul, "mod_ready")
            barrier(ve, "ve")
            if stages < 2:
                return
            v(ve.memset(gtmp[0:4, :], 0.0))
            b = got("gi")
            copy(gi[0:4, :], b[0:4, 0:NTOK], VD)
            b = got("gf")
            copy(gf[0:4, :], b[0:4, 0:NTOK], VD)
            stt(gml[0:4, :], gf[0:4, :], -1.0, gf[0:4, :], mul, mn, "forget_abs")
            ve.wait_ge(sem("state_small"), 16 * 3)
            b = got("n0T")
            copy(n0T, b[:, 0:32], VD)
            ve.wait_ge(sem("forget_log"), 2)
            stt(gf[0:4, :], gf[0:4, :], 0.0, gml[0:4, :], mn, sub)
            v(ve.tensor_tensor_scan(gb[0:4, 0:256], gf[0:4, 0:256], gtmp[0:4, 0:256], 0.0, add, add))

            def smp(t_):
                return t_[0:4, 256:288].rearrange("p (b t) -> p b t", t=DT)

            copy(smp(gb)[:, :, 0:1], smp(gf)[:, :, 0:1])
            for t in range(1, DT):
                tt(smp(gb)[:, :, t:t + 1], smp(gb)[:, :, t - 1:t], smp(gf)[:, :, t:t + 1], add)
            tt(ga_[0:4, :], gi[0:4, :], gb[0:4, :], sub)
            v(ve.tensor_tensor_scan(gM[0:4, 0:256], ga_[0:4, 0:256], gtmp[0:4, 0:256], 0.0, mx, add))
            m0b = m0T[0:4, :].unsqueeze(2)
            tt(smp(gM)[:, :, 0:1], smp(ga_)[:, :, 0:1], m0b, mx)
            for t in range(1, DT):
                tt(smp(gM)[:, :, t:t + 1], smp(gM)[:, :, t - 1:t], smp(ga_)[:, :, t:t + 1], mx)
            ML = smp(gM)[:, :, DT - 1:DT]
            tt(gnd[0:4, :], gb[0:4, :], gM[0:4, :], add)
            copy(mfin[0:4, 0:1], gnd[0:4, 255:256])
            copy(mfin[0:4, 1:9].unsqueeze(2), smp(gnd)[:, :, DT - 1:DT], "m_final")
            r4 = lambda t_: t_[0:4, :].rearrange("p (b t) -> p b t", t=DT)
            tt(r4(gws), smp(ga_), ML.to_broadcast([4, DB, DT]), sub)
            tt(r4(gwi), m0b.to_broadcast([4, DB, DT]), smp(gM), sub)
            tt(gwc[0:4, :].unsqueeze(2), m0b, ML, sub, "gate_logs")
            b = got("gcols")
            for i, (o, n) in enumerate(TILES):
                copy(aT[0:n, i, :], b[0:n, i * 4:i * 4 + 4])
                copy(ndT[0:n, i, :], b[0:n, 12 + i * 4:16 + i * 4])
            copy(wsT[0:32, :], b[0:32, 24:28])
            copy(wiT[0:32, :], b[0:32, 28:32])
            copy(wcT[0:8, :], b[0:8, 32:36], VD)
            b = got("wcb")
            copy(wcb, b[:, 0:32], VD)
            for h in range(MH):
                hb = h % 2
                b = got(("krow", h))
                copy(krow[0:32, hb, 256:384], b[0:32, 256:384])
                copy(krow[:, hb, 0:256], b[:, 0:256], VD)
                b = got(("M", h))
                tt(DTt[:, hb, 0:256], C[:, CC["causal_t"][0]:CC["zeros_t"][1]], b[:, 0:256], sub)
                tt(DTt[:, hb, 256:384], K("causal_t"), b[:, 128:256], sub)
                tt(DTt[0:32, hb, 384:416], K("sample_t", 32), b[0:32, 256:288], sub, VD)
                ve.wait_ge(sem("decays"), 3 * (h + 1))
                b = got(("S", h))
                tt(STt[0:32, hb, 384:416], b[0:32, 384:416], WT[0:32, hb, 384:416], mul)
                tt(STt[:, hb, 0:384], b[:, 0:384], WT[:, hb, 0:384], mul, VD)
                b = got(("num", h))
                for i, (nc_, dc, n) in enumerate(((0, 128, P), (129, 257, P), (258, 386, 32))):
                    if i == 2:
                        copy(hrw[0:32, hb, 256:384], b[0:32, 258:386])
                        copy(den[0:32, hb, 3:4], b[0:32, 386:387], VD)
                    else:
                        d_ = den[0:n, hb, i:i + 1]
                        copy(d_, b[0:n, dc:dc + 1])
                        stt(d_, d_, -1.0, d_, mul, mx)
                        tt(d_, d_, ndT[0:n, i, h:h + 1], mx)
                        recip(d_, d_)
                        ts(hrw[0:n, hb, i * P:(i + 1) * P], b[0:n, nc_:nc_ + P], d_, mul)
                b = got(("numI", h))
                tt(vwb[0:32, hb, 0:8], b[0:32, 64:72], K("batch_of", 32), mul)
                copy(numI[:, hb, :], b[:, 0:32], VD)
                v(ve.nop(), "inter_rows")
                red(nqT[0:32, h:h + 1], vwb[0:32, hb, 0:8], add)
                b = got(("numIT", h))
                hs = hrw[0:32, hb, 256:384]
                stt(hs, b[0:32, 0:128], wiT[0:32, h:h + 1], hs, mul, add, VD)
                d_ = den[0:32, hb, 2:3]
                stt(d_, nqT[0:32, h:h + 1], wiT[0:32, h:h + 1], den[0:32, hb, 3:4], mul, add)
                stt(d_, d_, -1.0, d_, mul, mx)
                tt(d_, d_, ndT[0:32, 2, h:h + 1], mx)
                recip(d_, d_)
                ts(hs, hs, d_, mul)
                v(ve.nop(), "head_rows")
                for i, c in ((0, 255), (1, 383)):
                    ts(vw[:, hb, i * P:(i + 1) * P], ze(i, P, ZV + h * MD, MD), WT[:, hb, c:c + 1], mul)
                ts(wsb[0:32, hb, :], K("batch_of", 32), wsT[0:32, h:h + 1], mul)
                tt(vwb[0:32, hb, :].rearrange("p (b k) -> p b k", b=DB),
                   ze(2, 32, ZV + h * MD, MD).unsqueeze(1).to_broadcast([32, DB, MD]),
                   wsb[0:32, hb, :].unsqueeze(2).to_broadcast([32, DB, MD]), mul, "state_ops")
                b = got(("Cp", h))
                if h >= 2:
                    ve.wait_ge(sem(f"state_stored_{hb}"), 32 * (h // 2))
                copy(npr[0:1, h, :], b[0:1, 128:256])
                copy(Cpr[:, hb, :], b[:, 0:128], VD)
                ve.wait_ge(sem(f"state_C_{hb}"), 16 * (h // 2 + 1))
                for half in range(2):
                    b = got(("Cs", h, half))
                    for j in range(4):
                        bb = half * 4 + j
                        stt(Cn[:, hb, bb * P:(bb + 1) * P], C0h[:, hb, bb * P:(bb + 1) * P], wcb[:, h * 8 + bb:h * 8 + bb + 1],
                            b[:, j * P:(j + 1) * P], mul, add, VD if j == 3 else None)
                b = got(("ns", h))
                stt(nsr[0:8, h, :], n0s[0:8, h, :], wcT[0:8, h:h + 1], b[0:8, 0:128], mul, add, VD)
                v(ve.nop(), "new_state")
            barrier(ve, "ve")
            if stages < 3:
                return
            b = got("pe")
            copy(y2c[0:64, 0, 0:2], b[64:128, 1:4:2])
            tt(pebc[0:64, :], b[0:64, 0:4:2], y2c[0:64, 0, 0:2], add)
            copy(pebc[64:128, :], pebc[0:64, :], VD)
            ve.wait_ge(sem("page_table_loaded"), 16)
            copy(pgf[0:1, :], pgi[0:1, :], "page_rows")
            v(ve.memset(grd.rearrange("p a b -> p (a b)"), 0.0), "gates_cleared")
            ve.wait_ge(sem("norm_rows"), 16 * 4)
            qgb = qg.unsqueeze(1).unsqueeze(1)
            for i, (o, n) in enumerate(TILES):
                ib = i % 2
                if i == 2:
                    after(ve, "s", ("k", 0))

                def norm(src, heads, out, gain, out_is_pairs):
                    s3 = src.rearrange("p (h d) -> p h d", d=DH)
                    w = sq[0:n, 0:heads * DH]
                    w3 = w.rearrange("p (h d) -> p h d", d=DH)
                    tt(w, src, src, mul)
                    red(rs8[0:n, 0:heads], w3, add, "norm_sum")
                    ve.wait_ge(sem("norm_root"), v.count["norm_sum"])
                    recip(rs8[0:n, 0:heads], rs8[0:n, 0:heads])
                    tt(w3, s3, rs8[0:n, 0:heads].unsqueeze(2).to_broadcast([n, heads, DH]), mul)
                    if out_is_pairs:
                        for g in range(2):
                            tt(out.rearrange("p (j g d) -> p g j d", g=2, d=DH)[:, g],
                               w.rearrange("p (g j d) -> p g j d", g=2, d=DH)[:, g],
                               gain[0:n].unsqueeze(1).to_broadcast([n, HPG, DH]), mul)
                    else:
                        tt(s3, w3, gain[0:n].unsqueeze(1).to_broadcast([n, heads, DH]), mul)

                def rope(view, heads, name=None):
                    s3 = view.rearrange("p (h d) -> p h d", d=DH)
                    x1, x2 = s3[:, :, 0:8], s3[:, :, 8:16]
                    co = K("cos", n, i * 8, i * 8 + 8).unsqueeze(1).to_broadcast([n, heads, 8])
                    si = K("sin", n, i * 8, i * 8 + 8).unsqueeze(1).to_broadcast([n, heads, 8])
                    r = [rt[0:n, m, 0:heads * 8].rearrange("p (h d) -> p h d", d=8) for m in range(4)]
                    tt(r[0], x1, co, mul)
                    tt(r[1], x2, si, mul)
                    tt(r[2], x1, si, mul)
                    tt(r[3], x2, co, mul)
                    tt(x1, r[0], r[1], sub)
                    tt(x2, r[2], r[3], add, name)

                norm(ze(i, n, ZQ, 512), 8, qn[0:n, ib, :], qg, True)
                copy(qr[0:n, ib, :], qn[0:n, ib, :])
                rope(qr[0:n, ib, :], 8, "q_rows")
                norm(kvrows(i, n, 2), 2, None, kg[:, 1, :], False)
                rope(kvrows(i, n, 2), 2)
                norm(kvrows(i, n, 4), 2, None, kg[:, 2, :], False)
                rope(kvrows(i, n, 4), 2, "kv_rows")
            b = got("pages")
            b3 = b[:, 0:64].rearrange("p (i h) -> p i h", h=2)
            i3 = idx_f.rearrange("p (a i) -> p a i", a=2)
            ts(i3[:, 0, :], b3[:, :, 0], K("first_page"), mul)
            ts(i3[:, 1, :], b3[:, :, 1], K("second_page"), mul, name=VD)
            tt(idx_t[:, 0:32], i3[:, 0, :], i3[:, 1, :], add)
            ts(idx_t[:, 0:32], idx_t[:, 0:32], float(PAGE // 2), mul, K("pair_in_page"), add)
            copy(idx_u, idx_t[:, 0:32], "cache_index")
            b = got("cmp_p")
            for g in range(2):
                for kind, dst in ((0, kcT), (1, vcT)):
                    c = (kind * 2 + g) * 16
                    copy(y2c[0:64, kind, 0:16], b[64:128, c:c + 16])
                    tt(dst[g * DH:(g + 1) * DH, 0:NC_P], b[0:64, c:c + NC_P], y2c[0:64, kind, 1:16], add,
                       VD if (g, kind) == (1, 1) else None)
            ts(vcT[:, 0:NC_P], vcT[:, 0:NC_P], pebc[:, 1:2], add)
            ts(kcT[:, 0:NC_P], kcT[:, 0:NC_P], pebc[:, 0:1], add)
            tt(tmpT[:, 0:NC_P], kcT[:, 0:NC_P], kcT[:, 0:NC_P], mul, "kc_squared")
            b = got("kc_mean")
            ts(tmpT[:, 0:NC_P], b[:, 0:NC_P], EPS, add, name=VD)
            v(ve.nop(), "kc_var")
            b = got("vc_rows")
            copy(vcr[0:NC_P, 0, :], b[0:NC_P, 0:P], VD)
            ve.wait_ge(sem("kc_root"), 1)
            recip(tmpT[:, 0:NC_P], tmpT[:, 0:NC_P])
            stt(kcT[:, 0:NC_P], kcT[:, 0:NC_P], colT[:, 28:29], tmpT[:, 0:NC_P], mul, mul, "kc_ready")
            ve.wait_ge(sem("branch_gates_ready"), 3)
            st8 = lambda m: stat[:, m, 0:8]
            for i in range(2):
                s3 = sc_c[:, i, :].rearrange("p (h n) -> p h n", n=16)[:, :, 0:NC_P]
                for g in range(2):
                    b = got(("cs", i, g))
                    tt(s3[:, 4 * g:4 * g + 4], b[:, 0:64].rearrange("p (h n) -> p h n", n=16)[:, :, 0:NC_P],
                       K("cmp_mask", P, i * NC_P, (i + 1) * NC_P).unsqueeze(1).to_broadcast([P, HPG, NC_P]), add, VD)
                red(st8(i), s3, mx)
                tt(s3, s3, st8(i).unsqueeze(2).to_broadcast([P, AH, NC_P]), sub, "cmp_shifted")
            for i in range(2):
                ve.wait_ge(sem("cmp_probs"), i + 1)
                s3 = sc_c[:, i, :].rearrange("p (h n) -> p h n", n=16)[:, :, 0:NC_P]
                red(st8(2 + i), s3, add)
                recip(st8(2 + i), st8(2 + i))
                stt(st8(2 + i), st8(2 + i), K("cmp_valid", P, i, i + 1), gt24[:, i, 0:24:3], mul, mul)
            for i in range(2):
                b = got(("oc", i))
                tt(ob[:, i, :].rearrange("p (h d) -> p h d", d=DH), b[:, :].rearrange("p (h d) -> p h d", d=DH),
                   st8(2 + i).unsqueeze(2).to_broadcast([P, AH, DH]), mul, VD)

            def masked(u):
                br, i, g, jp = UNITS[u]
                nk, ub = (i + 1) * P, u % 2
                b = got(("sc", u))
                m0 = CC["causal"][1] - nk
                s3 = Su[:, ub, 0:2 * nk].rearrange("p (h n) -> p h n", h=2)
                tt(s3, b[:, 0:2 * nk].rearrange("p (h n) -> p h n", h=2),
                   C[:, m0:m0 + nk].unsqueeze(1).to_broadcast([P, 2, nk]), add, VD)
                st = stat[:, ub, 8:10]
                red(st, s3, mx)
                ts(st, st, -SCALE, mul, name="score_max")

            masked(0)
            for u, (br, i, g, jp) in enumerate(UNITS):
                if u + 1 < len(UNITS):
                    masked(u + 1)
                b = got(("pv", u))
                sm = stat[:, u % 2, 12:14]
                recip(sm, sm)
                for hh in range(2):
                    h = g * HPG + 2 * jp + hh
                    tt(sm[:, hh:hh + 1], sm[:, hh:hh + 1], gt24[:, i, 3 * h + 1 + br:3 * h + 2 + br], mul)
                    o_ = ob[:, i, h * DH:(h + 1) * DH]
                    stt(o_, b[:, hh * DH:(hh + 1) * DH], sm[:, hh:hh + 1], o_, mul, add, VD if hh else None)
            v(ve.nop(), "prompt_out")
            ve.wait_ge(sem("output_gate"), 1)
            tt(hmT, hmT, moT, mul, "gated")
            barrier(ve, "ve")
            if stages < 4:
                return
            v(ve.memset(kc2.rearrange("p a b -> p (a b)"), 0.0))
            v(ve.memset(vc2.rearrange("p a b -> p (a b)"), 0.0))
            v(ve.memset(qTr.rearrange("p a b -> p (a b)"), 0.0))
            v(ve.memset(qrTr.rearrange("p a b -> p (a b)"), 0.0))
            v(ve.memset(imp[:, :], 0.0))
            m_, s_, x_ = (lambda k: st4[:, k:k + 1]), (lambda k: st4[:, 4 + k:5 + k]), (lambda k: st4[:, 8 + k:9 + k])
            ve.wait_ge(sem("round_gates"), 16 * 16)

            def front(r):
                for kind, dst in ((0, kc2), (1, vc2)):
                    for m2 in (0, 2):
                        b = got(("cT", r, kind, m2))
                        for g in range(2):
                            for par in range(2):
                                copy(cT[par * DH:(par + 1) * DH, g, m2 * 256:(m2 + 1) * 256],
                                     b[g * DH:(g + 1) * DH, par * 256:(par + 1) * 256], VD if (g, par) == (1, 1) else None)
                    b = got(("cmp_s", r, kind))
                    if kind == 0:
                        for b2 in range(2):
                            c0 = 256 + (2 * r + b2) * 4
                            for src, dq in ((qT, qTr), (qrT, qrTr)):
                                copy(dq[:, b2, 0:16].rearrange("p (j t) -> p j t", t=4), src[:, :, c0:c0 + 4])
                    for g in range(2):
                        gb_ = slice(g * P, (g + 1) * P)
                        copy(y22[0:64, :], b[64:128, gb_])
                        tt(dst[g * DH:(g + 1) * DH, :, 0:NC_S], b[0:64, gb_].rearrange("p (b n) -> p b n", b=2)[:, :, 0:NC_S],
                           y22[0:64, :].rearrange("p (b n) -> p b n", b=2)[:, :, 1:64], add, VD if g else None)
                    ts(dst, dst, pebc[:, kind:kind + 1], add)
                kf = kc2.rearrange("p a b -> p (a b)")
                tt(t2, kf, kf, mul, "kc_squared")
                b = got(("kc_mean", r))
                ts(t2, b[:, 0:P], EPS, add, name=VD)
                v(ve.nop(), "kc_var")
                b = got(("vc_rows", r))
                copy(vcr2[0:NC_S, :, :], b[0:NC_S, 0:256].rearrange("p (a b) -> p a b", a=2), VD)
                ve.wait_ge(sem("kc_root"), 2 + r)
                recip(t2, t2)
                stt(kf, kf, colT[:, 28:29], t2, mul, mul, "kc_ready")

            def scored(r):
                b = got(("sc_c", r))
                copy(Sc[:, 0:NC_S], b[:, 0:NC_S], VD)
                red(m_(0), Sc[:, 0:NC_S], mx)
                ts(m_(0), m_(0), -SCALE, mul, name="cmp_max")
                for half in range(2):
                    b = got(("sc_s", r, half))
                    copy(Ss[:, half * 512:(half + 1) * 512], b[:, :], VD)
                b = got(("sc_n", r))
                nm = K("new_mask", P, r * 32, r * 32 + 32)
                tt(Ss[:, 1024:1056], b[:, 0:32], nm, add, VD)
                b = got(("sc_w", r))
                tt(Sw[:, 0:512], b[:, :], K("win_mask"), add, VD)
                b = got(("sc_v", r))
                tt(Sw[:, 512:544], b[:, 0:32], nm, add, VD)
                red(m_(2), Sw[:, :], mx)
                ts(m_(2), m_(2), -SCALE, mul, name="win_max")
                ve.wait_ge(sem("cmp_exp"), r + 1)
                recip(x_(0), s_(0))
                ts(pnrm[:, 0:NC_S], Sc[:, 0:NC_S], x_(0), mul, name="cmp_norm")
                b = got(("imp", r))
                copy(imp[:, 0:NC_S], b[:, 0:NC_S], VD)
                I_ = [imb[:, k, :] for k in range(4)]
                red(I_[0], imp.rearrange("p (n q) -> p n q", q=4), add)
                red(m_(1), I_[0], mn)
                ts(I_[1], I_[0], m_(1), ALU.is_equal)
                tt(I_[1], I_[1], K("blk1"), mul)
                red(x_(1), I_[1], mx)
                ts(I_[2], I_[1], x_(1), ALU.is_equal, NEG, mul)
                for m in range(8):
                    view = Ss[:, m * P:(m + 1) * P].rearrange("p (q x) -> p q x", q=4)
                    tt(view, view, I_[2][:, 4 * (m // 2):4 * (m // 2) + 4].unsqueeze(2).to_broadcast([P, 4, 32]), add)
                red(m_(1), Ss[:, :], mx)
                ts(m_(1), m_(1), -SCALE, mul, name="sel_max")
                b = got(("o_c", r))
                ts(orow[:, :], b[:, 0:DH], grd[:, r, 0:1], mul, name=VD)
                ve.wait_ge(sem("win_probs"), r + 1)
                add_branch(r, 2, "o_w")

            def add_branch(r, k, tag):
                recip(x_(k), s_(k))
                tt(x_(k), x_(k), grd[:, r, k:k + 1], mul)
                b = got((tag, r))
                stt(orow[:, :], b[:, 0:DH], x_(k), orow[:, :], mul, add, VD)

            def selected(r):
                ve.wait_ge(sem("sel_probs"), r + 1)
                add_branch(r, 1, "o_s")
                v(ve.nop(), "round_out")
                b = got(("oTr", r))
                for g in range(2):
                    for jj in range(2):
                        for jp in range(2):
                            c0 = 256 + 8 * r
                            dst = oT[jp * DH:(jp + 1) * DH, 2 * g + jj, c0:c0 + 8].rearrange("p (b t) -> p b t", t=4)
                            src = b[0:DH, 0:P].rearrange("p (b g x) -> p b g x", b=2, g=2)[:, :, g, (2 * jj + jp) * 4:(2 * jj + jp) * 4 + 4]
                            copy(dst, src, VD if (g, jj, jp) == (1, 1, 1) else None)

            rounds(front, scored, selected)
            barrier(ve, "ve")
            if stages < 5:
                return
            ve_late(ve, v, got, copy, tt, ts, stt, red, recip)

        @block.scalar
        def _(se):
            s = Steps(se, "scalar_step", sem)

            def act(out, in_, f, name=None, **kw):
                s(se.activation(out, in_, f, **kw), name)

            def got(tag):
                return drain(se, "s", tag)

            SD = "s_drained"
            se.wait_ge(sem("first_loads"), 16 * L1_FIRST)
            act(ctmp[0:9, :], crow[0:9, :], ACT.Sigmoid, "c_sigmoid")
            b = got("cols")
            act(colT[:, 0:61], b[:, 0:61], ACT.Copy, SD)
            act(colT[:, 4:8], colT[:, 4:8], ACT.Copy, scale=MD ** -0.5)
            se.wait_ge(sem("small_loads"), 16 * L1_SMALL)
            for i, (o, n) in enumerate(TILES):
                act(sqs[0:n, :], x[0:n, i, :], ACT.Square, accum_out=ssum[0:n, i:i + 1])
                act(ssum[0:n, i:i + 1], ssum[0:n, i:i + 1], ACT.Sqrt, "rms", bias=K("eps", n), scale=1.0 / D)
            for i, (o, n) in enumerate(TILES):
                for half in range(2):
                    b = got(("hT", i, half))
                    act(hT[:, 4 * half:4 * half + 4, o:o + n], b[:, 0:4 * n].rearrange("p (j n) -> p j n", j=4), ACT.Copy, SD)
            for c in range(2):
                for m in range(4):
                    b = got(("col", c, m))
                    k = c * 4 + m
                    act(mq[:, k, :], b[:, 0:NTOK], ACT.Identity, SD, bias=colT[:, k:k + 1], scale=MD ** -0.5 if c else 1.0)
            barrier(se, "se")
            if stages < 2:
                return
            se.wait_ge(sem("forget_abs"), 1)
            act(gml[0:4, :], gml[0:4, :], ACT.Exp, "forget_log")
            act(gml[0:4, :], gml[0:4, :], ACT.Ln, "forget_log", bias=K("one", 4))
            se.wait_ge(sem("gate_logs"), 1)
            se.wait_ge(sem("m_final"), 1)
            act(gnd[0:4, :], gnd[0:4, :], ACT.Exp, "gate_exps", scale=-1.0)
            for t_ in (gws, gwi, gwc):
                act(t_[0:4, :], t_[0:4, :], ACT.Exp, "gate_exps")
            for h in range(MH):
                hb = h % 2
                after(se, "v", ("M", h))
                act(WT[:, hb, 0:256], DTt[:, hb, 0:256], ACT.Exp, "decays", bias=aT[:, 0, h:h + 1])
                act(WT[:, hb, 256:384], DTt[:, hb, 256:384], ACT.Exp, "decays", bias=aT[:, 1, h:h + 1])
                act(WT[0:32, hb, 384:416], DTt[0:32, hb, 384:416], ACT.Exp, "decays", bias=aT[0:32, 2, h:h + 1])
                for half in range(2):
                    b = got(("CT", h, half))
                    act(CTh[:, hb, half * 512:(half + 1) * 512], b[:, :], ACT.Copy, SD)
                b = got(("hmT", h))
                act(hmT[:, h, :], b[:, 0:NTOK], ACT.Copy, SD)
            barrier(se, "se")
            if stages < 3:
                return
            for i, (o, n) in enumerate(TILES):
                act(gt24[0:n, i, :], ze(i, n, ZG, 24), ACT.Sigmoid, "branch_gates_ready")
            groups = iter(GATE_GROUPS)

            def gate_groups(count):
                for _ in range(count):
                    c, m = next(groups)
                    b = got(("col", c, m))
                    k = 8 + (c - 2) * 4 + m
                    dst = moT[:, m, :] if c == 2 else gT[:, k - 12, :]
                    act(dst, b[:, 0:NTOK], ACT.Identity, SD, bias=colT[:, k:k + 1])

            def root(i, n, k, heads):
                se.wait_ge(sem("norm_sum"), 3 * i + k + 1)
                act(rs8[0:n, 0:heads], rs8[0:n, 0:heads], ACT.Sqrt, "norm_root", bias=K("eps", n), scale=1.0 / DH)

            for i, (o, n) in enumerate(TILES):
                root(i, n, 0, 8)
                gate_groups(2)
                for name, dst in (("q", qT), ("qr", qrT)):
                    b = got((name, i))
                    act(dst[:, :, o:o + n], b[:, 0:4 * n].rearrange("p (j n) -> p j n", j=4), ACT.Copy, SD)
                root(i, n, 1, 2)
                gate_groups(1)
                root(i, n, 2, 2)
                b = got(("k", i))
                act(kselT[:, o:o + n], b[:, 0:n], ACT.Copy)
                act(kwinT[:, o:o + n], b[:, n:2 * n], ACT.Copy, SD)
            gate_groups(3)
            b = got("cTp")
            for kind in range(2):
                for g in range(2):
                    for par in range(2):
                        c = (2 * kind + par) * P
                        act(cTp[par * DH:(par + 1) * DH, 2 * kind + g, :], b[g * DH:(g + 1) * DH, c:c + P], ACT.Copy,
                            SD if (kind, g, par) == (1, 1, 1) else None)
            gate_groups(2)
            se.wait_ge(sem("kc_var"), 1)
            act(tmpT[:, 0:NC_P], tmpT[:, 0:NC_P], ACT.Sqrt, "kc_root")
            gate_groups(2)
            for i in range(2):
                se.wait_ge(sem("cmp_shifted"), i + 1)
                v3 = sc_c[:, i, :].rearrange("p (h n) -> p h n", n=16)[:, :, 0:NC_P]
                act(v3, v3, ACT.Exp, "cmp_probs", scale=SCALE)
            for i in range(2):
                if i == 1:
                    gate_groups(1)
                for half in range(2):
                    b = got(("pc", i, half))
                    if i == 1:
                        after(se, "v", ("oc", 0))
                    act(ptc[0:NC_P, 4 * half:4 * half + 4, :], b[0:NC_P, :].rearrange("p (j n) -> p j n", j=4), ACT.Copy, SD)

            gate_groups(3)
            act(moT, moT, ACT.Sigmoid, "output_gate")

            def exps(u):
                br, i, g, jp = UNITS[u]
                nk, ub = (i + 1) * P, u % 2
                se.wait_ge(sem("score_max"), u + 1)
                if u >= 2:
                    after(se, "v", ("pv", u - 2))
                for hh in range(2):
                    act(Pu[:, ub, hh * nk:(hh + 1) * nk], Su[:, ub, hh * nk:(hh + 1) * nk], ACT.Exp, "probs",
                        bias=stat[:, ub, 8 + hh:9 + hh], scale=SCALE, accum_out=stat[:, ub, 12 + hh:13 + hh])

            exps(0)
            for u, (br, i, g, jp) in enumerate(UNITS):
                if u + 1 < len(UNITS):
                    exps(u + 1)
                w = 2 * (i + 1) * P
                b = got(("pt", u))
                act(PTu[:, u % 2, 0:w], b[:, 0:w], ACT.Copy, SD)
            for i in range(2):
                b = got(("oT", i))
                act(oT[:, :, i * P:(i + 1) * P], b[:, :].rearrange("p (t n) -> p t n", t=4), ACT.Copy, SD)
            barrier(se, "se")
            if stages < 4:
                return
            def front(r):
                for kind in range(2):
                    for m2 in (1, 3):
                        b = got(("cT", r, kind, m2))
                        for g in range(2):
                            for par in range(2):
                                act(cT[par * DH:(par + 1) * DH, g, m2 * 256:(m2 + 1) * 256],
                                    b[g * DH:(g + 1) * DH, par * 256:(par + 1) * 256], ACT.Copy, SD if (g, par) == (1, 1) else None)
                for q4 in range(4):
                    b = got(("ks", r, q4))
                    act(ksT[:, q4 // 2, (q4 % 2) * 512:(q4 % 2) * 512 + 512], b[:, :], ACT.Copy, SD)
                for q2 in range(2):
                    b = got(("kw", r, q2))
                    act(kwT[:, q2, :], b[:, :], ACT.Copy, SD)
                se.wait_ge(sem("kc_var"), 2 + r)
                act(t2, t2, ACT.Sqrt, "kc_root")

            def scored(r):
                se.wait_ge(sem("cmp_max"), r + 1)
                act(Sc[:, 0:NC_S], Sc[:, 0:NC_S], ACT.Exp, "cmp_exp", bias=st4[:, 0:1], scale=SCALE, accum_out=st4[:, 4:5])
                se.wait_ge(sem("win_max"), r + 1)
                act(Sw[:, :], Sw[:, :], ACT.Exp, "win_probs", bias=st4[:, 2:3], scale=SCALE, accum_out=st4[:, 6:7])
                b = got(("PTc", r))
                act(PTc[0:NC_S, :], b[0:NC_S, 0:P], ACT.Copy, SD)
                b = got(("PTw", r))
                act(PTw[:, 0:4, :], b[:, :].rearrange("p (t n) -> p t n", t=4), ACT.Copy, SD)
                b = got(("PTv", r))
                act(PTw[0:32, 4, :], b[0:32, 0:P], ACT.Copy, SD)
                se.wait_ge(sem("sel_max"), r + 1)
                act(Ss[:, :], Ss[:, :], ACT.Exp, "sel_probs", bias=st4[:, 1:2], scale=SCALE, accum_out=st4[:, 5:6])

            def selected(r):
                for half in range(2):
                    b = got(("PTs", r, half))
                    act(PTs[:, 4 * half:4 * half + 4, :], b[:, :].rearrange("p (t n) -> p t n", t=4), ACT.Copy, SD)
                b = got(("PTn", r))
                act(PTs[0:32, 8, :], b[0:32, 0:P], ACT.Copy, SD)
                act(gT[:, 4 * r:4 * r + 4, :], gT[:, 4 * r:4 * r + 4, :], ACT.Sigmoid, "merge_gates")

            rounds(front, scored, selected)
            barrier(se, "se")
            if stages < 5:
                return
            se_late(se, act, got)

        @block.gpsimd
        def _(pool):
            def dma(out, in_, name, tiny=False):
                pool.dma_start(out, in_, allow_slow_non_contiguous=tiny).then_inc(sem(name), 16)

            rows = A["cache_nsa_kv"][0].rearrange("n (q r) a g d -> (n q) (r a g d)", r=2)

            def sample_rows(r):
                for m in range(8):
                    pool.indirect_dma_start(out=pts[r % 2][:, m, :], out_offset=None, in_=rows,
                                            in_offset=bass.IndirectOffsetOnAxis(idx_u[:, 8 * r + m:8 * r + m + 1], 0)
                                            ).then_inc(sem(f"cache_rows_{r % 2}"), 16)
                for b2 in range(2):
                    dma(wns[r % 2][:, b2, :, :], A["state_win_kv"][0][2 * r + b2].rearrange("(c p) a g d -> p c (a g d)", p=P),
                        f"win_rows_{r % 2}")

            pool.wait_ge(sem("mod_ready"), 2)
            dma(mod_dram, mod[0:9, :], "mod_stored")
            pool.wait_ge(sem("mod_stored"), 16)
            barrier(pool, "pool")
            if stages < 2:
                return
            dma(m0T[0:4, :], A["state_mlstm_m"][0].rearrange("b h -> h b"), "state_small", True)
            dma(n0r[0:32, :], A["state_mlstm_n"][0].rearrange("b h k -> (b h) k"), "state_small")
            dma(n0s[0:8, :, :], A["state_mlstm_n"][0], "state_small")
            for h in range(MH):
                hb = h % 2
                if h >= 2:
                    pool.wait_ge(sem("new_state"), h - 1)
                dma(C0h[:, hb, :].rearrange("p (b k) -> p b k", b=DB), A["state_mlstm_C"][0][:, h].rearrange("b v k -> v b k"), f"state_C_{hb}")
                if h >= 1:
                    store_state(pool, dma, h - 1)
            store_state(pool, dma, MH - 1)
            dma(n_prompt[0], npr[0:1, :, :], "rows_stored")
            dma(n_sample[0], nsr[0:8, :, :], "rows_stored")
            dma(m_prompt[0].rearrange("b h -> h b"), mfin[0:4, 0:1], "rows_stored", True)
            dma(m_sample[0].rearrange("b h -> h b"), mfin[0:4, 1:9], "rows_stored", True)
            pool.wait_ge(sem("rows_stored"), 16 * 4)
            for hb in range(2):
                pool.wait_ge(sem(f"state_stored_{hb}"), 64)
            barrier(pool, "pool")
            if stages < 3:
                return
            dma(pgi[0:1, :], A["page_table"].rearrange("(a b) n -> a (b n)", a=1), "page_table_loaded")
            dma(qg, bc(A["q_norm_g"][0], P), "norm_rows")
            for m in range(3):
                dma(kg[:, m, :], bc(A["k_norm_g"][0][m], P), "norm_rows")
            dma(win_sample[0][:, 0:WIN - DT], A["state_win_kv"][0][:, DT:WIN], "window_moved")
            pool.wait_ge(sem("branch_gates_ready"), 3)
            dma(gate_dram, gt24[0:32, 2, :], "gates_stored")
            for i in range(2):
                pool.wait_ge(sem("kv_rows"), i + 1)
                dma(kv_prompt[0][0, i * P:(i + 1) * P].rearrange("t a g d -> t (a g d)"), zr[:, i, ZKV:ZKV + 512], "kv_stored")
                dma(win_prompt[0][0, i * P:(i + 1) * P].rearrange("t a g d -> t (a g d)"), zr[:, i, ZKV + 512:ZKV + 768], "kv_stored")
            pool.wait_ge(sem("kv_stored"), 64)
            dma(pair, kv_prompt[0][0].rearrange("(p r) a g d -> p (r a g d)", r=2), "pair_rows")
            pool.wait_ge(sem("kv_rows"), 3)
            dma(kv_sample[0].rearrange("b t a g d -> (b t) (a g d)"), zr[0:32, 2, ZKV:ZKV + 512], "kv_stored")
            ws_ = win_sample[0][:, WIN - DT:WIN].rearrange("b t a g d -> b t (a g d)")
            for bb in range(DB):
                dma(ws_[bb], zr[bb * DT:(bb + 1) * DT, 2, ZKV + 512:ZKV + 768], "window_moved")
            pool.wait_ge(sem("gates_stored"), 16)
            pool.wait_ge(sem("gates_cleared"), 1)
            for r in range(4):
                for c in range(4):
                    b_ = 2 * r + c // 2
                    g = c % 2
                    src = gate_dram[b_ * DT:(b_ + 1) * DT, g * HPG * 3:(g + 1) * HPG * 3].rearrange("t (j k) -> j t k", k=3)
                    dma(grd[32 * c:32 * c + 16, r, :], src, "round_gates")
            pool.wait_ge(sem("cache_index"), 1)
            ring, k = chunk_last[("col", len(COL_CHUNKS) - 1)]
            pool.wait_ge(sem(f"{ring}_filled"), k)
            sample_rows(0)
            pool.wait_ge(sem("window_moved"), 16 * 9)
            pool.wait_ge(sem("kv_stored"), 16 * 5)
            barrier(pool, "pool")
            if stages < 4:
                return
            for r in range(1, 4):
                if r >= 2:
                    after(pool, "v", ("o_s", r - 2))
                sample_rows(r)
            barrier(pool, "pool")
            if stages < 5:
                return
            pool_late(pool, dma)

        @block.sync
        def _(sp):
            for o_, i_ in first:
                sp.dma_start(o_, i_).then_inc(sem("first_loads"), 16)
            for o_, i_ in small:
                sp.dma_start(o_, i_).then_inc(sem("small_loads"), 16)
            passed = 1

            def load(n):
                tag, src = chunks[n]
                if n >= NW:
                    ring, k = chunk_last[chunks[n - NW][0]]
                    sp.wait_ge(sem(f"{ring}_filled"), k)
                t, w = src.shape[1], src.shape[2]
                sp.dma_start(slots[n % NW][:, 0:t * w].rearrange("p (t n) -> p t n", t=t), src).then_inc(sem(f"weights_{n % NW}"), 16)

            n1 = 4 + len(STAGE1)
            for n in range(n1):
                load(n)
            for j in range(D // P):
                sp.dma_start(y_dram[NEXP * CAP:, j * P:(j + 1) * P].rearrange("(b s) n -> s b n", s=CAP),
                             K("zeros", CAP).unsqueeze(1).to_broadcast([CAP, OVER, P])).then_inc(sem("further_cleared"), 16)
            late = [3, 3, 2]
            barrier(sp, "sp")
            for count in late:
                if count == late[-1]:
                    sp.wait_ge(sem("v_filled"), tags["v"].index(("o_s", 2)) + 1)
                for n in range(n1, n1 + count):
                    load(n)
                n1 += count
                barrier(sp, "sp")
            for n in range(n1, NCHUNK):
                load(n)
            sp_late(sp)


_OUTS = [((1, SEQ, D), "y_prompt"), ((DB, DT, D), "y_sample"),
         ((1, 1, SEQ, 4, KV, DH), "kv_prompt"), ((1, DB, DT, 4, KV, DH), "kv_sample"),
         ((1, 1, SEQ, 2, KV, DH), "win_prompt"), ((1, DB, WIN, 2, KV, DH), "win_sample"),
         ((1, 1, MH, MD, MD), "C_prompt"), ((1, 1, MH, MD), "n_prompt"), ((1, 1, MH), "m_prompt"),
         ((1, DB, MH, MD, MD), "C_sample"), ((1, DB, MH, MD), "n_sample"), ((1, DB, MH), "m_sample")]


def kernel(**inputs):
    import concourse.bacc as _bacc
    from concourse.bass_utils import run_bass_kernel_spmd as _run

    nc = _bacc.Bacc("TRN2", target_bir_lowering=False, num_devices=1)
    arrays = {"in_" + k: np.ascontiguousarray(v) for k, v in inputs.items()}
    arrays["in_tables"] = constants()[0]
    args = {k[3:]: nc.dram_tensor(k, v.shape, mybir.dt.from_np(v.dtype), kind="ExternalInput").ap()
            for k, v in arrays.items()}
    outs = [nc.dram_tensor("out_" + name, shape, F32, kind="ExternalOutput").ap() for shape, name in _OUTS]
    program(nc, args, outs, stages=STAGES)
    r = _run(nc, [arrays], core_ids=[0])
    return tuple(r.results[0]["out_" + name] for _, name in _OUTS)
```

```python
import numpy as np
import concourse.bass as bass
from concourse import mybir
from contextlib import ExitStack

F32 = mybir.dt.float32
BF16 = mybir.dt.bfloat16
I32 = mybir.dt.int32
U32 = mybir.dt.uint32
ALU = mybir.AluOpType
ACT = mybir.ActivationFunctionType
AX = mybir.AxisListType

P = 128
D = 1024
SEQ = 256
DB, DT = 8, 4
NTOK = SEQ + DB * DT
TILES = [(0, 128), (128, 128), (256, 32)]
PAST = 1024
PAGE = 128
MH, MD = 4, 128
AH, KV, HPG, DH = 8, 2, 4, 64
SEG = 16
NC_P = SEQ // SEG - 1
NC_S = PAST // SEG - 1
WIN = 512
NEXP, TOPK = 32, 4
CAP = 64
OVER = (NTOK * TOPK + NEXP * (CAP - 1)) // CAP - NEXP
NBLK = NEXP + OVER
SCALE = DH ** -0.5
EPS = 1e-6
NEG = -1e30

ZV, ZI, ZF, ZQ, ZKV, ZG, ZN = 0, 512, 516, 520, 1032, 1800, 1824
ROW_CHUNKS = [(1024, 512, 0), (2048, 512, 512), (2560, 512, 1024), (3072, 288, 1536)]
COL_CHUNKS = [0, 512, 1536, 3360, 3872, 4384, 4896]
STAGE1 = [("ada", 4), ("row", 0), ("ada", 5), ("ada", 6), ("row", 1), ("ada", 7), ("row", 2), ("ada", 8),
          ("row", 3), ("ada", 9), ("col", 0), ("ada", 10), ("col", 1), ("ada", 11)]
GATE_CHUNKS = [3, 4, 5, 6, 2]
WORDS = 4096
NW = 3


def constants():
    t = {}
    i = np.arange(P)
    t["ident"] = np.eye(P)
    t["zeros"] = np.zeros((P, P))
    t["causal"] = np.where(i[None, :] <= i[:, None], 0.0, NEG)
    t["causal_t"] = np.where(i[:, None] <= i[None, :], 0.0, NEG)
    t["zeros_t"] = np.zeros((P, P))
    sel = np.zeros((P, NTOK))
    sel[0, :SEQ] = 1
    for b in range(DB):
        sel[1 + b, SEQ + b * DT:SEQ + (b + 1) * DT] = 1
    t["sel"] = sel
    pos = np.concatenate([np.arange(SEQ), PAST + np.tile(np.arange(DT), DB)]).astype(np.float32)
    inv = (np.float32(500000.0) ** (-np.arange(8, dtype=np.float32) * np.float32(2.0 / 16))).astype(np.float32)
    ang = np.zeros((3 * P, 8), np.float32)
    ang[:NTOK] = pos[:, None] * inv[None, :]
    t["cos"] = np.cos(ang.astype(np.float64)).reshape(3, P, 8).transpose(1, 0, 2).reshape(P, 24)
    t["sin"] = np.sin(ang.astype(np.float64)).reshape(3, P, 8).transpose(1, 0, 2).reshape(P, 24)
    oh = np.zeros((P, MH * P))
    for h in range(MH):
        oh[h, h * P:(h + 1) * P] = 1
    t["head_row"] = oh
    r = np.arange(DB * DT)
    same = (r[:, None] // DT == r[None, :] // DT) & (r[:, None] <= r[None, :])
    m = np.full((P, DB * DT), NEG)
    m[:DB * DT] = np.where(same, 0.0, NEG)
    t["sample_t"] = m
    m = np.zeros((P, DB))
    m[r, r // DT] = 1
    t["batch_of"] = m
    t["ones"] = np.ones((P, P))
    n = np.arange(NC_P)
    q = np.arange(SEQ)
    m = np.where(n[None, :] * SEG + 2 * SEG - 1 <= q[:, None], 0.0, NEG)
    t["cmp_mask"] = m.reshape(2, P, NC_P).transpose(1, 0, 2).reshape(P, 2 * NC_P)
    t["cmp_valid"] = (q >= 2 * SEG - 1).astype(float).reshape(2, P).T
    combo, j, tt = i // 32, (i % 32) // DT, i % DT
    used = i % 32 < HPG * DT
    g = (combo[:, None] == combo[None, :]) & (tt[:, None] == tt[None, :]) & used[:, None] & used[None, :]
    t["head_sum"] = g.astype(float)
    m = np.full((P, 4, DB * DT), 0.0)
    for rnd in range(4):
        b = 2 * rnd + combo // 2
        ok = (r[None, :] // DT == b[:, None]) & (r[None, :] % DT <= tt[:, None])
        m[:, rnd] = np.where(ok, 0.0, NEG)
    t["new_mask"] = m.reshape(P, -1)
    key = np.arange(WIN)
    t["win_mask"] = np.where(key[None, :] > tt[:, None], 0.0, NEG)
    t["blk1"] = np.tile(np.arange(1, 17), (P, 1))
    blk = (i[:, None] // DH == i[None, :] // DH) / DH
    t["half_mean"] = blk
    t["pair_in_page"] = (i % 64)[:, None]
    t["first_page"] = (i < 64)[:, None].astype(float)
    t["second_page"] = (i >= 64)[:, None].astype(float)
    t["before"] = (i[:, None] < i[None, :]).astype(float)
    t["expert"] = np.tile(np.arange(NEXP), (P, 1))
    t["token"] = np.stack([i, i + 128, i + 256], 1)
    t["expert_mod"] = (i % NEXP)[:, None]
    t["over_id"] = np.tile(np.arange(OVER), (P, 1))
    m = np.zeros((P, NEXP))
    m[np.arange(96), np.arange(96) % NEXP] = 1
    t["expert_row"] = m
    t["one"] = np.ones((P, 1))
    t["eps"] = np.full((P, 1), EPS)
    cols, at = {}, 0
    for k, v in t.items():
        cols[k] = (at, at + v.shape[1])
        at += v.shape[1]
    return np.concatenate(list(t.values()), 1).astype(np.float32), cols



class Steps:

    def __init__(self, eng, own, sem):
        self.eng, self.own, self.sem, self.count = eng, own, sem, {}

    def __call__(self, ins, name=None):
        name = name or self.own
        self.count[name] = self.count.get(name, 0) + 1
        ins.then_inc(self.sem(name), 1)
        self.eng.wait_ge(self.sem(name), self.count[name])


def program(nc, a, outs):
    _, CC = constants()
    ncols = max(e for _, e in CC.values())
    (y_prompt, y_sample, kv_prompt, kv_sample, win_prompt, win_sample,
     C_prompt, n_prompt, m_prompt, C_sample, n_sample, m_sample) = outs
    ctx = ExitStack()
    with ctx:
        def sb(name, shape, dt=F32):
            return ctx.enter_context(nc.sbuf_tensor(name, shape, dt))

        names = {}

        def sem(name):
            if name not in names:
                names[name] = ctx.enter_context(nc.semaphore(name))
            return names[name]

        mod_dram = nc.dram_tensor("mod_rows", [9, 6 * D], F32).ap()
        h2_dram = nc.dram_tensor("h2_rows", [NTOK, D], F32).ap()
        y_dram = nc.dram_tensor("expert_rows", [NBLK * CAP, D], F32).ap()
        slot_dram = nc.dram_tensor("slot_token", [(NBLK + 1) * CAP, 1], F32).ap()
        gate_dram = nc.dram_tensor("branch_gates", [DB * DT, AH * 3], F32).ap()

        C = sb("const_tables", [P, ncols])
        x = sb("x_rows", [P, 3, D])
        ARENA = 47300
        arena = sb("arena", [P, ARENA])

        def K(name, rows=P, lo=0, hi=None):
            b, e = CC[name]
            return C[0:rows, b + lo:(b + hi if hi is not None else e)]

        at = [NW * WORDS]

        def take(*shape, dt=F32):
            n = int(np.prod(shape))
            words = n if dt != BF16 else (n + 1) // 2
            words += words % 2
            assert at[0] + words <= ARENA, (at[0] + words, ARENA)
            v = arena[:, at[0]:at[0] + words]
            at[0] += words
            if dt != F32:
                v = v.bitcast(dt)
            v = v[:, 0:n]
            if len(shape) == 2:
                v = v.rearrange("p (a b) -> p a b", a=shape[0])
            if len(shape) == 3:
                v = v.rearrange("p (a b c) -> p a b c", a=shape[0], b=shape[1])
            return v

        slots = [arena[:, n * WORDS:(n + 1) * WORDS] for n in range(NW)]
        zr = take(3, ZN)
        hT = take(8, NTOK)
        qT = take(HPG, NTOK)
        qrT = take(HPG, NTOK)
        kselT = take(NTOK)
        kwinT = take(NTOK)
        oT = take(4, NTOK)
        hmT = take(MH, NTOK)
        w2 = take(2, 8, 128)
        colT = take(62)
        pebc = take(2)
        BASE = at[0]
        mq = take(8, NTOK)
        AFTER_MQ = at[0]

        bank_v = [ctx.enter_context(nc.psum_tensor(f"bank_v{n}", [P, 512], F32)) for n in range(4)]
        bank_s = [ctx.enter_context(nc.psum_tensor(f"bank_s{n}", [P, 512], F32)) for n in range(4)]
        tags = {"v": [], "s": [], "v_taken": [], "s_taken": []}
        cur = {}

        def fill(pe, ring, tag):
            n = len(tags[ring])
            tags[ring].append(tag)
            if n >= 4:
                pe.wait_ge(sem(f"{ring}_drained"), n - 3)
            return (bank_v if ring == "v" else bank_s)[n % 4]

        def filled(ring, ins):
            ins.then_inc(sem(f"{ring}_filled"), 1)

        def drain(eng, ring, tag):
            n = len(tags[ring + "_taken"])
            assert tags[ring][n] == tag, (tags[ring][n], tag)
            tags[ring + "_taken"].append(tag)
            eng.wait_ge(sem(f"{ring}_filled"), n + 1)
            return (bank_v if ring == "v" else bank_s)[n % 4]

        def after(eng, ring, tag):
            n = len(tags[ring]) - 1 - tags[ring][::-1].index(tag)
            eng.wait_ge(sem(f"{ring}_drained"), n + 1)

        barriers = {}

        def barrier(eng, who):
            n = barriers[who] = barriers.get(who, 0) + 1
            eng.drain().then_inc(sem("stage_left"), 1)
            eng.wait_ge(sem("stage_left"), 5 * n)

        def vec(ap_):
            return ap_.rearrange("(a n) -> a n", a=1)

        A = a
        w_in, b_in = A["w_in"][0], A["b_in"][0]
        kt_ = lambda w: w.rearrange("(t p) n -> p t n", p=P)
        chunks = []
        def chunk_of(tag):
            kind, n = tag
            if kind == "ada":
                return kt_(A["w_ada"][0][:, n * 512:(n + 1) * 512])
            c, w = (ROW_CHUNKS[n][0], ROW_CHUNKS[n][1]) if kind == "row" else (COL_CHUNKS[n], 512)
            return kt_(w_in[:, c:c + w])

        for tag in [("ada", n) for n in range(4)] + STAGE1 + [("col", n) for n in GATE_CHUNKS]:
            chunks.append((tag, chunk_of(tag)))
        chunks.append((("up_m", 0), kt_(A["w_up_m"][0])))
        chunks.append((("up_a", 0), kt_(A["w_up_a"][0])))
        for n in range(2):
            chunks.append((("out", n), kt_(A["w_out"][0][:, n * 512:(n + 1) * 512])))
        NCHUNK = len(chunks)
        chunk_at = {c[0]: n for n, c in enumerate(chunks)}
        FIRST_UP = chunk_at[("up_m", 0)]
        slot_of = [n % NW for n in range(FIRST_UP)] + [n % NW for n in range(NCHUNK - FIRST_UP)]

        def before_in_slot(n):
            return [k for k in range(n) if slot_of[k] == slot_of[n]]

        def weights(pe, tag):
            n = chunk_at[tag]
            pe.wait_ge(sem(f"weights_{slot_of[n]}"), 16 * (len(before_in_slot(n)) + 1))
            src = chunks[n][1]
            t, w = src.shape[1], src.shape[2]
            return slots[slot_of[n]][:, 0:t * w].rearrange("p (t n) -> p t n", t=t)

        at[0] = BASE + 2304
        csil = take(8, 9)
        crow = take(D)
        ctmp = take(D)
        gmix = take(D)
        gffn = take(D)
        mod = take(6 * D)
        hrow = take(2, D)
        rowbias = take(ZN)
        ssum = take(3)
        rstd = take(3)
        rows61 = take(P)
        sqs = take(D)
        at[0] = AFTER_MQ
        gi, gf, gb, ga_, gM, gnd, gml = (take(NTOK) for _ in range(7))
        gtmp = take(NTOK)
        gws, gwi = take(32), take(32)
        m0T = take(8)
        gwc = take(8)
        aT = take(3, 4)
        ndT = take(3, 4)
        wsT, wiT, wcT = take(4), take(4), take(4)
        wcb = take(32)
        n0r, n0T = take(P), take(32)
        nqT = take(4)
        DTt = take(2, 416)
        WT = take(2, 416)
        STt = take(2, 416)
        C0h = take(2, 1024)
        flat = x.rearrange("p a b -> p (a b)")
        CTh = flat[:, 0:2048].rearrange("p (a b) -> p a b", a=2)
        krow = flat[:, 2048:2816].rearrange("p (a b) -> p a b", a=2)
        Cn = arena[:, qT.offset:qT.offset + 2048].rearrange("p (a b) -> p a b", a=2)
        vw = take(2, 256)
        wsb = take(2, 8)
        vwb = take(2, 1024)
        numI = take(2, 32)
        hrw = take(2, 384)
        den = take(2, 4)
        Cpr = take(2, P)
        npr = take(MH, P)
        nsr = take(MH, P)
        n0s = take(MH, P)
        mfin = take(16)
        assert at[0] <= ARENA - 16 * NTOK, at[0]
        at[0] = BASE
        sq = take(512)
        qg = flat[:, 2816:2880]
        kg = flat[:, 2880:3072].rearrange("p (a b) -> p a b", a=3)
        rs8 = take(8)
        qn = take(2, 512)
        qr = take(2, 512)
        rt = take(4, 64)
        pair = take(1024)
        cTp = take(4, P)
        y2c = take(2, 128)
        kcT = take(P)
        vcT = take(P)
        tmpT = take(P)
        vcr = take(2, P)
        sc_c = take(2, 128)
        ptc = take(8, P)
        moT = take(MH, NTOK)
        assert at[0] <= 42000
        at[0] = ARENA - 16 * NTOK
        gT = take(16, NTOK)
        KEPT = ARENA - 16 * NTOK - 540
        at[0] = KEPT
        gt24 = take(3, 24)
        stat = take(4, 16)
        grd = take(4, 3)
        idx_f = take(64)
        idx_t = take(64)
        idx_u = take(32, dt=U32)
        pgi = take(64, dt=I32)
        pgf = take(64)
        assert at[0] <= ARENA - 16 * NTOK, at[0]
        Su, PTu, ob = (x[:, n, :].rearrange("p (a b) -> p a b", a=2) for n in range(3))
        at[0] = 0
        pt_even = take(8, 1024)
        Ss = take(1056)
        Sw = take(544)
        PTs = take(9, P)
        kc2 = take(2, 64)
        vc2 = take(2, 64)
        t2 = take(P)
        y22 = take(P)
        vcr2 = take(2, P)
        PTc = take(P)
        imp = take(64)
        pnrm = take(64)
        Sc = take(64)
        assert at[0] <= 3 * WORDS
        at[0] = hT.offset
        wn_even = take(2, 4, 256)
        at[0] = BASE
        pts, wns = (pt_even, take(8, 1024)), (wn_even, take(2, 4, 256))
        cT = take(2, 1024)
        ksT = take(2, 1024)
        kwT = cT[:, 0, :].rearrange("p (b n) -> p b n", b=2)
        PTw = cT[:, 1, 0:640].rearrange("p (t n) -> p t n", t=5)
        imb = take(4, 16)
        st4 = take(16)
        qTr = take(2, 32)
        qrTr = take(2, 32)
        orow = take(64)
        assert at[0] <= KEPT, at[0]

        def ze(i, n, c, w):
            return zr[0:n, i, c:c + w]

        def kvrows(i, n, kind, g=None):
            c = ZKV + kind * 128
            return ze(i, n, c, 128) if g is None else ze(i, n, c + g * DH, DH)

        ident = K("ident")
        UNITS = [(br, i, g, jp) for br in range(2) for i in range(2) for g in range(2) for jp in range(2)]
        chunk_last = {}

        GATE_GROUPS = [(c, m) for c in GATE_CHUNKS for m in range(4)]

        def quarters(w):
            return [(c0, min(P, w - c0)) for c0 in range(0, w, P)]

        def cols_of(lo, n):
            return b_in[lo:lo + n * P].rearrange("(a p) -> a p", p=P)

        def bc(v, n):
            return v.partition_broadcast(n)

        first = [(C[:, :], A["tables"]),
                 (crow[0:1, :], A["c_prompt"]), (crow[1:9, :], A["c_sample"])]
        small = [(rows61[0:8, :], cols_of(0, 8)), (rows61[8:12, :], cols_of(1536, 4)),
                 (rows61[12:28, :], cols_of(3360, 16)),
                 (rows61[28:29, 0:64], A["k_norm_g"][0][0:1]), (rows61[28:29, 64:128], A["k_norm_g"][0][0:1]),
                 (rows61[29:45, :], A["cmp_pe_k"][0].rearrange("(a r) d -> a (r d)", r=2)),
                 (rows61[45:61, :], A["cmp_pe_v"][0].rearrange("(a r) d -> a (r d)", r=2)),
                 (gmix[0:9, :], bc(A["g_mix"][0], 9)), (gffn[0:9, :], bc(A["g_ffn"][0], 9)),
                 (mod[0:9, :], bc(A["b_ada"][0], 9)),
                 (x[:, 0, :], A["x_prompt"][0][0:128]), (x[:, 1, :], A["x_prompt"][0][128:256]),
                 (x[0:32, 2, :], A["x_sample"].rearrange("b t d -> (b t) d"))]
        after_ada = [(rowbias[:, 0:512], bc(b_in[1024:1536], P)), (rowbias[:, 512:ZN], bc(b_in[2048:3360], P))]
        for kind, name in enumerate(("cmp_w_k", "cmp_w_v")):
            src = A[name][0].rearrange("(h u r) d e -> r h d u e", h=2, r=2)
            for par in range(2):
                for half in range(2):
                    after_ada.append((w2[par * DH:(par + 1) * DH, kind, :, half * DH:(half + 1) * DH], src[par, half]))
        L1_FIRST, L1_SMALL = len(first), len(small)


        def view_at(v_, *shape):
            o = v_.offset
            n = int(np.prod(shape))
            w_ = arena[:, o:o + n]
            return w_.rearrange("p (a b) -> p a b", a=shape[0]) if len(shape) == 2 else w_

        merged = view_at(qT, 8, NTOK)
        at[0] = BASE
        squares = take(D)
        modl = take(3, D)
        h2 = take(3, D)
        h2T = take(8, NTOK)
        bparts = take(3, D, dt=BF16)
        assert at[0] <= 38400
        at[0] = 38400
        wr = take(8, NEXP)
        brt = take(NEXP)
        ss2 = take(3)
        L = take(3, NEXP)
        m8 = take(3, 8)
        i8 = take(3, 8, dt=U32)
        i8f = take(3, 8)
        pick = take(4, 3 * NEXP)
        picked = take(3, NEXP)
        pos = take(3, NEXP)
        cnt = take(NEXP)
        ov = take(NEXP)
        ove = take(NEXP)
        ovs = take(NEXP)
        base_ = take(NEXP)
        tmp32 = take(OVER * NEXP)
        tmp32b = take(OVER * NEXP)
        destf = take(3, 4)
        zslot = take(P)
        slotr = take(P)
        assert at[0] <= 41000, at[0]
        at[0] = 41000
        bias3 = take(3 * D, dt=BF16)
        gt2 = take(D)
        gate4 = take(3, 4)
        dest = take(12, dt=U32)
        slotu = take(NBLK + 1, dt=U32)
        over_e = take(OVER, dt=I32)
        over_n = take(2, dt=I32)
        ohx = take(NBLK + 1)
        bfi = take(OVER)
        brow = take(D)
        assert brow.offset >= gT.offset
        NE = 6
        eslots = [arena[:, n * WORDS:(n + 1) * WORDS] for n in range(NE)]
        at[0] = NE * WORDS
        xg = take(D)
        xT = take(8, CAP)
        gbuf = take(2, 512)
        sgb = take(2, 512)
        ub = take(2, 512)
        actT = take(2, 4 * CAP)
        yb = take(512)
        idx_cur = take(2, dt=U32)
        bsel_gu = take(CAP, dt=BF16)
        bsel_dn = take(CAP, dt=BF16)
        assert at[0] <= 38400
        at[0] = 0
        yk = take(12, D)
        fin = take(3, D)
        gate2 = take(2, D)
        diag = take(TOPK, P)
        ROUNDS_OVER = -(-NTOK // CAP) - 1

        def ebank(k):
            return (bank_v + bank_s)[k]

        block = ctx.enter_context(nc.Block())

        def pe_late(pe, mm, tr, col_chunk, used):
            w = weights(pe, ("up_a", 0))
            for m in range(8):
                b = fill(pe, "v", ("up_a", m))
                for t in range(4):
                    last = mm(b[:, 0:NTOK], w[:, t, m * P:(m + 1) * P], oT[:, t, :], t == 0, t == 3)
                filled("v", last)
            used(("up_a", 0), "v")
            pe.wait_ge(sem("mod_reloaded"), 16 * 3)

            def spread(i, n, row, tag):
                o = TILES[i][0]
                b = fill(pe, "v", tag)
                filled("v", mm(b[0:n, :], K("sel", 9, o, o + n), row, True, True))

            pe.wait_ge(sem("merged_ready"), 8)
            for half in range(2):
                w = weights(pe, ("out", half))
                hs = slice(half * 512, half * 512 + 512)
                for i, (o, n) in enumerate(TILES):
                    b = fill(pe, "v", ("mix", half, i))
                    for t in range(8):
                        if i < 2:
                            last = mm(b[0:n, :], merged[:, t, o:o + n], w[:, t, :], t == 0, t == 7)
                        else:
                            for j in range(4):
                                last = mm(b[32 * j:32 * j + n, 0:P], merged[:, t, o:o + n], w[:, t, j * P:(j + 1) * P], t == 0, t == 7)
                    filled("v", last)
                    spread(i, n, modl[0:9, 0, hs], ("gate1", half, i))
                used(("out", half), "v")
            for i, (o, n) in enumerate(TILES):
                for half in range(2):
                    hs = slice(half * 512, half * 512 + 512)
                    spread(i, n, modl[0:9, 2, hs], ("scale2", i, half))
                    spread(i, n, modl[0:9, 1, hs], ("shift2", i, half))
                for half in range(2):
                    pe.wait_ge(sem("h2_rows"), 2 * i + half + 1)
                    b = fill(pe, "s", ("h2T", i, half))
                    for j in range(4):
                        last = tr(b[:, j * n:(j + 1) * n], h2[0:n, i, (4 * half + j) * P:(4 * half + j + 1) * P])
                    filled("s", last)
            pe.wait_ge(sem("router_loaded"), 32)
            after(pe, "s", ("h2T", 2, 1))
            for i, (o, n) in enumerate(TILES):
                b = fill(pe, "v", ("router", i))
                for t in range(8):
                    last = mm(b[0:n, 0:NEXP], h2T[:, t, o:o + n], wr[:, t, :], t == 0, t == 7)
                filled("v", last)
            pe.wait_ge(sem("picked_ready"), 1)
            for i, (o, n) in enumerate(TILES):
                b = fill(pe, "v", ("place", i))
                for j in range(i + 1):
                    nj = TILES[j][1]
                    lhs = K("before", nj, 0, n) if j == i else K("ones", nj, 0, n)
                    last = mm(b[0:n, 0:NEXP], lhs, picked[0:nj, j, :], j == 0, j == i)
                filled("v", last)
            b = fill(pe, "v", "count")
            for i, (o, n) in enumerate(TILES):
                last = mm(b[:, 0:NEXP], K("ones", n), picked[0:n, i, :], i == 0, i == 2)
            filled("v", last)
            pe.wait_ge(sem("slots_loaded"), 16)
            b = fill(pe, "v", "slots")
            filled("v", tr(b[0:CAP, 0:NBLK + 1], slotr[0:NBLK + 1, 0:CAP]))
            barrier(pe, "pe")
            W = eslots

            def beside(bank, half):
                return ebank(bank)[half * CAP:(half + 1) * CAP, :]

            def turn(bank, rows, c0):
                for j in range(4):
                    last = tr(ebank(bank)[:, j * CAP:(j + 1) * CAP], rows[:, c0 + j * P:c0 + (j + 1) * P])
                return last

            def pe_block(e):
                pe.wait_ge(sem("rows_turned"), 2 * e + 2)
                pe.wait_ge(sem("gu_bias_ready"), e + 1)
                for c in range(2):
                    pe.wait_ge(sem(f"expert_weights_{2 * c}"), 16 * e + 16)
                    pe.wait_ge(sem(f"expert_weights_{2 * c + 1}"), 16 * e + 16)
                    pe.wait_ge(sem("gu_drained"), 2 * e + c + 1)
                    for q in range(2):
                        b0 = q * D + c * 512
                        mm(beside(c, q), bsel_gu[0:96, :], bias3[0:96, b0:b0 + 512], True, False)
                    for t in range(8):
                        for q in range(2):
                            w = W[2 * c + q].rearrange("p (t n) -> p t n", t=8)
                            last = mm(beside(c, q), xT[:, t, :], w[:, t, :], False, t == 7)
                    last.then_inc(sem("gu_filled"), 1)
                for c in range(2):
                    pe.wait_ge(sem("act_ready"), 2 * e + c + 1)
                    if c == 1:
                        pe.wait_ge(sem("rows_turned"), 2 * e + 3)
                    pe.sem_inc(sem("act_seen"), 1)
                    turn(6 + c, ub[0:CAP, c, :], 0).then_inc(sem("act_turning"), 1)
                    if c == 0:
                        pe.wait_ge(sem("act_turned"), 2 * e + 2)
                        pe.wait_ge(sem("rows_gathered"), 16 * e + 32)
                        pe.sem_inc(sem("rows_seen"), 1)
                        turn(7, xg[0:CAP, :], 0).then_inc(sem("rows_turning"), 1)
                        pe.wait_ge(sem("act_turned"), 2 * e + 3)
                        pe.sem_inc(sem("rows_seen"), 1)
                        turn(6, xg[0:CAP, :], 512).then_inc(sem("rows_turning"), 1)
                        pe.wait_ge(sem("y_drained"), e + 1)
                        pe.wait_ge(sem("dn_bias_ready"), e + 1)
                        for half in range(2):
                            b0 = 2 * D + half * 512
                            mm(beside(4, half), bsel_dn[0:96, :], bias3[0:96, b0:b0 + 512], True, False)
                    pe.wait_ge(sem("act_turned"), 2 * e + 3 + c)
                    pe.wait_ge(sem(f"expert_weights_{4 + c}"), 16 * e + 16)
                    w = W[4 + c].rearrange("p (t n) -> p t n", t=4)
                    for t in range(4):
                        for half in range(2):
                            last = mm(beside(4, half), actT[:, c, t * CAP:(t + 1) * CAP], w[:, t, half * 512:half * 512 + 512],
                                      False, c == 1 and t == 3)
                    last.then_inc(sem("dn_filled"), 1)

            pe.wait_ge(sem("bias_placed"), 16 * 9)
            pe.wait_ge(sem("rows_gathered"), 16)
            turn(7, xg[0:CAP, :], 0).then_inc(sem("rows_turning"), 1)
            turn(6, xg[0:CAP, :], 512).then_inc(sem("rows_turning"), 1)
            blocks(pe, pe_block)
            barrier(pe, "pe")
            pe.wait_ge(sem("gate2_loaded"), 16)
            for i in (0, 2):
                o, n = TILES[i]
                for half in range(2):
                    b = fill(pe, "s", ("gate2", i, half))
                    filled("s", mm(b[0:n, :], K("sel", 9, o, o + n), gt2[0:9, half * 512:half * 512 + 512], True, True))
            pe.wait_ge(sem("choice_weights"), TOPK)
            pe.wait_ge(sem("picked_rows_1"), 16 * TOPK)
            for half in range(2):
                b = fill(pe, "v", ("sum", half))
                for k in range(TOPK):
                    last = mm(b[:, :], diag[:, k, :], yk[:, TOPK + k, half * 512:half * 512 + 512], k == 0, k == TOPK - 1)
                filled("v", last)
            barrier(pe, "pe")

        def rounds(front, scored, selected):
            front(0)
            for r in range(4):
                scored(r)
                if r < 3:
                    front(r + 1)
                selected(r)

        def blocks(eng, body, further=None):
            with eng.Fori(0, NEXP) as e:
                body(e)
            n = eng.value_load(over_n[0:1, 0:1], min_val=0, max_val=OVER)
            with eng.If(n > 0):
                with eng.Fori(NEXP, NEXP + n) as e:
                    (further or body)(e)

        def ve_late(ve, v, got, copy, tt, ts, stt, red, recip):
            VD, add, mul, sub, mx, mn = "v_drained", ALU.add, ALU.mult, ALU.subtract, ALU.max, ALU.min
            for m in range(8):
                b = got(("up_a", m))
                tt(gT[:, 8 + m, :], b[:, 0:NTOK], gT[:, 8 + m, :], mul, VD)
                tt(merged[:, m, :], gT[:, m, :], gT[:, 8 + m, :], add, "merged_ready")
            ve.wait_ge(sem("mod_reloaded"), 16 * 3)
            ve.wait_ge(sem("x_again"), 48)
            for half in range(2):
                hs = slice(half * 512, half * 512 + 512)
                for i, (o, n) in enumerate(TILES):
                    b = got(("mix", half, i))
                    t_ = h2[0:n, 0, 0:512]
                    if i < 2:
                        copy(t_, b[0:n, :], VD)
                    else:
                        for j in range(4):
                            copy(h2[0:n, 0, j * P:(j + 1) * P], b[32 * j:32 * j + n, 0:P], VD if j == 3 else None)
                    b = got(("gate1", half, i))
                    tt(t_, t_, b[0:n, :], mul, VD)
                    tt(x[0:n, i, hs], x[0:n, i, hs], t_, add, "x_mixed")
            for i, (o, n) in enumerate(TILES):
                ve.wait_ge(sem("rms"), 4 + i)
                recip(ss2[0:n, i:i + 1], ss2[0:n, i:i + 1])
                for half in range(2):
                    hs = slice(half * 512, (half + 1) * 512)
                    b = got(("scale2", i, half))
                    stt(h2[0:n, i, hs], x[0:n, i, hs], ss2[0:n, i:i + 1], b[0:n, :], mul, mul, VD)
                    b = got(("shift2", i, half))
                    tt(h2[0:n, i, hs], h2[0:n, i, hs], b[0:n, :], add, VD)
                    v(ve.nop(), "h2_rows")
            v(ve.memset(zslot[:, :], 0.0), "zero_slots")
            for t_ in (L, m8, i8f, pos):
                v(ve.memset(t_[:, 2, :], 0.0))
            for i, (o, n) in enumerate(TILES):
                b = got(("router", i))
                l_ = L[0:n, i, :]
                tt(l_, b[0:n, 0:NEXP], brt[0:n, :], add, VD)
                v(ve.max(m8[0:n, i, :], l_))
                v(ve.max_index(i8[0:n, i, :], m8[0:n, i, :], l_))
                copy(i8f[0:n, i, :], i8[0:n, i, :])
                ts(gate4[0:n, i, :], m8[0:n, i, 0:4], m8[0:n, i, 0:1], sub, name="gate_shifted")
            all3 = [P, 3, NEXP]
            experts = K("expert").unsqueeze(1).to_broadcast(all3)
            pick3 = [pick[:, k, :].rearrange("p (i e) -> p i e", i=3) for k in range(TOPK)]
            for k in range(TOPK):
                tt(pick3[k], experts, i8f[:, :, k:k + 1].to_broadcast(all3), ALU.is_equal)
            tt(picked, pick3[0], pick3[1], add)
            tt(picked, picked, pick3[2], add)
            tt(picked, picked, pick3[3], add, "picked_ready")
            for i, (o, n) in enumerate(TILES):
                b = got(("place", i))
                copy(pos[0:n, i, :], b[0:n, 0:NEXP], VD)
            b = got("count")
            copy(cnt, b[:, 0:NEXP], VD)
            ts(ov, cnt, float(CAP), ALU.is_gt)
            for j in range(2, ROUNDS_OVER + 1):
                ts(ovs, cnt, float(CAP * j), ALU.is_gt)
                tt(ov, ov, ovs, add)
            v(ve.memset(ovs, 0.0))
            v(ve.tensor_tensor_scan(ove, ov, ovs, 0.0, add, add))
            tt(ovs, ove, ov, sub)
            ts(base_, ovs, float(NEXP - 1), add)
            tt(base_, base_, K("expert"), sub)
            t3 = tmp32[:, 0:3 * NEXP].rearrange("p (i e) -> p i e", i=3)
            ts(t3, pos, float(CAP), ALU.is_ge)
            tt(t3, t3, base_.unsqueeze(1).to_broadcast(all3), mul)
            tt(t3, t3, experts, add)
            stt(pos, t3, float(CAP), pos, mul, add)
            for k in range(TOPK):
                tt(pick3[k], pick3[k], pos, mul)
                red(destf[:, :, k:k + 1].rearrange("p i o -> p (i o)"), pick3[k], add)
            copy(dest.rearrange("p (i k) -> p i k", i=3), destf)
            v(ve.nop(), "dest_ready")
            ve.wait_ge(sem("bias_loaded"), 48)
            for k in range(3):
                copy(bparts[0:96, k, :], brow[0:96, :], "bias_parts" if k == 2 else None)
                if k < 2:
                    tt(brow[0:96, :], brow[0:96, :], bparts[0:96, k, :], sub)
            o3 = lambda t_: t_.rearrange("p (b e) -> p b e", b=OVER)
            full = [P, OVER, NEXP]
            ids = K("over_id").unsqueeze(2).to_broadcast(full)
            tt(o3(tmp32), ovs.unsqueeze(1).to_broadcast(full), ids, ALU.is_le)
            tt(o3(tmp32b), ove.unsqueeze(1).to_broadcast(full), ids, ALU.is_gt)
            tt(o3(tmp32), o3(tmp32), o3(tmp32b), mul)
            tt(o3(tmp32), o3(tmp32), K("expert").unsqueeze(1).to_broadcast(full), mul)
            red(bfi, o3(tmp32), add)
            copy(over_e, bfi)
            copy(over_n[:, 0:1], ove[:, NEXP - 1:NEXP])
            v(ve.memset(ohx, 0.0))
            copy(ohx[0:96, 0:NEXP], K("expert_row", 96))
            ts(ohx[0:96, NEXP:NBLK], bfi[0:96, :], K("expert_mod", 96), ALU.is_equal)
            for i, (o, n) in enumerate(TILES):
                ve.wait_ge(sem("gate_exp"), i + 1)
                red(ss2[0:n, i:i + 1], gate4[0:n, i, :], add)
                recip(ss2[0:n, i:i + 1], ss2[0:n, i:i + 1])
                ts(gate4[0:n, i, :], gate4[0:n, i, :], ss2[0:n, i:i + 1], mul)
            b = got("slots")
            copy(slotu[0:CAP, :], b[0:CAP, 0:NBLK + 1], VD)
            v(ve.nop(), "slots_ready")
            for _ in range(2):
                ve.nop().then_inc(sem("gu_drained"), 1)
            barrier(ve, "ve")

            def select(dst, e):
                return ve.tensor_scalar(dst[0:96, :], ohx[0:96, bass.ds(e, 1)].to_broadcast([96, CAP]), 1.0, None, mul)

            v(select(bsel_gu, 0), "gu_bias_ready")
            v(select(bsel_dn, 0), "dn_bias_ready")

            def ve_block(e):
                for c in range(2):
                    g_, u_, s_ = gbuf[0:CAP, c, :], ub[0:CAP, c, :], sgb[0:CAP, c, :]
                    ve.wait_ge(sem("gu_filled"), 2 * e + c + 1)
                    ve.tensor_scalar(g_, ebank(c)[0:CAP, :], 7.0, None, mn).then_inc(sem("g_ready"), 1)
                    ve.tensor_scalar(u_, ebank(c)[CAP:2 * CAP, :], 7.0, -7.0, mn, mx).then_inc(sem("gu_drained"), 1)
                    ve.wait_ge(sem("g_ready"), 2 * e + c + 1)
                    ve.wait_ge(sem("gu_drained"), 2 * e + c + 3)
                    ve.scalar_tensor_tensor(out=u_, in0=u_, scalar=1.0, in1=g_, op0=add, op1=mul).then_inc(sem("gu_product"), 1)
                    ve.wait_ge(sem("gu_product"), 2 * e + c + 1)
                    ve.wait_ge(sem("sigmoid_ready"), 2 * e + c + 1)
                    ve.tensor_tensor(u_, u_, s_, mul).then_inc(sem("act_ready"), 1)
                ve.wait_ge(sem("gu_filled"), 2 * e + 2)
                select(bsel_gu, e + 1).then_inc(sem("gu_bias_ready"), 1)
                ve.wait_ge(sem("dn_filled"), 2 * e + 1)
                select(bsel_dn, e + 1).then_inc(sem("dn_bias_ready"), 1)

            blocks(ve, ve_block)
            barrier(ve, "ve")
            for k in range(TOPK):
                ts(diag[:, k, :], K("ident"), gate4[:, 1, k:k + 1], mul, name="choice_weights")
            for i in (0, 2, 1):
                n = TILES[i][1]
                f_, g_ = fin[0:n, i, :], gate2[0:n, i // 2, :]
                if i != 1:
                    ve.wait_ge(sem(f"picked_rows_{i}"), 16 * TOPK)
                    ts(f_, yk[0:n, 4 * i, :], gate4[0:n, i, 0:1], mul)
                    for k in range(1, TOPK):
                        stt(f_, yk[0:n, 4 * i + k, :], gate4[0:n, i, k:k + 1], f_, mul, add)
                    after(ve, "s", ("gate2", i, 1))
                    tt(f_, f_, g_, mul)
                else:
                    for half in range(2):
                        hs = slice(half * 512, half * 512 + 512)
                        b = got(("sum", half))
                        tt(f_[:, hs], g_[:, hs], b[0:n, :], mul, VD)
                tt(f_, f_, x[0:n, i, :], add, f"y_rows_{i}")
            barrier(ve, "ve")

        def se_late(se, act, got):
            SD = "s_drained"
            se.wait_ge(sem("x_mixed"), 6)
            for i, (o, n) in enumerate(TILES):
                act(squares[0:n, :], x[0:n, i, :], ACT.Square, accum_out=ss2[0:n, i:i + 1])
                act(ss2[0:n, i:i + 1], ss2[0:n, i:i + 1], ACT.Sqrt, "rms", bias=K("eps", n), scale=1.0 / D)
            for i, (o, n) in enumerate(TILES):
                for half in range(2):
                    b = got(("h2T", i, half))
                    act(h2T[:, 4 * half:4 * half + 4, o:o + n], b[:, 0:4 * n].rearrange("p (j n) -> p j n", j=4), ACT.Copy, SD)
            for i, (o, n) in enumerate(TILES):
                se.wait_ge(sem("gate_shifted"), i + 1)
                act(gate4[0:n, i, :], gate4[0:n, i, :], ACT.Exp, "gate_exp")
            for _ in range(2):
                se.nop().then_inc(sem("act_turned"), 1)
            se.nop().then_inc(sem("y_drained"), 1)
            se.sem_inc(sem("y_stored"), 32)
            barrier(se, "se")
            for k, bank in ((0, 7), (1, 6)):
                se.wait_ge(sem("rows_turning"), k + 1)
                se.activation(xT[:, 4 * k:4 * k + 4, :], ebank(bank)[:, 0:4 * CAP].rearrange("p (j n) -> p j n", j=4), ACT.Copy).then_inc(sem("rows_turned"), 1)

            def se_block(e):
                for c in range(2):
                    se.wait_ge(sem("g_ready"), 2 * e + c + 1)
                    se.activation(sgb[0:CAP, c, :], gbuf[0:CAP, c, :], ACT.Sigmoid, scale=1.702).then_inc(sem("sigmoid_ready"), 1)

                def act_turn(c):
                    se.wait_ge(sem("act_turning"), 2 * e + c + 1)
                    se.activation(actT[:, c, :], ebank(6 + c)[:, 0:4 * CAP], ACT.Copy).then_inc(sem("act_turned"), 1)

                act_turn(0)
                for k, bank in ((0, 7), (1, 6)):
                    se.wait_ge(sem("rows_turning"), 2 * e + 3 + k)
                    se.activation(xT[:, 4 * k:4 * k + 4, :], ebank(bank)[:, 0:4 * CAP].rearrange("p (j n) -> p j n", j=4), ACT.Copy).then_inc(sem("rows_turned"), 1)
                act_turn(1)
                se.wait_ge(sem("dn_filled"), 2 * e + 2)
                se.wait_ge(sem("y_stored"), 32 * e + 32)
                se.activation(yb[:, :], ebank(4)[:, :], ACT.Copy).then_inc(sem("y_drained"), 1)
                se.wait_ge(sem("y_drained"), e + 2)
                for half in range(2):
                    dst = y_dram.rearrange("(b s) d -> b s d", s=CAP)[bass.ds(e, 1), :, half * 512:half * 512 + 512]
                    se.dma_start(dst.rearrange("o s d -> (o s) d"), yb[half * CAP:(half + 1) * CAP, :]).then_inc(sem("y_stored"), 16)

            def se_further(e):
                se_block(e)
                se.wait_ge(sem("y_stored"), 32 * e + 64)

            blocks(se, se_block, se_further)
            se.wait_ge(sem("y_stored"), 32 * NEXP + 32)
            barrier(se, "se")
            for i in (0, 2):
                n = TILES[i][1]
                for half in range(2):
                    b = got(("gate2", i, half))
                    act(gate2[0:n, i // 2, half * 512:half * 512 + 512], b[0:n, :], ACT.Copy, SD)
            barrier(se, "se")

        def pool_late(pool, dma):
            for i, (o, n) in enumerate(TILES):
                src = A["x_prompt"][0][o:o + n] if i < 2 else A["x_sample"].rearrange("b t d -> (b t) d")
                dma(x[0:n, i, :], src, "x_again")
            for k, part in enumerate((2, 3, 4)):
                dma(modl[0:9, k, :], mod_dram[:, part * D:(part + 1) * D], "mod_reloaded")
            dma(wr, A["w_router"][0].rearrange("(t p) e -> p t e", p=P), "router_loaded")
            dma(brt, bc(A["b_router"][0], P), "router_loaded")
            pool.wait_ge(sem("merged_ready"), 8)
            dma(gt2[0:9, :], mod_dram[:, 5 * D:6 * D], "gate2_loaded")
            dma(brow[0:32, :], A["b_gu"][0][:, 0:D], "bias_loaded")
            dma(brow[32:64, :], A["b_gu"][0][:, D:2 * D], "bias_loaded")
            dma(brow[64:96, :], A["b_dn"][0], "bias_loaded")
            for i, (o, n) in enumerate(TILES):
                pool.wait_ge(sem("h2_rows"), 2 * i + 2)
                dma(h2_dram[o:o + n, :], h2[0:n, i, :], f"h2_stored_{i}")
            pool.wait_ge(sem("zero_slots"), 1)
            dma(slot_dram.rearrange("(b s) o -> b (s o)", s=CAP), zslot[0:NBLK + 1, 0:CAP], "slots_cleared")
            pool.wait_ge(sem("slots_cleared"), 16)
            pool.wait_ge(sem("dest_ready"), 1)
            for i, (o, n) in enumerate(TILES):
                for k in range(TOPK):
                    pool.indirect_dma_start(out=slot_dram, out_offset=bass.IndirectOffsetOnAxis(dest[0:n, 4 * i + k:4 * i + k + 1], 0),
                                            in_=K("token", n, i, i + 1), in_offset=None).then_inc(sem("slots_written"), 16)
            pool.wait_ge(sem("slots_written"), 16 * 12)
            dma(slotr[0:NBLK + 1, 0:CAP], slot_dram.rearrange("(b s) o -> b (s o)", s=CAP), "slots_loaded")
            pool.wait_ge(sem("slots_loaded"), 16)
            for i in range(3):
                pool.wait_ge(sem(f"h2_stored_{i}"), 16)
            barrier(pool, "pool")
            def gather(e):
                pool.tensor_copy(idx_cur[0:CAP, 0:1], slotu[0:CAP, bass.ds(e, 1)]).then_inc(sem("block_index"), 1)
                pool.wait_ge(sem("block_index"), e + 1)
                pool.sem_inc(sem("block_index_seen"), 1)
                pool.indirect_dma_start(out=xg[0:CAP, :], out_offset=None, in_=h2_dram,
                                        in_offset=bass.IndirectOffsetOnAxis(idx_cur[0:CAP, 0:1], 0)).then_inc(sem("rows_gathered"), 16)

            gather(0)

            def pool_block(e):
                pool.wait_ge(sem("rows_turning"), 2 * e + 2)
                gather(e + 1)

            blocks(pool, pool_block)
            barrier(pool, "pool")
            for i in (0, 2, 1):
                n = TILES[i][1]
                for k in range(TOPK):
                    pool.indirect_dma_start(out=yk[0:n, 4 * i + k, :], out_offset=None, in_=y_dram,
                                            in_offset=bass.IndirectOffsetOnAxis(dest[0:n, 4 * i + k:4 * i + k + 1], 0)).then_inc(sem(f"picked_rows_{i}"), 16)
            for i in (0, 2, 1):
                o, n = TILES[i]
                pool.wait_ge(sem(f"y_rows_{i}"), 1)
                out = y_prompt[0][o:o + n, :] if i < 2 else y_sample.rearrange("b t d -> (b t) d")
                dma(out, fin[0:n, i, :], "output_stored")
            pool.wait_ge(sem("output_stored"), 48)
            barrier(pool, "pool")

        def sp_late(sp):
            wg, wd = A["w_gu"][0], A["w_dn"][0]

            def load_chunk(k, e):
                if k < 4:
                    c0 = (k % 2) * D + (k // 2) * 512
                    src = wg[bass.ds(e, 1), :, c0:c0 + 512].rearrange("o (t p) n -> p (o t) n", p=P)
                    dst = eslots[k].rearrange("p (t n) -> p t n", t=8)
                else:
                    r0 = (k - 4) * 512
                    src = wd[bass.ds(e, 1), r0:r0 + 512, :].rearrange("o (t p) n -> p (o t) n", p=P)
                    dst = eslots[k].rearrange("p (t n) -> p t n", t=4)
                sp.dma_start(dst, src).then_inc(sem(f"expert_weights_{k}"), 16)

            sp.wait_ge(sem("further_cleared"), 16 * (D // P))
            for k in range(3):
                last_in_slot = max(n for n in range(NCHUNK) if slot_of[n] == k)
                ring, m = chunk_last[chunks[last_in_slot][0]]
                sp.wait_ge(sem(f"{ring}_filled"), m)
                load_chunk(k, 0)
            ring, m = chunk_last[("out", 1)]
            sp.wait_ge(sem(f"{ring}_filled"), m)
            for k in range(3, 6):
                load_chunk(k, 0)
            sp.wait_ge(sem("bias_parts"), 1)
            for k in range(3):
                for j in range(3):
                    sp.dma_start(bias3[32 * k:32 * k + 32, j * D:(j + 1) * D], bparts[32 * j:32 * j + 32, k, :]).then_inc(sem("bias_placed"), 16)
            barrier(sp, "sp")

            def reload(e1, expert):
                for k in range(6):
                    if k < 4:
                        sp.wait_ge(sem("gu_filled"), 2 * e1 - 1 + k // 2)
                    else:
                        sp.wait_ge(sem("dn_filled"), 2 * e1 + (k - 5))
                    load_chunk(k, expert)

            with sp.Fori(1, NEXP) as e:
                reload(e, e)
            n = sp.value_load(over_n[0:1, 0:1], min_val=0, max_val=OVER)
            with sp.If(n > 0):
                with sp.Fori(0, n) as b:
                    expert = sp.value_load(over_e[0:1, bass.ds(b, 1)], min_val=0, max_val=NEXP - 1)
                    reload(NEXP + b, expert)
            barrier(sp, "sp")
            barrier(sp, "sp")

        @block.tensor
        def _(pe):
            def mm(out, l, r, first, last):
                return pe.matmul(out, l, r, start=first, stop=last)

            def tr(out, in_):
                n = in_.shape[0]
                return pe.transpose(out, in_, ident[0:n, 0:n])

            def used(tag, ring):
                chunk_last[tag] = (ring, len(tags[ring]))

            pe.wait_ge(sem("c_silu"), 1)
            pe.wait_ge(sem("first_loads"), 16 * L1_FIRST)
            b = fill(pe, "v", "cT")
            for t in range(8):
                last = tr(b[:, t * 9:t * 9 + 9], crow[0:9, t * P:(t + 1) * P])
            filled("v", last)
            b = fill(pe, "s", "cols")
            pe.wait_ge(sem("small_loads"), 16 * L1_SMALL)
            filled("s", tr(b[:, 0:61], rows61[0:61, :]))
            after(pe, "v", "cT")

            def ada_chunk(n):
                w = weights(pe, ("ada", n))
                b = fill(pe, "v", ("ada", n))
                for t in range(8):
                    for j in range(4):
                        last = mm(b[32 * j:32 * j + 9, 0:P], csil[:, t, :], w[:, t, j * P:(j + 1) * P], t == 0, t == 7)
                filled("v", last)
                used(("ada", n), "v")

            for n in range(4):
                ada_chunk(n)
            pe.wait_ge(sem("mod_ready"), 1)

            def spread(i, n, part, half, tag):
                o = TILES[i][0]
                b = fill(pe, "v", tag)
                filled("v", mm(b[0:n, :], K("sel", 9, o, o + n), mod[0:9, part * D + half * 512:part * D + half * 512 + 512], True, True))

            for i, (o, n) in enumerate(TILES):
                for half in range(2):
                    spread(i, n, 1, half, ("scale", i, half))
                    spread(i, n, 0, half, ("shift", i, half))
            for i, (o, n) in enumerate(TILES):
                for half in range(2):
                    pe.wait_ge(sem("h_rows"), 2 * i + half + 1)
                    b = fill(pe, "s", ("hT", i, half))
                    for j in range(4):
                        last = tr(b[:, j * n:(j + 1) * n], hrow[0:n, i % 2, (4 * half + j) * P:(4 * half + j + 1) * P])
                    filled("s", last)
            after(pe, "s", ("hT", 2, 1))

            def row_chunk(c):
                w_ = ROW_CHUNKS[c][1]
                w = weights(pe, ("row", c))
                for i, (o, n) in enumerate(TILES):
                    b = fill(pe, "v", ("row", c, i))
                    for t in range(8):
                        if i < 2:
                            last = mm(b[0:n, 0:w_], hT[:, t, o:o + n], w[:, t, :], t == 0, t == 7)
                        else:
                            for j, (c0, cw) in enumerate(quarters(w_)):
                                last = mm(b[32 * j:32 * j + n, 0:cw], hT[:, t, o:o + n], w[:, t, c0:c0 + cw], t == 0, t == 7)
                    filled("v", last)
                used(("row", c), "v")

            def col_group(c, m):
                if m == 0:
                    cur["col"] = weights(pe, ("col", c))
                b = fill(pe, "s", ("col", c, m))
                for t in range(8):
                    last = mm(b[:, 0:NTOK], cur["col"][:, t, m * P:(m + 1) * P], hT[:, t, :], t == 0, t == 7)
                filled("s", last)
                if m == 3:
                    used(("col", c), "s")

            def col_chunk(c):
                for m in range(4):
                    col_group(c, m)

            for kind, n in STAGE1:
                {"ada": ada_chunk, "row": row_chunk, "col": col_chunk}[kind](n)
            barrier(pe, "pe")
            groups = iter(GATE_GROUPS)

            def gate_groups(count):
                for _ in range(count):
                    col_group(*next(groups))

            for name, c in (("gi", ZI), ("gf", ZF)):
                b = fill(pe, "v", name)
                for i, (o, n) in enumerate(TILES):
                    last = tr(b[0:4, o:o + n], ze(i, n, c, 4))
                filled("v", last)
            pe.wait_ge(sem("state_small"), 16 * 3)
            b = fill(pe, "v", "n0T")
            filled("v", tr(b[:, 0:32], n0r[0:32, :]))
            gate_groups(4)
            pe.wait_ge(sem("gate_exps"), 4)
            pe.wait_ge(sem("gate_logs"), 1)
            b = fill(pe, "v", "gcols")
            for i, (o, n) in enumerate(TILES):
                tr(b[0:n, i * 4:i * 4 + 4], ga_[0:4, o:o + n])
                tr(b[0:n, 12 + i * 4:16 + i * 4], gnd[0:4, o:o + n])
            tr(b[0:32, 24:28], gws[0:4, :])
            tr(b[0:32, 28:32], gwi[0:4, :])
            filled("v", tr(b[0:8, 32:36], gwc[0:4, :]))
            b = fill(pe, "v", "wcb")
            for h in range(MH):
                last = mm(b[:, h * 8:h * 8 + 8], K("head_row", 4, h * P, (h + 1) * P), gwc[0:4, :], True, True)
            filled("v", last)
            for h in range(MH):
                q_, k_ = mq[:, h, :], mq[:, 4 + h, :]
                b = fill(pe, "v", ("krow", h))
                for i, (o, n) in enumerate(TILES):
                    last = tr(b[0:n, o:o + P], k_[:, o:o + n])
                filled("v", last)
                b = fill(pe, "v", ("M", h))
                filled("v", mm(b[:, 0:NTOK], K("head_row", 4, h * P, (h + 1) * P), gM[0:4, :], True, True))
                b = fill(pe, "v", ("S", h))
                mm(b[:, 0:256], k_[:, 0:128], q_[:, 0:256], True, True)
                mm(b[:, 256:384], k_[:, 128:256], q_[:, 128:256], True, True)
                filled("v", mm(b[0:32, 384:416], k_[:, 256:288], q_[:, 256:288], True, True))
                gate_groups(1)
                pe.wait_ge(sem(f"state_C_{h % 2}"), 16 * (h // 2 + 1))
                for half in range(2):
                    b = fill(pe, "s", ("CT", h, half))
                    for j in range(4):
                        bb = half * 4 + j
                        last = tr(b[:, j * P:(j + 1) * P], C0h[:, h % 2, bb * P:(bb + 1) * P])
                    filled("s", last)
                after(pe, "v", ("S", h))
                b = fill(pe, "v", ("num", h))
                S_ = STt[:, h % 2, :]
                one = K("one")
                v_ = [ze(i, n, ZV + h * MD, MD) for i, (o, n) in enumerate(TILES)]
                mm(b[:, 0:128], S_[:, 0:128], v_[0], True, True)
                mm(b[:, 128:129], S_[:, 0:128], one, True, True)
                mm(b[:, 129:257], S_[:, 128:256], v_[0], True, False)
                mm(b[:, 129:257], S_[:, 256:384], v_[1], False, True)
                mm(b[:, 257:258], S_[:, 128:256], one, True, False)
                mm(b[:, 257:258], S_[:, 256:384], one, False, True)
                mm(b[0:32, 258:386], S_[0:32, 384:416], v_[2], True, True)
                filled("v", mm(b[0:32, 386:387], S_[0:32, 384:416], one[0:32, :], True, True))
                after(pe, "s", ("CT", h, 1))
                b = fill(pe, "v", ("numI", h))
                for bb in range(DB):
                    mm(b[:, bb * 4:bb * 4 + 4], CTh[:, h % 2, bb * P:(bb + 1) * P], q_[:, 256 + 4 * bb:260 + 4 * bb], True, True)
                filled("v", mm(b[0:32, 64:72], q_[:, 256:288], n0T[:, h:32:4], True, True))
                gate_groups(1)
                pe.wait_ge(sem("inter_rows"), h + 1)
                b = fill(pe, "v", ("numIT", h))
                filled("v", tr(b[0:32, 0:128], numI[:, h % 2, :]))
                gate_groups(1)
                pe.wait_ge(sem("state_ops"), h + 1)
                kr = krow[:, h % 2, :]
                b = fill(pe, "v", ("Cp", h))
                mm(b[:, 0:128], vw[:, h % 2, 0:128], kr[:, 0:128], True, False)
                mm(b[:, 0:128], vw[:, h % 2, 128:256], kr[:, 128:256], False, True)
                mm(b[0:1, 128:256], WT[:, h % 2, 255:256], kr[:, 0:128], True, False)
                filled("v", mm(b[0:1, 128:256], WT[:, h % 2, 383:384], kr[:, 128:256], False, True))
                for half in range(2):
                    b = fill(pe, "v", ("Cs", h, half))
                    for j in range(4):
                        bb = half * 4 + j
                        last = mm(b[:, j * P:(j + 1) * P], vwb[0:32, h % 2, bb * P:(bb + 1) * P], kr[0:32, 256:384], True, True)
                    filled("v", last)
                b = fill(pe, "v", ("ns", h))
                filled("v", mm(b[0:8, 0:128], wsb[0:32, h % 2, :], kr[0:32, 256:384], True, True))
                pe.wait_ge(sem("head_rows"), h + 1)
                b = fill(pe, "s", ("hmT", h))
                for i, (o, n) in enumerate(TILES):
                    last = tr(b[:, o:o + n], hrw[0:n, h % 2, o:o + P])
                filled("s", last)
            barrier(pe, "pe")
            for i, (o, n) in enumerate(TILES):
                gate_groups(1)
                pe.wait_ge(sem("q_rows"), i + 1)
                for name, src in (("q", qn), ("qr", qr)):
                    b = fill(pe, "s", (name, i))
                    for j in range(4):
                        last = tr(b[:, j * n:(j + 1) * n], src[0:n, i % 2, j * P:(j + 1) * P])
                    filled("s", last)
                if i == 2:
                    b = fill(pe, "v", "pe")
                    for kind in range(2):
                        for u in range(8):
                            c = 29 + kind * 16 + u
                            last = mm(b[:, kind * 2:kind * 2 + 2], w2[:, kind, u, :], colT[:, c:c + 9:8], u == 0, u == 7)
                    filled("v", last)
                pe.wait_ge(sem("kv_rows"), i + 1)
                b = fill(pe, "s", ("k", i))
                tr(b[:, 0:n], kvrows(i, n, 2))
                filled("s", tr(b[:, n:2 * n], kvrows(i, n, 4)))
            b = fill(pe, "v", "pages")
            pe.wait_ge(sem("page_rows"), 1)
            filled("v", mm(b[:, 0:64], K("ones", 1), pgf[0:1, :], True, True))
            gate_groups(1)
            pe.wait_ge(sem("pair_rows"), 16)
            b = fill(pe, "s", "cTp")
            for kp in range(4):
                c = (kp % 2) * 512 + (kp // 2) * P
                last = tr(b[:, kp * P:(kp + 1) * P], pair[:, c:c + P])
            filled("s", last)
            after(pe, "s", "cTp")
            b = fill(pe, "v", "cmp_p")
            for kind in range(2):
                for u in range(8):
                    last = mm(b[:, kind * 32:kind * 32 + 32], w2[:, kind, u, :], cTp[:, 2 * kind:2 * kind + 2, u:P:8], u == 0, u == 7)
            filled("v", last)
            pe.wait_ge(sem("kc_squared"), 1)
            b = fill(pe, "v", "kc_mean")
            filled("v", mm(b[:, 0:NC_P], K("half_mean"), tmpT[:, 0:NC_P], True, True))
            b = fill(pe, "v", "vc_rows")
            filled("v", tr(b[0:NC_P, 0:P], vcT[:, 0:NC_P]))
            pe.wait_ge(sem("kc_ready"), 1)
            for i in range(2):
                for g in range(2):
                    b = fill(pe, "v", ("cs", i, g))
                    gp = slice(g * DH, (g + 1) * DH)
                    for j in range(HPG):
                        last = mm(b[:, j * 16:j * 16 + NC_P], qT[gp, j, i * P:(i + 1) * P], kcT[gp, 0:NC_P], True, True)
                    filled("v", last)
            for i in range(2):
                pe.wait_ge(sem("cmp_probs"), i + 1)
                for half in range(2):
                    b = fill(pe, "s", ("pc", i, half))
                    for j in range(4):
                        h = half * 4 + j
                        last = tr(b[0:NC_P, j * P:(j + 1) * P], sc_c[:, i, h * 16:h * 16 + NC_P])
                    filled("s", last)
                after(pe, "s", ("pc", i, 1))
                b = fill(pe, "v", ("oc", i))
                for h in range(AH):
                    g = h // HPG
                    last = mm(b[:, h * DH:(h + 1) * DH], ptc[0:NC_P, h, :], vcr[0:NC_P, 0, g * DH:(g + 1) * DH], True, True)
                filled("v", last)

            def scores(u):
                br, i, g, jp = UNITS[u]
                keys = (kselT, kwinT)[br]
                nk = (i + 1) * P
                b = fill(pe, "v", ("sc", u))
                gp = slice(g * DH, (g + 1) * DH)
                for hh in range(2):
                    last = mm(b[:, hh * nk:(hh + 1) * nk], qrT[gp, 2 * jp + hh, i * P:(i + 1) * P], keys[gp, 0:nk], True, True)
                filled("v", last)

            assert next(groups, None) is None
            def turned(u):
                br, i, g, jp = UNITS[u]
                nt = i + 1
                pe.wait_ge(sem("probs"), 2 * (u + 1))
                b = fill(pe, "s", ("pt", u))
                for m in range(2 * nt):
                    last = tr(b[:, m * P:(m + 1) * P], Su[:, u % 2, m * P:(m + 1) * P])
                filled("s", last)

            def weighted(u):
                br, i, g, jp = UNITS[u]
                nt = i + 1
                after(pe, "s", ("pt", u))
                b = fill(pe, "v", ("pv", u))
                for hh in range(2):
                    for t in range(nt):
                        m = hh * nt + t
                        last = mm(b[:, hh * DH:(hh + 1) * DH], PTu[:, u % 2, m * P:(m + 1) * P], kvrows(t, P, 3 + 2 * br, g), t == 0, t == nt - 1)
                filled("v", last)
            unit_steps = iter(range(len(UNITS) + 2))

            def unit():
                k = next(unit_steps, None)
                if k is not None:
                    if k < len(UNITS):
                        scores(k)
                    if 0 <= k - 1 < len(UNITS):
                        turned(k - 1)
                    if k >= 2:
                        weighted(k - 2)

            barrier(pe, "pe")
            def rows_of(r):
                return [pts[r % 2][:, m, :].rearrange("p (r c) -> p r c", r=2) for m in range(8)]

            def front(r):
                tv, wn = rows_of(r), wns[r % 2]
                pe.wait_ge(sem(f"cache_rows_{r % 2}"), 16 * 8 * (r // 2 + 1))
                for kind in range(2):
                    for m2 in range(4):
                        ring = "vs"[m2 % 2]
                        b = fill(pe, ring, ("cT", r, kind, m2))
                        for q in range(4):
                            m, par = 2 * m2 + q % 2, q // 2
                            last = tr(b[:, q * P:(q + 1) * P], tv[m][:, par, kind * P:(kind + 1) * P])
                        filled(ring, last)
                    after(pe, "v", ("cT", r, kind, 2))
                    after(pe, "s", ("cT", r, kind, 3))
                    b = fill(pe, "v", ("cmp_s", r, kind))
                    for g in range(2):
                        for u in range(8):
                            last = mm(b[:, g * P:(g + 1) * P], w2[:, kind, u, :], cT[:, g, u:1024:8], u == 0, u == 7)
                    filled("v", last)
                for q4 in range(4):
                    b = fill(pe, "s", ("ks", r, q4))
                    for q in range(4):
                        m, par = (4 * q4 + q) // 2, q % 2
                        last = tr(b[:, q * P:(q + 1) * P], tv[m][:, par, 2 * P:3 * P])
                    filled("s", last)
                pe.wait_ge(sem(f"win_rows_{r % 2}"), 32 * (r // 2 + 1))
                for q2 in range(2):
                    b = fill(pe, "s", ("kw", r, q2))
                    for q in range(4):
                        last = tr(b[:, q * P:(q + 1) * P], wn[:, q2, q, 0:P])
                    filled("s", last)
                unit()
                pe.wait_ge(sem("kc_squared"), 2 + r)
                b = fill(pe, "v", ("kc_mean", r))
                filled("v", mm(b[:, 0:P], K("half_mean"), t2[:, :], True, True))
                b = fill(pe, "v", ("vc_rows", r))
                for b2 in range(2):
                    last = tr(b[0:NC_S, b2 * P:(b2 + 1) * P], vc2[:, b2, 0:NC_S])
                filled("v", last)

            def four(tag, width, lhs, rhs):
                b = fill(pe, "v", tag)
                for c in range(4):
                    b2, g = c // 2, c % 2
                    gp = slice(g * DH, (g + 1) * DH)
                    last = mm(b[32 * c:32 * c + 32, 0:width], lhs(gp, b2), rhs(gp, b2), True, True)
                filled("v", last)

            up_steps = iter(range(8))

            def up(r, count):
                if r < 3:
                    return
                for _ in range(count):
                    m = next(up_steps)
                    if m == 0:
                        pe.wait_ge(sem("gated"), 1)
                        cur["up"] = weights(pe, ("up_m", 0))
                    b = fill(pe, "v", ("up_m", m))
                    for t in range(4):
                        last = mm(b[:, 0:NTOK], cur["up"][:, t, m * P:(m + 1) * P], hmT[:, t, :], t == 0, t == 3)
                    filled("v", last)
                    if m == 7:
                        used(("up_m", 0), "v")

            def scored(r):
                wn = wns[r % 2]
                pe.wait_ge(sem("kc_ready"), 2 + r)
                four(("sc_c", r), NC_S, lambda gp, b2: qTr[gp, b2, :], lambda gp, b2: kc2[gp, b2, 0:NC_S])
                after(pe, "s", ("ks", r, 3))
                for half in range(2):
                    four(("sc_s", r, half), 512, lambda gp, b2: qrTr[gp, b2, :],
                         lambda gp, b2: ksT[gp, b2, half * 512:(half + 1) * 512])
                four(("sc_n", r), 32, lambda gp, b2: qrTr[gp, b2, :], lambda gp, b2: kselT[gp, 256:288])
                after(pe, "s", ("kw", r, 1))
                four(("sc_w", r), 512, lambda gp, b2: qrTr[gp, b2, :], lambda gp, b2: kwT[gp, b2, :])
                four(("sc_v", r), 32, lambda gp, b2: qrTr[gp, b2, :], lambda gp, b2: kwinT[gp, 256:288])
                unit()
                up(r, 2)
                pe.wait_ge(sem("cmp_norm"), r + 1)
                b = fill(pe, "v", ("imp", r))
                filled("v", mm(b[:, 0:NC_S], K("head_sum"), pnrm[:, 0:NC_S], True, True))
                b = fill(pe, "s", ("PTc", r))
                filled("s", tr(b[0:NC_S, 0:P], pnrm[:, 0:NC_S]))
                after(pe, "s", ("PTc", r))
                b = fill(pe, "v", ("o_c", r))
                for c in range(4):
                    b2, g = c // 2, c % 2
                    last = mm(b[32 * c:32 * c + 32, 0:DH], PTc[0:NC_S, 32 * c:32 * c + 32], vcr2[0:NC_S, b2, g * DH:(g + 1) * DH], True, True)
                filled("v", last)
                unit()
                up(r, 2)
                pe.wait_ge(sem("win_probs"), r + 1)
                b = fill(pe, "s", ("PTw", r))
                for t in range(4):
                    last = tr(b[:, t * P:(t + 1) * P], Sw[:, t * P:(t + 1) * P])
                filled("s", last)
                b = fill(pe, "s", ("PTv", r))
                filled("s", tr(b[0:32, 0:P], Sw[:, 512:544]))
                after(pe, "s", ("PTv", r))
                b = fill(pe, "v", ("o_w", r))
                for c in range(4):
                    b2, g = c // 2, c % 2
                    o_ = b[32 * c:32 * c + 32, 0:DH]
                    for t in range(4):
                        mm(o_, PTw[:, t, 32 * c:32 * c + 32], wn[:, b2, t, P + g * DH:P + (g + 1) * DH], t == 0, False)
                    last = mm(o_, PTw[0:32, 4, 32 * c:32 * c + 32], kvrows(2, 32, 5, g), False, True)
                filled("v", last)

            def selected(r):
                tv = rows_of(r)
                unit()
                up(r, 2)
                pe.wait_ge(sem("sel_probs"), r + 1)
                for half in range(2):
                    b = fill(pe, "s", ("PTs", r, half))
                    for t in range(4):
                        last = tr(b[:, t * P:(t + 1) * P], Ss[:, (half * 4 + t) * P:(half * 4 + t + 1) * P])
                    filled("s", last)
                b = fill(pe, "s", ("PTn", r))
                filled("s", tr(b[0:32, 0:P], Ss[:, 1024:1056]))
                after(pe, "s", ("PTn", r))
                b = fill(pe, "v", ("o_s", r))
                for c in range(4):
                    b2, g = c // 2, c % 2
                    o_ = b[32 * c:32 * c + 32, 0:DH]
                    for t in range(8):
                        v_ = tv[4 * b2 + t // 2][:, t % 2, 3 * P + g * DH:3 * P + (g + 1) * DH]
                        mm(o_, PTs[:, t, 32 * c:32 * c + 32], v_, t == 0, False)
                    last = mm(o_, PTs[0:32, 8, 32 * c:32 * c + 32], kvrows(2, 32, 3, g), False, True)
                filled("v", last)
                unit()
                up(r, 2)
                pe.wait_ge(sem("round_out"), r + 1)
                b = fill(pe, "v", ("oTr", r))
                filled("v", tr(b[0:DH, 0:P], orow[:, :]))

            rounds(front, scored, selected)
            assert next(unit_steps, None) is None
            pe.wait_ge(sem("prompt_out"), 1)
            for i in range(2):
                b = fill(pe, "s", ("oT", i))
                for t in range(4):
                    last = tr(b[:, t * P:(t + 1) * P], ob[:, i, t * P:(t + 1) * P])
                filled("s", last)
            barrier(pe, "pe")
            pe_late(pe, mm, tr, col_chunk, used)


        def store_state(eng, dma, h):
            eng.wait_ge(sem("new_state"), h + 1)
            dma(C_prompt[0][0, h], Cpr[:, h % 2, :], f"state_stored_{h % 2}")
            dma(C_sample[0][:, h].rearrange("b v k -> v b k"), Cn[:, h % 2, :].rearrange("p (b k) -> p b k", b=DB), f"state_stored_{h % 2}")

        @block.vector
        def _(ve):
            v = Steps(ve, "vector_step", sem)

            def copy(out, in_, name=None):
                v(ve.tensor_copy(out, in_), name)

            def tt(out, p, q, op, name=None):
                v(ve.tensor_tensor(out, p, q, op), name)

            def ts(out, p, s1, op0, s2=None, op1=None, name=None):
                if op1 is None:
                    v(ve.tensor_scalar(out, p, s1, None, op0), name)
                else:
                    v(ve.tensor_scalar(out, p, s1, s2, op0, op1), name)

            def stt(out, p, s1, q, op0, op1, name=None):
                v(ve.scalar_tensor_tensor(out=out, in0=p, scalar=s1, in1=q, op0=op0, op1=op1), name)

            def red(out, p, op, name=None, negate=None):
                v(ve.tensor_reduce(out, p, AX.X, op, negate=negate), name)

            def recip(out, p, name=None):
                v(ve.reciprocal(out, p), name)

            def got(tag):
                return drain(ve, "v", tag)

            VD, add, mul, sub, mx, mn = "v_drained", ALU.add, ALU.mult, ALU.subtract, ALU.max, ALU.min

            ve.wait_ge(sem("first_loads"), 16 * L1_FIRST)
            ve.wait_ge(sem("c_sigmoid"), 1)
            tt(crow[0:9, :], crow[0:9, :], ctmp[0:9, :], mul, "c_silu")
            b = got("cT")
            copy(csil.rearrange("p a b -> p (a b)"), b[:, 0:72], VD)
            ve.wait_ge(sem("small_loads"), 16 * L1_SMALL)

            def ada_chunk(n):
                b = got(("ada", n))
                for j in range(4):
                    cs = slice(n * 512 + j * P, n * 512 + (j + 1) * P)
                    tt(mod[0:9, cs], b[32 * j:32 * j + 9, 0:P], mod[0:9, cs], add, VD if j == 3 else None)

            def row_chunk(c):
                _, w_, zc = ROW_CHUNKS[c]
                for i, (o, n) in enumerate(TILES):
                    b = got(("row", c, i))
                    if i < 2:
                        tt(zr[0:n, i, zc:zc + w_], b[0:n, 0:w_], rowbias[0:n, zc:zc + w_], add, VD)
                        continue
                    parts = quarters(w_)
                    for j, (c0, cw) in enumerate(parts):
                        tt(zr[0:n, i, zc + c0:zc + c0 + cw], b[32 * j:32 * j + n, 0:cw], rowbias[0:n, zc + c0:zc + c0 + cw], add,
                           VD if j == len(parts) - 1 else None)

            for n in range(4):
                ada_chunk(n)
            stt(mod[0:9, D:2 * D], mod[0:9, D:2 * D], 1.0, gmix[0:9, :], add, mul, "mod_ready")
            for i, (o, n) in enumerate(TILES):
                ve.wait_ge(sem("rms"), i + 1)
                recip(rstd[0:n, i:i + 1], ssum[0:n, i:i + 1])
                if i == 2:
                    after(ve, "s", ("hT", 0, 1))
                for half in range(2):
                    hs = slice(half * 512, (half + 1) * 512)
                    b = got(("scale", i, half))
                    stt(hrow[0:n, i % 2, hs], x[0:n, i, hs], rstd[0:n, i:i + 1], b[0:n, :], mul, mul, VD)
                    b = got(("shift", i, half))
                    tt(hrow[0:n, i % 2, hs], hrow[0:n, i % 2, hs], b[0:n, :], add, VD)
                    v(ve.nop(), "h_rows")
            ve.wait_ge(sem("later_loads"), 16 * len(after_ada))
            for kind, n in STAGE1:
                if kind != "col":
                    {"ada": ada_chunk, "row": row_chunk}[kind](n)
            stt(mod[0:9, 4 * D:5 * D], mod[0:9, 4 * D:5 * D], 1.0, gffn[0:9, :], add, mul, "mod_ready")
            barrier(ve, "ve")
            v(ve.memset(gtmp[0:4, :], 0.0))
            b = got("gi")
            copy(gi[0:4, :], b[0:4, 0:NTOK], VD)
            b = got("gf")
            copy(gf[0:4, :], b[0:4, 0:NTOK], VD)
            stt(gml[0:4, :], gf[0:4, :], -1.0, gf[0:4, :], mul, mn, "forget_abs")
            ve.wait_ge(sem("state_small"), 16 * 3)
            b = got("n0T")
            copy(n0T, b[:, 0:32], VD)
            ve.wait_ge(sem("forget_log"), 2)
            stt(gf[0:4, :], gf[0:4, :], 0.0, gml[0:4, :], mn, sub)
            v(ve.tensor_tensor_scan(gb[0:4, 0:256], gf[0:4, 0:256], gtmp[0:4, 0:256], 0.0, add, add))

            def smp(t_):
                return t_[0:4, 256:288].rearrange("p (b t) -> p b t", t=DT)

            copy(smp(gb)[:, :, 0:1], smp(gf)[:, :, 0:1])
            for t in range(1, DT):
                tt(smp(gb)[:, :, t:t + 1], smp(gb)[:, :, t - 1:t], smp(gf)[:, :, t:t + 1], add)
            tt(ga_[0:4, :], gi[0:4, :], gb[0:4, :], sub)
            v(ve.tensor_tensor_scan(gM[0:4, 0:256], ga_[0:4, 0:256], gtmp[0:4, 0:256], 0.0, mx, add))
            m0b = m0T[0:4, :].unsqueeze(2)
            tt(smp(gM)[:, :, 0:1], smp(ga_)[:, :, 0:1], m0b, mx)
            for t in range(1, DT):
                tt(smp(gM)[:, :, t:t + 1], smp(gM)[:, :, t - 1:t], smp(ga_)[:, :, t:t + 1], mx)
            ML = smp(gM)[:, :, DT - 1:DT]
            tt(gnd[0:4, :], gb[0:4, :], gM[0:4, :], add)
            copy(mfin[0:4, 0:1], gnd[0:4, 255:256])
            copy(mfin[0:4, 1:9].unsqueeze(2), smp(gnd)[:, :, DT - 1:DT], "m_final")
            r4 = lambda t_: t_[0:4, :].rearrange("p (b t) -> p b t", t=DT)
            tt(r4(gws), smp(ga_), ML.to_broadcast([4, DB, DT]), sub)
            tt(r4(gwi), m0b.to_broadcast([4, DB, DT]), smp(gM), sub)
            tt(gwc[0:4, :].unsqueeze(2), m0b, ML, sub, "gate_logs")
            b = got("gcols")
            for i, (o, n) in enumerate(TILES):
                copy(aT[0:n, i, :], b[0:n, i * 4:i * 4 + 4])
                copy(ndT[0:n, i, :], b[0:n, 12 + i * 4:16 + i * 4])
            copy(wsT[0:32, :], b[0:32, 24:28])
            copy(wiT[0:32, :], b[0:32, 28:32])
            copy(wcT[0:8, :], b[0:8, 32:36], VD)
            b = got("wcb")
            copy(wcb, b[:, 0:32], VD)
            for h in range(MH):
                hb = h % 2
                b = got(("krow", h))
                copy(krow[0:32, hb, 256:384], b[0:32, 256:384])
                copy(krow[:, hb, 0:256], b[:, 0:256], VD)
                b = got(("M", h))
                tt(DTt[:, hb, 0:256], C[:, CC["causal_t"][0]:CC["zeros_t"][1]], b[:, 0:256], sub)
                tt(DTt[:, hb, 256:384], K("causal_t"), b[:, 128:256], sub)
                tt(DTt[0:32, hb, 384:416], K("sample_t", 32), b[0:32, 256:288], sub, VD)
                ve.wait_ge(sem("decays"), 3 * (h + 1))
                b = got(("S", h))
                tt(STt[0:32, hb, 384:416], b[0:32, 384:416], WT[0:32, hb, 384:416], mul)
                tt(STt[:, hb, 0:384], b[:, 0:384], WT[:, hb, 0:384], mul, VD)
                b = got(("num", h))
                for i, (nc_, dc, n) in enumerate(((0, 128, P), (129, 257, P), (258, 386, 32))):
                    if i == 2:
                        copy(hrw[0:32, hb, 256:384], b[0:32, 258:386])
                        copy(den[0:32, hb, 3:4], b[0:32, 386:387], VD)
                    else:
                        d_ = den[0:n, hb, i:i + 1]
                        copy(d_, b[0:n, dc:dc + 1])
                        stt(d_, d_, -1.0, d_, mul, mx)
                        tt(d_, d_, ndT[0:n, i, h:h + 1], mx)
                        recip(d_, d_)
                        ts(hrw[0:n, hb, i * P:(i + 1) * P], b[0:n, nc_:nc_ + P], d_, mul)
                b = got(("numI", h))
                tt(vwb[0:32, hb, 0:8], b[0:32, 64:72], K("batch_of", 32), mul)
                copy(numI[:, hb, :], b[:, 0:32], VD)
                v(ve.nop(), "inter_rows")
                red(nqT[0:32, h:h + 1], vwb[0:32, hb, 0:8], add)
                b = got(("numIT", h))
                hs = hrw[0:32, hb, 256:384]
                stt(hs, b[0:32, 0:128], wiT[0:32, h:h + 1], hs, mul, add, VD)
                d_ = den[0:32, hb, 2:3]
                stt(d_, nqT[0:32, h:h + 1], wiT[0:32, h:h + 1], den[0:32, hb, 3:4], mul, add)
                stt(d_, d_, -1.0, d_, mul, mx)
                tt(d_, d_, ndT[0:32, 2, h:h + 1], mx)
                recip(d_, d_)
                ts(hs, hs, d_, mul)
                v(ve.nop(), "head_rows")
                for i, c in ((0, 255), (1, 383)):
                    ts(vw[:, hb, i * P:(i + 1) * P], ze(i, P, ZV + h * MD, MD), WT[:, hb, c:c + 1], mul)
                ts(wsb[0:32, hb, :], K("batch_of", 32), wsT[0:32, h:h + 1], mul)
                tt(vwb[0:32, hb, :].rearrange("p (b k) -> p b k", b=DB),
                   ze(2, 32, ZV + h * MD, MD).unsqueeze(1).to_broadcast([32, DB, MD]),
                   wsb[0:32, hb, :].unsqueeze(2).to_broadcast([32, DB, MD]), mul, "state_ops")
                b = got(("Cp", h))
                if h >= 2:
                    ve.wait_ge(sem(f"state_stored_{hb}"), 32 * (h // 2))
                copy(npr[0:1, h, :], b[0:1, 128:256])
                copy(Cpr[:, hb, :], b[:, 0:128], VD)
                ve.wait_ge(sem(f"state_C_{hb}"), 16 * (h // 2 + 1))
                for half in range(2):
                    b = got(("Cs", h, half))
                    for j in range(4):
                        bb = half * 4 + j
                        stt(Cn[:, hb, bb * P:(bb + 1) * P], C0h[:, hb, bb * P:(bb + 1) * P], wcb[:, h * 8 + bb:h * 8 + bb + 1],
                            b[:, j * P:(j + 1) * P], mul, add, VD if j == 3 else None)
                b = got(("ns", h))
                stt(nsr[0:8, h, :], n0s[0:8, h, :], wcT[0:8, h:h + 1], b[0:8, 0:128], mul, add, VD)
                v(ve.nop(), "new_state")
            barrier(ve, "ve")
            ve.wait_ge(sem("page_table_loaded"), 16)
            copy(pgf[0:1, :], pgi[0:1, :], "page_rows")
            v(ve.memset(grd.rearrange("p a b -> p (a b)"), 0.0), "gates_cleared")
            ve.wait_ge(sem("norm_rows"), 16 * 4)
            for i, (o, n) in enumerate(TILES):
                ib = i % 2
                if i == 2:
                    after(ve, "s", ("k", 0))

                def norm(src, heads, out, gain, out_is_pairs):
                    s3 = src.rearrange("p (h d) -> p h d", d=DH)
                    w = sq[0:n, 0:heads * DH]
                    w3 = w.rearrange("p (h d) -> p h d", d=DH)
                    tt(w, src, src, mul)
                    red(rs8[0:n, 0:heads], w3, add, "norm_sum")
                    ve.wait_ge(sem("norm_root"), v.count["norm_sum"])
                    recip(rs8[0:n, 0:heads], rs8[0:n, 0:heads])
                    tt(w3, s3, rs8[0:n, 0:heads].unsqueeze(2).to_broadcast([n, heads, DH]), mul)
                    if out_is_pairs:
                        for g in range(2):
                            tt(out.rearrange("p (j g d) -> p g j d", g=2, d=DH)[:, g],
                               w.rearrange("p (g j d) -> p g j d", g=2, d=DH)[:, g],
                               gain[0:n].unsqueeze(1).to_broadcast([n, HPG, DH]), mul)
                    else:
                        tt(s3, w3, gain[0:n].unsqueeze(1).to_broadcast([n, heads, DH]), mul)

                def rope(view, heads, name=None):
                    s3 = view.rearrange("p (h d) -> p h d", d=DH)
                    x1, x2 = s3[:, :, 0:8], s3[:, :, 8:16]
                    co = K("cos", n, i * 8, i * 8 + 8).unsqueeze(1).to_broadcast([n, heads, 8])
                    si = K("sin", n, i * 8, i * 8 + 8).unsqueeze(1).to_broadcast([n, heads, 8])
                    r = [rt[0:n, m, 0:heads * 8].rearrange("p (h d) -> p h d", d=8) for m in range(4)]
                    tt(r[0], x1, co, mul)
                    tt(r[1], x2, si, mul)
                    tt(r[2], x1, si, mul)
                    tt(r[3], x2, co, mul)
                    tt(x1, r[0], r[1], sub)
                    tt(x2, r[2], r[3], add, name)

                norm(ze(i, n, ZQ, 512), 8, qn[0:n, ib, :], qg, True)
                copy(qr[0:n, ib, :], qn[0:n, ib, :])
                rope(qr[0:n, ib, :], 8, "q_rows")
                norm(kvrows(i, n, 2), 2, None, kg[:, 1, :], False)
                rope(kvrows(i, n, 2), 2)
                norm(kvrows(i, n, 4), 2, None, kg[:, 2, :], False)
                rope(kvrows(i, n, 4), 2, "kv_rows")
            b = got("pe")
            copy(y2c[0:64, 0, 0:2], b[64:128, 1:4:2])
            tt(pebc[0:64, :], b[0:64, 0:4:2], y2c[0:64, 0, 0:2], add)
            copy(pebc[64:128, :], pebc[0:64, :], VD)
            b = got("pages")
            b3 = b[:, 0:64].rearrange("p (i h) -> p i h", h=2)
            i3 = idx_f.rearrange("p (a i) -> p a i", a=2)
            ts(i3[:, 0, :], b3[:, :, 0], K("first_page"), mul)
            ts(i3[:, 1, :], b3[:, :, 1], K("second_page"), mul, name=VD)
            tt(idx_t[:, 0:32], i3[:, 0, :], i3[:, 1, :], add)
            ts(idx_t[:, 0:32], idx_t[:, 0:32], float(PAGE // 2), mul, K("pair_in_page"), add)
            copy(idx_u, idx_t[:, 0:32], "cache_index")
            b = got("cmp_p")
            for g in range(2):
                for kind, dst in ((0, kcT), (1, vcT)):
                    c = (kind * 2 + g) * 16
                    copy(y2c[0:64, kind, 0:16], b[64:128, c:c + 16])
                    tt(dst[g * DH:(g + 1) * DH, 0:NC_P], b[0:64, c:c + NC_P], y2c[0:64, kind, 1:16], add,
                       VD if (g, kind) == (1, 1) else None)
            ts(vcT[:, 0:NC_P], vcT[:, 0:NC_P], pebc[:, 1:2], add)
            ts(kcT[:, 0:NC_P], kcT[:, 0:NC_P], pebc[:, 0:1], add)
            tt(tmpT[:, 0:NC_P], kcT[:, 0:NC_P], kcT[:, 0:NC_P], mul, "kc_squared")
            b = got("kc_mean")
            ts(tmpT[:, 0:NC_P], b[:, 0:NC_P], EPS, add, name=VD)
            v(ve.nop(), "kc_var")
            b = got("vc_rows")
            copy(vcr[0:NC_P, 0, :], b[0:NC_P, 0:P], VD)
            ve.wait_ge(sem("kc_root"), 1)
            recip(tmpT[:, 0:NC_P], tmpT[:, 0:NC_P])
            stt(kcT[:, 0:NC_P], kcT[:, 0:NC_P], colT[:, 28:29], tmpT[:, 0:NC_P], mul, mul, "kc_ready")
            ve.wait_ge(sem("branch_gates_ready"), 3)
            st8 = lambda m: stat[:, m, 0:8]
            for i in range(2):
                s3 = sc_c[:, i, :].rearrange("p (h n) -> p h n", n=16)[:, :, 0:NC_P]
                for g in range(2):
                    b = got(("cs", i, g))
                    tt(s3[:, 4 * g:4 * g + 4], b[:, 0:64].rearrange("p (h n) -> p h n", n=16)[:, :, 0:NC_P],
                       K("cmp_mask", P, i * NC_P, (i + 1) * NC_P).unsqueeze(1).to_broadcast([P, HPG, NC_P]), add, VD)
                red(st8(i), s3, mx)
                tt(s3, s3, st8(i).unsqueeze(2).to_broadcast([P, AH, NC_P]), sub, "cmp_shifted")
            for i in range(2):
                ve.wait_ge(sem("cmp_probs"), i + 1)
                s3 = sc_c[:, i, :].rearrange("p (h n) -> p h n", n=16)[:, :, 0:NC_P]
                red(st8(2 + i), s3, add)
                recip(st8(2 + i), st8(2 + i))
                stt(st8(2 + i), st8(2 + i), K("cmp_valid", P, i, i + 1), gt24[:, i, 0:24:3], mul, mul)
            for i in range(2):
                b = got(("oc", i))
                tt(ob[:, i, :].rearrange("p (h d) -> p h d", d=DH), b[:, :].rearrange("p (h d) -> p h d", d=DH),
                   st8(2 + i).unsqueeze(2).to_broadcast([P, AH, DH]), mul, VD)

            def masked(u):
                br, i, g, jp = UNITS[u]
                nk, ub = (i + 1) * P, u % 2
                b = got(("sc", u))
                m0 = CC["causal"][1] - nk
                s3 = Su[:, ub, 0:2 * nk].rearrange("p (h n) -> p h n", h=2)
                tt(s3, b[:, 0:2 * nk].rearrange("p (h n) -> p h n", h=2),
                   C[:, m0:m0 + nk].unsqueeze(1).to_broadcast([P, 2, nk]), add, VD)
                st = stat[:, u % 4, 8:10]
                red(st, s3, mx)
                ts(st, st, -SCALE, mul, name="score_max")

            def weighted(u):
                br, i, g, jp = UNITS[u]
                b = got(("pv", u))
                sm = stat[:, u % 4, 12:14]
                recip(sm, sm)
                for hh in range(2):
                    h = g * HPG + 2 * jp + hh
                    tt(sm[:, hh:hh + 1], sm[:, hh:hh + 1], gt24[:, i, 3 * h + 1 + br:3 * h + 2 + br], mul)
                    o_ = ob[:, i, h * DH:(h + 1) * DH]
                    stt(o_, b[:, hh * DH:(hh + 1) * DH], sm[:, hh:hh + 1], o_, mul, add, VD if hh else None)
            unit_steps = iter(range(len(UNITS) + 2))

            def unit():
                k = next(unit_steps, None)
                if k is not None:
                    if k < len(UNITS):
                        masked(k)
                    if k >= 2:
                        weighted(k - 2)

            ve.wait_ge(sem("output_gate"), 1)
            tt(hmT, hmT, moT, mul, "gated")
            barrier(ve, "ve")
            v(ve.memset(kc2.rearrange("p a b -> p (a b)"), 0.0))
            v(ve.memset(vc2.rearrange("p a b -> p (a b)"), 0.0))
            v(ve.memset(qTr.rearrange("p a b -> p (a b)"), 0.0))
            v(ve.memset(qrTr.rearrange("p a b -> p (a b)"), 0.0))
            v(ve.memset(imp[:, :], 0.0))
            m_, s_, x_ = (lambda k: st4[:, k:k + 1]), (lambda k: st4[:, 4 + k:5 + k]), (lambda k: st4[:, 8 + k:9 + k])
            ve.wait_ge(sem("round_gates"), 16 * 16)

            def front(r):
                for kind, dst in ((0, kc2), (1, vc2)):
                    for m2 in (0, 2):
                        b = got(("cT", r, kind, m2))
                        for g in range(2):
                            for par in range(2):
                                copy(cT[par * DH:(par + 1) * DH, g, m2 * 256:(m2 + 1) * 256],
                                     b[g * DH:(g + 1) * DH, par * 256:(par + 1) * 256], VD if (g, par) == (1, 1) else None)
                    b = got(("cmp_s", r, kind))
                    if kind == 0:
                        for b2 in range(2):
                            c0 = 256 + (2 * r + b2) * 4
                            for src, dq in ((qT, qTr), (qrT, qrTr)):
                                copy(dq[:, b2, 0:16].rearrange("p (j t) -> p j t", t=4), src[:, :, c0:c0 + 4])
                    for g in range(2):
                        gb_ = slice(g * P, (g + 1) * P)
                        copy(y22[0:64, :], b[64:128, gb_])
                        tt(dst[g * DH:(g + 1) * DH, :, 0:NC_S], b[0:64, gb_].rearrange("p (b n) -> p b n", b=2)[:, :, 0:NC_S],
                           y22[0:64, :].rearrange("p (b n) -> p b n", b=2)[:, :, 1:64], add, VD if g else None)
                    ts(dst, dst, pebc[:, kind:kind + 1], add)
                kf = kc2.rearrange("p a b -> p (a b)")
                tt(t2, kf, kf, mul, "kc_squared")
                unit()
                b = got(("kc_mean", r))
                ts(t2, b[:, 0:P], EPS, add, name=VD)
                v(ve.nop(), "kc_var")
                b = got(("vc_rows", r))
                copy(vcr2[0:NC_S, :, :], b[0:NC_S, 0:256].rearrange("p (a b) -> p a b", a=2), VD)
                ve.wait_ge(sem("kc_root"), 2 + r)
                recip(t2, t2)
                stt(kf, kf, colT[:, 28:29], t2, mul, mul, "kc_ready")

            def scored(r):
                b = got(("sc_c", r))
                copy(Sc[:, 0:NC_S], b[:, 0:NC_S], VD)
                red(m_(0), Sc[:, 0:NC_S], mx)
                ts(m_(0), m_(0), -SCALE, mul, name="cmp_max")
                for half in range(2):
                    b = got(("sc_s", r, half))
                    copy(Ss[:, half * 512:(half + 1) * 512], b[:, :], VD)
                b = got(("sc_n", r))
                nm = K("new_mask", P, r * 32, r * 32 + 32)
                tt(Ss[:, 1024:1056], b[:, 0:32], nm, add, VD)
                b = got(("sc_w", r))
                tt(Sw[:, 0:512], b[:, :], K("win_mask"), add, VD)
                b = got(("sc_v", r))
                tt(Sw[:, 512:544], b[:, 0:32], nm, add, VD)
                red(m_(2), Sw[:, :], mx)
                ts(m_(2), m_(2), -SCALE, mul, name="win_max")
                ve.wait_ge(sem("cmp_exp"), r + 1)
                recip(x_(0), s_(0))
                ts(pnrm[:, 0:NC_S], Sc[:, 0:NC_S], x_(0), mul, name="cmp_norm")
                unit()
                up(r, 2)
                b = got(("imp", r))
                copy(imp[:, 0:NC_S], b[:, 0:NC_S], VD)
                I_ = [imb[:, k, :] for k in range(4)]
                red(I_[0], imp.rearrange("p (n q) -> p n q", q=4), add)
                red(m_(1), I_[0], mn)
                ts(I_[1], I_[0], m_(1), ALU.is_equal)
                tt(I_[1], I_[1], K("blk1"), mul)
                red(x_(1), I_[1], mx)
                ts(I_[2], I_[1], x_(1), ALU.is_equal, NEG, mul)
                for m in range(8):
                    view = Ss[:, m * P:(m + 1) * P].rearrange("p (q x) -> p q x", q=4)
                    tt(view, view, I_[2][:, 4 * (m // 2):4 * (m // 2) + 4].unsqueeze(2).to_broadcast([P, 4, 32]), add)
                red(m_(1), Ss[:, :], mx)
                ts(m_(1), m_(1), -SCALE, mul, name="sel_max")
                b = got(("o_c", r))
                ts(orow[:, :], b[:, 0:DH], grd[:, r, 0:1], mul, name=VD)
                unit()
                up(r, 2)
                ve.wait_ge(sem("win_probs"), r + 1)
                add_branch(r, 2, "o_w")

            up_steps = iter(range(8))

            def up(r, count):
                if r == 3:
                    for _ in range(count):
                        m = next(up_steps)
                        b = got(("up_m", m))
                        if m == 0:
                            ve.wait_ge(sem("merge_gates"), 2)
                        tt(gT[:, m, :], b[:, 0:NTOK], gT[:, m, :], mul, VD)

            def add_branch(r, k, tag):
                recip(x_(k), s_(k))
                tt(x_(k), x_(k), grd[:, r, k:k + 1], mul)
                b = got((tag, r))
                stt(orow[:, :], b[:, 0:DH], x_(k), orow[:, :], mul, add, VD)

            def selected(r):
                unit()
                up(r, 2)
                ve.wait_ge(sem("sel_probs"), r + 1)
                add_branch(r, 1, "o_s")
                v(ve.nop(), "round_out")
                unit()
                up(r, 2)
                b = got(("oTr", r))
                for g in range(2):
                    for jj in range(2):
                        for jp in range(2):
                            c0 = 256 + 8 * r
                            dst = oT[jp * DH:(jp + 1) * DH, 2 * g + jj, c0:c0 + 8].rearrange("p (b t) -> p b t", t=4)
                            src = b[0:DH, 0:P].rearrange("p (b g x) -> p b g x", b=2, g=2)[:, :, g, (2 * jj + jp) * 4:(2 * jj + jp) * 4 + 4]
                            copy(dst, src, VD if (g, jj, jp) == (1, 1, 1) else None)

            rounds(front, scored, selected)
            v(ve.nop(), "prompt_out")
            barrier(ve, "ve")
            ve_late(ve, v, got, copy, tt, ts, stt, red, recip)

        @block.scalar
        def _(se):
            s = Steps(se, "scalar_step", sem)

            def act(out, in_, f, name=None, **kw):
                s(se.activation(out, in_, f, **kw), name)

            def got(tag):
                return drain(se, "s", tag)

            SD = "s_drained"
            se.wait_ge(sem("first_loads"), 16 * L1_FIRST)
            act(ctmp[0:9, :], crow[0:9, :], ACT.Sigmoid, "c_sigmoid")
            b = got("cols")
            act(colT[:, 0:61], b[:, 0:61], ACT.Copy, SD)
            act(colT[:, 4:8], colT[:, 4:8], ACT.Copy, scale=MD ** -0.5)
            se.wait_ge(sem("small_loads"), 16 * L1_SMALL)
            for i, (o, n) in enumerate(TILES):
                act(sqs[0:n, :], x[0:n, i, :], ACT.Square, accum_out=ssum[0:n, i:i + 1])
                act(ssum[0:n, i:i + 1], ssum[0:n, i:i + 1], ACT.Sqrt, "rms", bias=K("eps", n), scale=1.0 / D)
            for i, (o, n) in enumerate(TILES):
                for half in range(2):
                    b = got(("hT", i, half))
                    act(hT[:, 4 * half:4 * half + 4, o:o + n], b[:, 0:4 * n].rearrange("p (j n) -> p j n", j=4), ACT.Copy, SD)
            for c in range(2):
                for m in range(4):
                    b = got(("col", c, m))
                    k = c * 4 + m
                    act(mq[:, k, :], b[:, 0:NTOK], ACT.Identity, SD, bias=colT[:, k:k + 1], scale=MD ** -0.5 if c else 1.0)
            barrier(se, "se")
            groups = iter(GATE_GROUPS)

            def gate_groups(count):
                for _ in range(count):
                    c, m = next(groups)
                    b = got(("col", c, m))
                    k = 8 + (c - 2) * 4 + m
                    dst = moT[:, m, :] if c == 2 else gT[:, k - 12, :]
                    act(dst, b[:, 0:NTOK], ACT.Identity, SD, bias=colT[:, k:k + 1])

            se.wait_ge(sem("forget_abs"), 1)
            act(gml[0:4, :], gml[0:4, :], ACT.Exp, "forget_log")
            act(gml[0:4, :], gml[0:4, :], ACT.Ln, "forget_log", bias=K("one", 4))
            gate_groups(2)
            se.wait_ge(sem("gate_logs"), 1)
            se.wait_ge(sem("m_final"), 1)
            act(gnd[0:4, :], gnd[0:4, :], ACT.Exp, "gate_exps", scale=-1.0)
            for t_ in (gws, gwi, gwc):
                act(t_[0:4, :], t_[0:4, :], ACT.Exp, "gate_exps")
            gate_groups(2)
            for h in range(MH):
                hb = h % 2
                after(se, "v", ("M", h))
                act(WT[:, hb, 0:256], DTt[:, hb, 0:256], ACT.Exp, "decays", bias=aT[:, 0, h:h + 1])
                act(WT[:, hb, 256:384], DTt[:, hb, 256:384], ACT.Exp, "decays", bias=aT[:, 1, h:h + 1])
                act(WT[0:32, hb, 384:416], DTt[0:32, hb, 384:416], ACT.Exp, "decays", bias=aT[0:32, 2, h:h + 1])
                gate_groups(1)
                for half in range(2):
                    b = got(("CT", h, half))
                    act(CTh[:, hb, half * 512:(half + 1) * 512], b[:, :], ACT.Copy, SD)
                gate_groups(2)
                b = got(("hmT", h))
                act(hmT[:, h, :], b[:, 0:NTOK], ACT.Copy, SD)
            barrier(se, "se")
            for i, (o, n) in enumerate(TILES):
                act(gt24[0:n, i, :], ze(i, n, ZG, 24), ACT.Sigmoid, "branch_gates_ready")
            def root(i, n, k, heads):
                se.wait_ge(sem("norm_sum"), 3 * i + k + 1)
                act(rs8[0:n, 0:heads], rs8[0:n, 0:heads], ACT.Sqrt, "norm_root", bias=K("eps", n), scale=1.0 / DH)

            for i, (o, n) in enumerate(TILES):
                root(i, n, 0, 8)
                gate_groups(1)
                for name, dst in (("q", qT), ("qr", qrT)):
                    b = got((name, i))
                    act(dst[:, :, o:o + n], b[:, 0:4 * n].rearrange("p (j n) -> p j n", j=4), ACT.Copy, SD)
                root(i, n, 1, 2)
                root(i, n, 2, 2)
                b = got(("k", i))
                act(kselT[:, o:o + n], b[:, 0:n], ACT.Copy)
                act(kwinT[:, o:o + n], b[:, n:2 * n], ACT.Copy, SD)
            gate_groups(1)
            b = got("cTp")
            for kind in range(2):
                for g in range(2):
                    for par in range(2):
                        c = (2 * kind + par) * P
                        act(cTp[par * DH:(par + 1) * DH, 2 * kind + g, :], b[g * DH:(g + 1) * DH, c:c + P], ACT.Copy,
                            SD if (kind, g, par) == (1, 1, 1) else None)
            se.wait_ge(sem("kc_var"), 1)
            act(tmpT[:, 0:NC_P], tmpT[:, 0:NC_P], ACT.Sqrt, "kc_root")
            for i in range(2):
                se.wait_ge(sem("cmp_shifted"), i + 1)
                v3 = sc_c[:, i, :].rearrange("p (h n) -> p h n", n=16)[:, :, 0:NC_P]
                act(v3, v3, ACT.Exp, "cmp_probs", scale=SCALE)
            for i in range(2):
                for half in range(2):
                    b = got(("pc", i, half))
                    if i == 1:
                        after(se, "v", ("oc", 0))
                    act(ptc[0:NC_P, 4 * half:4 * half + 4, :], b[0:NC_P, :].rearrange("p (j n) -> p j n", j=4), ACT.Copy, SD)

            act(moT, moT, ACT.Sigmoid, "output_gate")

            def exps(u):
                br, i, g, jp = UNITS[u]
                nk, ub, us = (i + 1) * P, u % 2, u % 4
                se.wait_ge(sem("score_max"), u + 1)
                for hh in range(2):
                    act(Su[:, ub, hh * nk:(hh + 1) * nk], Su[:, ub, hh * nk:(hh + 1) * nk], ACT.Exp, "probs",
                        bias=stat[:, us, 8 + hh:9 + hh], scale=SCALE, accum_out=stat[:, us, 12 + hh:13 + hh])

            turned_steps, exp_steps = iter(range(len(UNITS) + 2)), iter(range(len(UNITS) + 2))

            def unit_turned():
                u = next(turned_steps, len(UNITS) + 2) - 1
                if 0 <= u < len(UNITS):
                    w = 2 * (UNITS[u][1] + 1) * P
                    b = got(("pt", u))
                    act(PTu[:, u % 2, 0:w], b[:, 0:w], ACT.Copy, SD)

            def unit_exps():
                u = next(exp_steps, len(UNITS))
                if u < len(UNITS):
                    exps(u)

            barrier(se, "se")
            def front(r):
                for kind in range(2):
                    for m2 in (1, 3):
                        b = got(("cT", r, kind, m2))
                        for g in range(2):
                            for par in range(2):
                                act(cT[par * DH:(par + 1) * DH, g, m2 * 256:(m2 + 1) * 256],
                                    b[g * DH:(g + 1) * DH, par * 256:(par + 1) * 256], ACT.Copy, SD if (g, par) == (1, 1) else None)
                for q4 in range(4):
                    b = got(("ks", r, q4))
                    act(ksT[:, q4 // 2, (q4 % 2) * 512:(q4 % 2) * 512 + 512], b[:, :], ACT.Copy, SD)
                for q2 in range(2):
                    b = got(("kw", r, q2))
                    act(kwT[:, q2, :], b[:, :], ACT.Copy, SD)
                unit_turned()
                unit_exps()
                se.wait_ge(sem("kc_var"), 2 + r)
                act(t2, t2, ACT.Sqrt, "kc_root")

            def scored(r):
                se.wait_ge(sem("cmp_max"), r + 1)
                act(Sc[:, 0:NC_S], Sc[:, 0:NC_S], ACT.Exp, "cmp_exp", bias=st4[:, 0:1], scale=SCALE, accum_out=st4[:, 4:5])
                se.wait_ge(sem("win_max"), r + 1)
                act(Sw[:, :], Sw[:, :], ACT.Exp, "win_probs", bias=st4[:, 2:3], scale=SCALE, accum_out=st4[:, 6:7])
                unit_turned()
                unit_exps()
                b = got(("PTc", r))
                act(PTc[0:NC_S, :], b[0:NC_S, 0:P], ACT.Copy, SD)
                unit_turned()
                b = got(("PTw", r))
                act(PTw[:, 0:4, :], b[:, :].rearrange("p (t n) -> p t n", t=4), ACT.Copy, SD)
                b = got(("PTv", r))
                act(PTw[0:32, 4, :], b[0:32, 0:P], ACT.Copy, SD)
                se.wait_ge(sem("sel_max"), r + 1)
                act(Ss[:, :], Ss[:, :], ACT.Exp, "sel_probs", bias=st4[:, 1:2], scale=SCALE, accum_out=st4[:, 5:6])

                unit_exps()

            def selected(r):
                unit_turned()
                unit_exps()
                for half in range(2):
                    b = got(("PTs", r, half))
                    act(PTs[:, 4 * half:4 * half + 4, :], b[:, :].rearrange("p (t n) -> p t n", t=4), ACT.Copy, SD)
                b = got(("PTn", r))
                act(PTs[0:32, 8, :], b[0:32, 0:P], ACT.Copy, SD)
                unit_turned()
                unit_exps()
                act(gT[:, 4 * r:4 * r + 4, :], gT[:, 4 * r:4 * r + 4, :], ACT.Sigmoid, "merge_gates")

            rounds(front, scored, selected)
            for i in range(2):
                b = got(("oT", i))
                act(oT[:, :, i * P:(i + 1) * P], b[:, :].rearrange("p (t n) -> p t n", t=4), ACT.Copy, SD)
            barrier(se, "se")
            se_late(se, act, got)

        @block.gpsimd
        def _(pool):
            def dma(out, in_, name, tiny=False):
                pool.dma_start(out, in_, allow_slow_non_contiguous=tiny).then_inc(sem(name), 16)

            rows = A["cache_nsa_kv"][0].rearrange("n (q r) a g d -> (n q) (r a g d)", r=2)

            def sample_rows(r):
                for m in range(8):
                    pool.indirect_dma_start(out=pts[r % 2][:, m, :], out_offset=None, in_=rows,
                                            in_offset=bass.IndirectOffsetOnAxis(idx_u[:, 8 * r + m:8 * r + m + 1], 0)
                                            ).then_inc(sem(f"cache_rows_{r % 2}"), 16)
                for b2 in range(2):
                    dma(wns[r % 2][:, b2, :, :], A["state_win_kv"][0][2 * r + b2].rearrange("(c p) a g d -> p c (a g d)", p=P),
                        f"win_rows_{r % 2}")

            pool.wait_ge(sem("mod_ready"), 2)
            dma(mod_dram, mod[0:9, :], "mod_stored")
            pool.wait_ge(sem("mod_stored"), 16)
            barrier(pool, "pool")
            dma(m0T[0:4, :], A["state_mlstm_m"][0].rearrange("b h -> h b"), "state_small", True)
            dma(n0r[0:32, :], A["state_mlstm_n"][0].rearrange("b h k -> (b h) k"), "state_small")
            dma(n0s[0:8, :, :], A["state_mlstm_n"][0], "state_small")
            for h in range(MH):
                hb = h % 2
                if h >= 2:
                    pool.wait_ge(sem("new_state"), h - 1)
                dma(C0h[:, hb, :].rearrange("p (b k) -> p b k", b=DB), A["state_mlstm_C"][0][:, h].rearrange("b v k -> v b k"), f"state_C_{hb}")
            dma(pgi[0:1, :], A["page_table"].rearrange("(a b) n -> a (b n)", a=1), "page_table_loaded")
            dma(qg, bc(A["q_norm_g"][0], P), "norm_rows")
            for m in range(3):
                dma(kg[:, m, :], bc(A["k_norm_g"][0][m], P), "norm_rows")
            dma(win_sample[0][:, 0:WIN - DT], A["state_win_kv"][0][:, DT:WIN], "window_moved")
            barrier(pool, "pool")
            for i in range(2):
                pool.wait_ge(sem("kv_rows"), i + 1)
                dma(kv_prompt[0][0, i * P:(i + 1) * P].rearrange("t a g d -> t (a g d)"), zr[:, i, ZKV:ZKV + 512], "kv_stored")
                dma(win_prompt[0][0, i * P:(i + 1) * P].rearrange("t a g d -> t (a g d)"), zr[:, i, ZKV + 512:ZKV + 768], "kv_stored")
            pool.wait_ge(sem("kv_stored"), 64)
            dma(pair, kv_prompt[0][0].rearrange("(p r) a g d -> p (r a g d)", r=2), "pair_rows")
            pool.wait_ge(sem("cache_index"), 1)
            ring, k = chunk_last[("col", GATE_CHUNKS[-1])]
            pool.wait_ge(sem(f"{ring}_filled"), k)
            sample_rows(0)
            pool.wait_ge(sem("window_moved"), 16)
            barrier(pool, "pool")
            for r in range(1, 4):
                if r >= 2:
                    after(pool, "v", ("o_s", r - 2))
                sample_rows(r)
            barrier(pool, "pool")
            pool_late(pool, dma)

        @block.sync
        def _(sp):
            for o_, i_ in first:
                sp.dma_start(o_, i_).then_inc(sem("first_loads"), 16)
            for o_, i_ in small:
                sp.dma_start(o_, i_).then_inc(sem("small_loads"), 16)

            def load(n):
                tag, src = chunks[n]
                if before_in_slot(n):
                    ring, k = chunk_last[chunks[before_in_slot(n)[-1]][0]]
                    sp.wait_ge(sem(f"{ring}_filled"), k)
                t, w = src.shape[1], src.shape[2]
                sp.dma_start(slots[slot_of[n]][:, 0:t * w].rearrange("p (t n) -> p t n", t=t), src).then_inc(sem(f"weights_{slot_of[n]}"), 16)

            n1 = 4 + len(STAGE1)
            for n in range(n1):
                if n == 4:
                    for o_, i_ in after_ada:
                        sp.dma_start(o_, i_).then_inc(sem("later_loads"), 16)
                load(n)
            load(n1)
            for j in range(D // P):
                sp.dma_start(y_dram[NEXP * CAP:, j * P:(j + 1) * P].rearrange("(b s) n -> s b n", s=CAP),
                             K("zeros", CAP).unsqueeze(1).to_broadcast([CAP, OVER, P])).then_inc(sem("further_cleared"), 16)
            barrier(sp, "sp")
            sp.wait_ge(sem("state_small"), 16 * 3)
            sp.wait_ge(sem("state_C_0"), 16)
            sp.wait_ge(sem("state_C_1"), 16)
            def out_of(out, in_, name, tiny=False):
                sp.dma_start(out, in_, allow_slow_non_contiguous=tiny).then_inc(sem(name), 16)

            for n in range(n1 + 1, n1 + 3):
                load(n)
            for h, n in enumerate(range(n1 + 3, FIRST_UP)):
                store_state(sp, out_of, h)
                load(n)
            for h in range(FIRST_UP - n1 - 3, MH):
                store_state(sp, out_of, h)
            out_of(m_prompt[0].rearrange("b h -> h b"), mfin[0:4, 0:1], "rows_stored", True)
            out_of(m_sample[0].rearrange("b h -> h b"), mfin[0:4, 1:9], "rows_stored", True)
            out_of(n_prompt[0], npr[0:1, :, :], "rows_stored")
            out_of(n_sample[0], nsr[0:8, :, :], "rows_stored")
            sp.wait_ge(sem("rows_stored"), 16 * 4)
            for hb in range(2):
                sp.wait_ge(sem(f"state_stored_{hb}"), 64)
            barrier(sp, "sp")
            sp.wait_ge(sem("branch_gates_ready"), 3)
            out_of(gate_dram, gt24[0:32, 2, :], "gates_stored")
            sp.wait_ge(sem("gates_stored"), 16)
            sp.wait_ge(sem("gates_cleared"), 1)
            for r in range(4):
                for c in range(4):
                    b_ = 2 * r + c // 2
                    g = c % 2
                    src = gate_dram[b_ * DT:(b_ + 1) * DT, g * HPG * 3:(g + 1) * HPG * 3].rearrange("t (j k) -> j t k", k=3)
                    out_of(grd[32 * c:32 * c + 16, r, :], src, "round_gates")
            sp.wait_ge(sem("kv_rows"), 3)
            out_of(kv_sample[0].rearrange("b t a g d -> (b t) (a g d)"), zr[0:32, 2, ZKV:ZKV + 512], "sample_rows_stored")
            ws_ = win_sample[0][:, WIN - DT:WIN].rearrange("b t a g d -> b t (a g d)")
            for bb in range(DB):
                out_of(ws_[bb], zr[bb * DT:(bb + 1) * DT, 2, ZKV + 512:ZKV + 768], "sample_rows_stored")
            sp.wait_ge(sem("sample_rows_stored"), 16 * (DB + 1))
            barrier(sp, "sp")
            sp.wait_ge(sem("v_filled"), tags["v"].index(("o_s", 2)) + 1)
            for n in range(FIRST_UP, FIRST_UP + 2):
                load(n)
            barrier(sp, "sp")
            n1 = FIRST_UP + 2
            for n in range(n1, NCHUNK):
                load(n)
            sp_late(sp)


_OUTS = [((1, SEQ, D), "y_prompt"), ((DB, DT, D), "y_sample"),
         ((1, 1, SEQ, 4, KV, DH), "kv_prompt"), ((1, DB, DT, 4, KV, DH), "kv_sample"),
         ((1, 1, SEQ, 2, KV, DH), "win_prompt"), ((1, DB, WIN, 2, KV, DH), "win_sample"),
         ((1, 1, MH, MD, MD), "C_prompt"), ((1, 1, MH, MD), "n_prompt"), ((1, 1, MH), "m_prompt"),
         ((1, DB, MH, MD, MD), "C_sample"), ((1, DB, MH, MD), "n_sample"), ((1, DB, MH), "m_sample")]


def kernel(**inputs):
    import concourse.bacc as _bacc
    from concourse.bass_utils import run_bass_kernel_spmd as _run

    nc = _bacc.Bacc("TRN2", target_bir_lowering=False, num_devices=1)
    arrays = {"in_" + k: np.ascontiguousarray(v) for k, v in inputs.items()}
    arrays["in_tables"] = constants()[0]
    args = {k[3:]: nc.dram_tensor(k, v.shape, mybir.dt.from_np(v.dtype), kind="ExternalInput").ap()
            for k, v in arrays.items()}
    outs = [nc.dram_tensor("out_" + name, shape, F32, kind="ExternalOutput").ap() for shape, name in _OUTS]
    program(nc, args, outs)
    r = _run(nc, [arrays], core_ids=[0])
    return tuple(r.results[0]["out_" + name] for _, name in _OUTS)
```
